# Optimizing a Trainium2 kernel written in Bass

```python
import math, functools
import jax, jax.numpy as jnp
from jax import lax
import numpy as np

D_MODEL = 1024
BATCH = 1
SEQ = 256
DEPTH = 4
DEC_BATCH = 8
DEC_SEQ = 8
PAST_LEN = 2048
PAGE_SIZE = 128

N_MIXERS = 3
N_SGU_LAYERS = (DEPTH + 2) // 3
N_RET_LAYERS = (DEPTH + 1) // 3
N_GLA_LAYERS = DEPTH // 3

SGU_CHUNK = 128
SGU_WIDTH = D_MODEL
SGU_GROUPS = 4
RET_HEADS = 4
RET_DK = D_MODEL // RET_HEADS
RET_DV = 2 * D_MODEL // RET_HEADS
RET_CHUNK = 128
ROPE_BASE = 10000.0
GLA_HEADS = 4
GLA_DK = D_MODEL // 2 // GLA_HEADS
GLA_DV = D_MODEL // GLA_HEADS
GLA_GATE_RANK = 16
GLA_TAU = 16.0
GLA_CHUNK = 64
PEER_HEADS = 8
PEER_NKEYS = 128
PEER_EXPERTS = PEER_NKEYS * PEER_NKEYS
PEER_QDIM = 256
PEER_TOPK = 16
PEER_BLOCK = 256
DN_ALPHA = (2.0 * DEPTH) ** 0.25
DN_BETA = (8.0 * DEPTH) ** -0.25
LN_EPS = 1e-5

kernel_name = 'hybrid_sgu_retnet_gla_peer_step'

F32 = jnp.float32

def layer_norm(x, g, b):
    xf = x.astype(F32)
    mu = xf.mean(-1, keepdims=True)
    var = jnp.square(xf - mu).mean(-1, keepdims=True)
    return ((xf - mu) * lax.rsqrt(var + LN_EPS) * g + b).astype(x.dtype)

def split_heads(a, n, d):
    b_, l_ = a.shape[:2]
    return a.reshape(b_, l_, n, d).transpose(0, 2, 1, 3).astype(F32)

def merge_heads(a):
    b_, h_, l_, d_ = a.shape
    return a.transpose(0, 2, 1, 3).reshape(b_, l_, h_ * d_)

def rotary(x, pos):
    d = x.shape[-1]
    inv = ROPE_BASE ** (-jnp.arange(0, d, 2, dtype=F32) / d)
    ang = pos.astype(F32)[:, None] * inv[None, :]
    cos, sin = jnp.cos(ang), jnp.sin(ang)
    x1, x2 = x[..., : d // 2], x[..., d // 2:]
    return jnp.concatenate([x1 * cos - x2 * sin, x1 * sin + x2 * cos], axis=-1)

def chunked_scan(step, state, seqs, chunk):
    l_ = seqs[0].shape[2]
    n = l_ // chunk

    def to_chunks(a):
        return jnp.moveaxis(a.reshape(a.shape[0], a.shape[1], n, chunk, a.shape[-1]), 2, 0)

    state, outs = lax.scan(step, state, tuple(to_chunks(a) for a in seqs))
    outs = jnp.moveaxis(outs, 0, 2)
    return outs.reshape(outs.shape[0], outs.shape[1], l_, outs.shape[-1]), state

def sgu_mixer(x, w_in, b_in, v_g, v_b, w_s, b_s, w_out):
    b_, l_, _ = x.shape
    z = jax.nn.gelu(x @ w_in + b_in)
    u, v = jnp.split(z, 2, axis=-1)
    v = layer_norm(v, v_g, v_b)
    n_chunks = -(-l_ // SGU_CHUNK)
    lp = n_chunks * SGU_CHUNK
    vc = jnp.pad(v, ((0, 0), (0, lp - l_), (0, 0))).reshape(
        b_, n_chunks, SGU_CHUNK, SGU_GROUPS, SGU_WIDTH // SGU_GROUPS)
    causal = jnp.tril(jnp.ones((SGU_CHUNK, SGU_CHUNK), dtype=bool))
    w_m = jnp.where(causal, w_s, 0)
    mixed = jnp.einsum('gts,bnsgc->bntgc', w_m, vc) + b_s.T[:, :, None]
    mixed = mixed.reshape(b_, lp, SGU_WIDTH)[:, :l_]
    return (u * mixed) @ w_out, v

def ret_log_decay():
    return jnp.log1p(-jnp.exp2(-5.0 - jnp.arange(RET_HEADS, dtype=F32)))

def retention_chunk(state, qkv, log_g):
    q, k, v = qkv
    c = q.shape[2]
    idx = jnp.arange(c, dtype=F32)
    rel = idx[:, None] - idx[None, :]
    decay = jnp.where(rel >= 0, jnp.exp(jnp.maximum(rel, 0.0) * log_g[:, None, None]), 0.0)
    inner = jnp.einsum('bhtd,bhsd->bhts', q, k) * decay
    cross_decay = jnp.exp((idx + 1.0)[None, :] * log_g[:, None])[..., None]
    out = jnp.einsum('bhts,bhse->bhte', inner, v) + jnp.einsum('bhtd,bhde->bhte', q, state) * cross_decay
    k_decay = jnp.exp((c - 1.0 - idx)[None, :] * log_g[:, None])[..., None]
    state = jnp.exp(c * log_g)[:, None, None] * state + jnp.einsum('bhsd,bhse->bhde', k * k_decay, v)
    return state, out

def retention_mixer(x, pos, state, w_in, gn_g, w_out):
    b_, l_, _ = x.shape
    hk, hv = RET_HEADS * RET_DK, RET_HEADS * RET_DV
    q, k, v, g = jnp.split(x @ w_in, [hk, 2 * hk, 2 * hk + hv], axis=-1)
    q = rotary(split_heads(q, RET_HEADS, RET_DK), pos)
    k = rotary(split_heads(k, RET_HEADS, RET_DK), pos) * (RET_DK ** -0.5)
    v = split_heads(v, RET_HEADS, RET_DV)
    step = functools.partial(retention_chunk, log_g=ret_log_decay())
    o, state = chunked_scan(step, state.astype(F32), (q, k, v), math.gcd(l_, RET_CHUNK))
    mu = o.mean(-1, keepdims=True)
    var = jnp.square(o - mu).mean(-1, keepdims=True)
    o = merge_heads((o - mu) * lax.rsqrt(var + LN_EPS)) * gn_g
    return (jax.nn.silu(g) * o.astype(x.dtype)) @ w_out, state

def gla_chunk(state, inp):
    q, k, v, lg = inp
    c = q.shape[2]
    b = jnp.cumsum(lg, axis=2)
    causal = jnp.tril(jnp.ones((c, c), dtype=bool))[:, :, None]
    diff = b[:, :, :, None, :] - b[:, :, None, :, :]
    w = jnp.exp(jnp.where(causal, diff, -jnp.inf))
    att = jnp.einsum('bhtsd,bhsd->bhts', q[:, :, :, None, :] * w, k)
    out = jnp.einsum('bhts,bhse->bhte', att, v) + jnp.einsum('bhtd,bhde->bhte', q * jnp.exp(b), state)
    b_last = b[:, :, -1:, :]
    state = jnp.exp(b_last)[:, :, 0, :, None] * state + jnp.einsum(
        'bhsd,bhse->bhde', k * jnp.exp(b_last - b), v)
    return state, out

def gla_mixer(x, state, w_in, w_a2, b_a, rms_g, w_out):
    b_, l_, _ = x.shape
    hk, hv = GLA_HEADS * GLA_DK, GLA_HEADS * GLA_DV
    q, k, v, g, a = jnp.split(x @ w_in, [hk, 2 * hk, 2 * hk + hv, 2 * hk + 2 * hv], axis=-1)
    lg = jax.nn.log_sigmoid((a @ w_a2 + b_a).astype(F32)) / GLA_TAU
    q = split_heads(q, GLA_HEADS, GLA_DK) * (GLA_DK ** -0.5)
    k = split_heads(k, GLA_HEADS, GLA_DK)
    v = split_heads(v, GLA_HEADS, GLA_DV)
    lg = split_heads(lg, GLA_HEADS, GLA_DK)
    o, state = chunked_scan(gla_chunk, state.astype(F32), (q, k, v, lg), math.gcd(l_, GLA_CHUNK))
    o = o * lax.rsqrt(jnp.square(o).mean(-1, keepdims=True) + LN_EPS) * rms_g
    o = merge_heads(o)
    return (jax.nn.silu(g) * o.astype(x.dtype)) @ w_out, state

def peer_block(xb, w_q, keys_a, keys_b, u_tab, v_tab):
    t_ = xb.shape[0]
    q = (xb @ w_q).reshape(t_, PEER_HEADS, PEER_QDIM)
    qa, qb = jnp.split(q, 2, axis=-1)
    sa, ia = lax.top_k(jnp.einsum('thd,kd->thk', qa, keys_a), PEER_TOPK)
    sb, ib = lax.top_k(jnp.einsum('thd,kd->thk', qb, keys_b), PEER_TOPK)
    cand = (sa[..., :, None] + sb[..., None, :]).reshape(t_, PEER_HEADS, PEER_TOPK * PEER_TOPK)
    s, ci = lax.top_k(cand, PEER_TOPK)
    expert = (jnp.take_along_axis(ia, ci // PEER_TOPK, axis=-1) * PEER_NKEYS
              + jnp.take_along_axis(ib, ci % PEER_TOPK, axis=-1))
    gate = jax.nn.softmax(s.astype(F32), axis=-1)
    u = jnp.take(u_tab, expert, axis=0)
    h = jax.nn.gelu(jnp.einsum('thkd,td->thk', u, xb).astype(F32))
    v = jnp.take(v_tab, expert, axis=0)
    return jnp.einsum('thk,thkd->td', (gate * h).astype(xb.dtype), v)

def peer(x, w_q, keys_a, keys_b, u_tab, v_tab):
    b_, l_, d_ = x.shape
    t_ = b_ * l_
    blk = math.gcd(t_, PEER_BLOCK)
    xb = x.reshape(t_ // blk, blk, d_)
    y = lax.map(lambda xi: peer_block(xi, w_q, keys_a, keys_b, u_tab, v_tab), xb)
    return y.reshape(b_, l_, d_)

def trunk(x, pos, ret_states, gla_states, p):
    new_ret, new_gla, sgu_v = [], [], []
    for i in range(DEPTH):
        kind, j = i % N_MIXERS, i // N_MIXERS
        if kind == 0:
            h, v = sgu_mixer(x, p['sgu_w_in'][j], p['sgu_b_in'][j], p['sgu_v_g'][j], p['sgu_v_b'][j],
                             p['sgu_w_s'][j], p['sgu_b_s'][j], p['sgu_w_out'][j])
            sgu_v.append(v)
        elif kind == 1:
            h, s = retention_mixer(x, pos, ret_states[j], p['ret_w_in'][j], p['ret_gn_g'][j], p['ret_w_out'][j])
            new_ret.append(s)
        else:
            h, s = gla_mixer(x, gla_states[j], p['gla_w_in'][j], p['gla_w_a2'][j], p['gla_b_a'][j],
                             p['gla_rms_g'][j], p['gla_w_out'][j])
            new_gla.append(s)
        x = layer_norm(DN_ALPHA * x + h, p['ln_g'][i, 0], p['ln_b'][i, 0])
        f = peer(x, p['peer_w_q'][i], p['peer_keys_a'][i], p['peer_keys_b'][i], p['peer_u'][i], p['peer_v'][i])
        x = layer_norm(DN_ALPHA * x + f, p['ln_g'][i, 1], p['ln_b'][i, 1])
    return x, jnp.stack(new_ret), jnp.stack(new_gla), jnp.stack(sgu_v)

def setup_inputs(seed: int = 0) -> dict:
    key = jax.random.key(seed)
    ks = jax.random.split(key, 32)

    def nrm(i, shape, scale):
        return jax.random.normal(ks[i], shape, F32) * scale

    D = D_MODEL
    gam = 1.0 - 2.0 ** (-5.0 - np.arange(RET_HEADS, dtype=np.float32))
    ret_scale = jnp.asarray((RET_DK ** -0.5) / np.sqrt(1.0 - gam ** 2), F32)[None, None, :, None, None]
    return {
        'x_prompt': nrm(0, (BATCH, SEQ, D), 1.0),
        'x_sample': nrm(1, (DEC_BATCH, DEC_SEQ, D), 1.0),
        'state_ret': nrm(2, (N_RET_LAYERS, DEC_BATCH, RET_HEADS, RET_DK, RET_DV), 1.0) * ret_scale,
        'state_gla': nrm(3, (N_GLA_LAYERS, DEC_BATCH, GLA_HEADS, GLA_DK, GLA_DV), 3.0),
        'sgu_w_in': nrm(4, (N_SGU_LAYERS, D, 2 * SGU_WIDTH), D ** -0.5),
        'sgu_b_in': nrm(5, (N_SGU_LAYERS, 2 * SGU_WIDTH), 0.02),
        'sgu_v_g': 1.0 + nrm(6, (N_SGU_LAYERS, SGU_WIDTH), 0.05),
        'sgu_v_b': nrm(7, (N_SGU_LAYERS, SGU_WIDTH), 0.02),
        'sgu_w_s': nrm(8, (N_SGU_LAYERS, SGU_GROUPS, SGU_CHUNK, SGU_CHUNK), 0.5 * SGU_CHUNK ** -0.5),
        'sgu_b_s': 1.0 + nrm(9, (N_SGU_LAYERS, SGU_GROUPS, SGU_CHUNK), 0.1),
        'sgu_w_out': nrm(10, (N_SGU_LAYERS, SGU_WIDTH, D), DN_BETA * SGU_WIDTH ** -0.5),
        'ret_w_in': nrm(11, (N_RET_LAYERS, D, 2 * RET_HEADS * RET_DK + 2 * RET_HEADS * RET_DV), D ** -0.5),
        'ret_gn_g': 1.0 + nrm(12, (N_RET_LAYERS, RET_HEADS * RET_DV), 0.05),
        'ret_w_out': nrm(13, (N_RET_LAYERS, RET_HEADS * RET_DV, D), DN_BETA * (RET_HEADS * RET_DV) ** -0.5),
        'gla_w_in': nrm(14, (N_GLA_LAYERS, D, 2 * GLA_HEADS * GLA_DK + 2 * GLA_HEADS * GLA_DV + GLA_GATE_RANK), D ** -0.5),
        'gla_w_a2': nrm(15, (N_GLA_LAYERS, GLA_GATE_RANK, GLA_HEADS * GLA_DK), GLA_GATE_RANK ** -0.5),
        'gla_b_a': nrm(16, (N_GLA_LAYERS, GLA_HEADS * GLA_DK), 0.5),
        'gla_rms_g': 1.0 + nrm(17, (N_GLA_LAYERS, GLA_DV), 0.05),
        'gla_w_out': nrm(18, (N_GLA_LAYERS, GLA_HEADS * GLA_DV, D), DN_BETA * (GLA_HEADS * GLA_DV) ** -0.5),
        'peer_w_q': nrm(19, (DEPTH, D, PEER_HEADS * PEER_QDIM), D ** -0.5),
        'peer_keys_a': nrm(20, (DEPTH, PEER_NKEYS, PEER_QDIM // 2), (PEER_QDIM // 2) ** -0.5),
        'peer_keys_b': nrm(21, (DEPTH, PEER_NKEYS, PEER_QDIM // 2), (PEER_QDIM // 2) ** -0.5),
        'peer_u': nrm(22, (DEPTH, PEER_EXPERTS, D), D ** -0.5),
        'peer_v': nrm(23, (DEPTH, PEER_EXPERTS, D), DN_BETA * PEER_HEADS ** -0.5),
        'ln_g': 1.0 + nrm(24, (DEPTH, 2, D), 0.05),
        'ln_b': nrm(25, (DEPTH, 2, D), 0.02),
    }

def reference(x_prompt, x_sample, state_ret, state_gla,
              sgu_w_in, sgu_b_in, sgu_v_g, sgu_v_b, sgu_w_s, sgu_b_s, sgu_w_out,
              ret_w_in, ret_gn_g, ret_w_out,
              gla_w_in, gla_w_a2, gla_b_a, gla_rms_g, gla_w_out,
              peer_w_q, peer_keys_a, peer_keys_b, peer_u, peer_v,
              ln_g, ln_b):
    p = dict(sgu_w_in=sgu_w_in, sgu_b_in=sgu_b_in, sgu_v_g=sgu_v_g, sgu_v_b=sgu_v_b,
             sgu_w_s=sgu_w_s, sgu_b_s=sgu_b_s, sgu_w_out=sgu_w_out,
             ret_w_in=ret_w_in, ret_gn_g=ret_gn_g, ret_w_out=ret_w_out,
             gla_w_in=gla_w_in, gla_w_a2=gla_w_a2, gla_b_a=gla_b_a, gla_rms_g=gla_rms_g, gla_w_out=gla_w_out,
             peer_w_q=peer_w_q, peer_keys_a=peer_keys_a, peer_keys_b=peer_keys_b, peer_u=peer_u, peer_v=peer_v,
             ln_g=ln_g, ln_b=ln_b)
    bp, lp_ = x_prompt.shape[:2]
    ret0 = jnp.zeros((N_RET_LAYERS, bp, RET_HEADS, RET_DK, RET_DV), F32)
    gla0 = jnp.zeros((N_GLA_LAYERS, bp, GLA_HEADS, GLA_DK, GLA_DV), F32)
    pos_prompt = jnp.arange(lp_, dtype=jnp.int32)
    y_prompt, ret_prompt, gla_prompt, _ = trunk(x_prompt, pos_prompt, ret0, gla0, p)
    pos_sample = PAST_LEN + jnp.arange(x_sample.shape[1], dtype=jnp.int32)
    y_sample, ret_sample, gla_sample, sgu_v_sample = trunk(x_sample, pos_sample, state_ret, state_gla, p)
    return (y_prompt, y_sample, ret_prompt, ret_sample, gla_prompt, gla_sample, sgu_v_sample)


_drawn_inputs = setup_inputs


def setup_inputs(seed=0):
    import zlib

    import numpy as np

    out = dict(_drawn_inputs(seed))
    spreads = {}
    factors = {'sgu_v_b': 2.824, 'ret_gn_g': 4.976, 'gla_rms_g': 6.274}
    for name, (base, spread) in spreads.items():
        noise = np.random.default_rng([zlib.crc32(name.encode()), seed]).standard_normal(out[name].shape)
        drawn = base * np.exp(spread * noise) if base else spread * noise
        out[name] = __import__('jax').numpy.asarray(drawn.astype(out[name].dtype))
    for name, factor in factors.items():
        out[name] = (out[name] * factor).astype(out[name].dtype)
    return out
```

```python
from collections import namedtuple
from contextlib import ExitStack, contextmanager

import numpy as np
import concourse.bass as bass
from concourse import mybir

F32 = mybir.dt.float32
F16 = mybir.dt.float16
U32 = mybir.dt.uint32
ALU = mybir.AluOpType
ACT = mybir.ActivationFunctionType
AX = mybir.AxisListType.X

D = 1024
KT = D // 128
PROMPT, NB, LS = 256, 8, 8
SAMPLE = NB * LS
T = PROMPT + SAMPLE
ROWS = [128, 128, SAMPLE]
TILES = [(0, 128), (128, 128), (256, SAMPLE)]
DEPTH = 4
PAST = 2048
H = 4
EPS = 1e-5
ALPHA = (2.0 * DEPTH) ** 0.25
GROUP = 512
LEVELS = 7
PH, PK, NK = 8, 16, 128
QUARTER = NK // 4
GT = T // QUARTER
U_SCALE, V_SCALE, G_SCALE = 64.0, 16.0, 16.0
W_SCALE = 64.0
LOWEST = -3.0e38

Job = namedtuple("Job", "col kind dest func bias scale width")


def ret_log_decay():
    return np.log1p(-np.exp2(-5.0 - np.arange(H))).astype(np.float32)


def shape_constants():
    f = np.float32

    def exp(x):
        return np.exp(x.astype(np.float64)).astype(f)
    pos = np.concatenate([np.arange(PROMPT), np.tile(PAST + np.arange(LS), NB)]).astype(f)
    inv = (10000.0 ** (-np.arange(0, 256, 2) / 256)).astype(f)
    ang = (pos[None, :] * inv[:, None]).astype(f)
    lg = ret_log_decay()
    step = np.concatenate([np.arange(128), np.arange(128), np.tile(np.arange(LS), NB)]).astype(f)
    size = np.concatenate([np.full(PROMPT, 128), np.full(SAMPLE, LS)]).astype(f)
    cross = exp((step + 1)[None, :] * lg[:, None])
    keep = exp((size - 1 - step)[None, :] * lg[:, None]) / f(16)
    rel = np.arange(128)[None, :] - np.arange(128)[:, None]
    decay = np.where(rel >= 0, exp(np.maximum(rel, 0).astype(f)[None] * lg[:, None, None]) / f(16), 0).astype(f)
    seq = np.arange(SAMPLE) // LS
    same = seq[None, :] == seq[:, None]
    decay_s = np.where(same, decay[:, :SAMPLE, :SAMPLE], 0).astype(f)
    member = (seq[:, None] == np.arange(NB)[None, :]).astype(f)
    kd = np.zeros((128, 3, H), f)
    for i, (t0, n) in enumerate(TILES):
        kd[:n, i] = keep[:, t0:t0 + n].T
    kdm = np.einsum("sb,sh->sbh", member, kd[:SAMPLE, 2]).astype(f)
    s, t = np.arange(128)[:, None], np.arange(128)[None, :]
    levels = [s == t] + [(s // b == t // b) & (s % b < b // 2) & (t % b >= b // 2) for b in (2, 4, 8, 16, 32, 64)]
    start = np.ones(T, f)
    start[0:PROMPT:64] = 0
    start[PROMPT::LS] = 0
    dec = np.concatenate([np.repeat(exp(128 * lg)[:, None], 2, 1), np.repeat(exp(LS * lg)[:, None], NB, 1)], 1)
    rows = np.ones((128, 1), f)
    return {
        "c_cos": np.cos(ang.astype(np.float64)).astype(f),
        "c_sin": np.sin(ang.astype(np.float64)).astype(f),
        "c_cross": (rows[:, None] * cross[None]).astype(f),
        "c_decay": np.ascontiguousarray(decay.transpose(1, 0, 2)),
        "c_decay_s": np.ascontiguousarray(decay_s.transpose(1, 0, 2)),
        "c_kd": kd,
        "c_kdm": kdm,
        "c_member": member,
        "c_memcol": (rows[:, None] * member.T[None]).astype(f),
        "c_levels": np.ascontiguousarray(np.stack(levels).astype(f).transpose(1, 0, 2)),
        "c_start": (rows * start[None]).astype(f),
        "c_dec": (rows[:, None] * dec[None]).astype(f),
        "c_ident": np.eye(128, dtype=f),
        "c_iota": (rows * np.arange(NK)[None]).astype(f),
        "c_ones": np.ones((1, 128), f),
    }


def build(nc, io, out):

    @contextmanager
    def phase(*names):
        handles = [nc.alloc_semaphore(f"{n}_{nc.next_id()}") for n in names]
        with nc.Block() as block:
            yield block, namedtuple("Signals", names)(*handles)
        nc.clear_and_free_semaphores(handles)
        nc.all_engine_barrier()

    def linker(eng, sem):
        n = [0]

        def link(ins):
            n[0] += 1
            ins.then_inc(sem, 1)
            eng.wait_ge(sem, n[0])
        return link

    root = ExitStack()

    def sb(name, shape, dt=F32, ctx=root):
        return ctx.enter_context(nc.sbuf_tensor(f"{name}_{nc.next_id()}", shape, dt))

    ps = root.enter_context(nc.psum_tensor("ps", [128, 8, 512], F32))
    x_tok = sb("x_tok", [128, 3, D])
    x_T = sb("x_T", [128, KT, T])
    x_hi = sb("x_hi", [128, KT, T], F16)
    x_lo = sb("x_lo", [128, KT, T], F16)
    ident = sb("ident", [128, 128])
    ones = sb("ones", [1, 128])
    w_ones = sb("w_ones", [1, 128])
    eps = sb("eps", [128, 1])
    w_eps = sb("w_eps", [128, 1])

    def emit_transposes(pe, s, banks, wait_first):
        n = 0
        for i, (t0, r) in enumerate(TILES):
            wait_first(i)
            for q in range(KT // 4):
                if n >= 2:
                    pe.wait_ge(s.tp_used, n - 1)
                for j in range(4):
                    last = nc.tensor.transpose(ps[:, banks[n % 2], j * 128:j * 128 + r],
                                               x_tok[0:r, i, (4 * q + j) * 128:(4 * q + j + 1) * 128],
                                               ident[0:r, 0:r])
                last.then_inc(s.tp, 1)
                n += 1

    def emit_transpose_copies(act, s, banks):
        n = 0
        for i, (t0, r) in enumerate(TILES):
            for q in range(KT // 4):
                act.wait_ge(s.tp, n + 1)
                nc.scalar.copy(x_T[:, 4 * q:4 * q + 4, t0:t0 + r],
                               ps[:, banks[n % 2], :].rearrange("p (j t) -> p j t", j=4)[:, :, 0:r]
                               ).then_inc(s.tp_used, 1)
                n += 1

    def emit_high_parts(act, s):
        act.wait_ge(s.tp_used, 3 * KT // 4)
        for q in range(KT // 4):
            nc.scalar.copy(x_hi[:, 4 * q:4 * q + 4, :], x_T[:, 4 * q:4 * q + 4, :]).then_inc(s.hi, 1)

    def emit_low_parts(dve, s):
        for q in range(KT // 4):
            dve.wait_ge(s.hi, q + 1)
            nc.vector.tensor_tensor(x_lo[:, 4 * q:4 * q + 4, :], x_T[:, 4 * q:4 * q + 4, :],
                                    x_hi[:, 4 * q:4 * q + 4, :], ALU.subtract)

    with phase("loaded", "tp", "tp_used", "hi") as (block, s):
        @block.sync
        def _(sp):
            sp.dma_start(x_tok[:, 0:2, :], io["x_prompt"].rearrange("b (i p) d -> p (b i) d", p=128)
                         ).then_inc(s.loaded, 16)
            sp.dma_start(x_tok[0:SAMPLE, 2, :], io["x_sample"].rearrange("b l d -> (b l) d")
                         ).then_inc(s.loaded, 16)
            sp.dma_start(ident[:], io["c_ident"]).then_inc(s.loaded, 16)
            sp.dma_start(ones[:], io["c_ones"]).then_inc(s.loaded, 16)

        @block.vector
        def _(dve):
            nc.vector.memset(eps[:], EPS)
            nc.vector.memset(w_eps[:], EPS * W_SCALE ** 2)
            nc.vector.memset(w_ones[:], W_SCALE)
            emit_low_parts(dve, s)

        @block.tensor
        def _(pe):
            emit_transposes(pe, s, (0, 1), lambda i: pe.wait_ge(s.loaded, 64) if i == 0 else None)

        @block.scalar
        def _(act):
            emit_transpose_copies(act, s, (0, 1))
            emit_high_parts(act, s)

    def project_in(w, jobs):
        units = []
        for g, j in enumerate(jobs):
            for f in range(-(-j.width // 128) if j.kind == "feature" else 3):
                units.append((g, j, f))

        def units_through(g):
            return sum(u[0] <= g for u in units)

        with ExitStack() as ctx, phase("w0", "w1", "w_hi", "w_lo", "out", "out_used") as (block, s):
            w_in = sb("w_in", [128, 2, KT, GROUP], ctx=ctx)
            w_hi = sb("w_hi", [128, 2, KT, GROUP], F16, ctx=ctx)
            w_lo = sb("w_lo", [128, 2, KT, GROUP], F16, ctx=ctx)
            w_sem = (s.w0, s.w1)

            @block.sync
            def _(sp):
                for g, j in enumerate(jobs):
                    if g >= 2:
                        sp.wait_ge(s.w_lo, 2 * (g - 1))
                    for k in range(0, KT, KT // 2):
                        sp.dma_start(w_in[:, g % 2, k:k + KT // 2, 0:j.width],
                                     w[128 * k:128 * (k + KT // 2), j.col:j.col + j.width]
                                     .rearrange("(k p) n -> p k n", p=128)).then_inc(w_sem[g % 2], 16)

            @block.tensor
            def _(pe):
                for n, (g, j, f) in enumerate(units):
                    if f == 0:
                        pe.wait_ge(s.w_lo, 2 * (g + 1))
                        pe.wait_ge(s.w_hi, 2 * (g + 1))
                    if n >= 6:
                        pe.wait_ge(s.out_used, n - 5)
                    bank, p = n % 6, g % 2
                    parts = ((w_hi, x_hi), (w_hi, x_lo), (w_lo, x_hi))
                    if j.kind == "feature":
                        m = min(128, j.width - 128 * f)
                        for k in range(KT):
                            for e, (ww, xx) in enumerate(parts):
                                last = nc.tensor.matmul(ps[0:m, bank, 0:T], ww[:, p, k, 128 * f:128 * f + m],
                                                        xx[:, k, :], start=(k == 0 and e == 0),
                                                        stop=(k == KT - 1 and e == 2))
                    else:
                        t0, r = TILES[f]
                        for k in range(KT):
                            for e, (ww, xx) in enumerate(parts):
                                last = nc.tensor.matmul(ps[0:r, bank, 0:j.width], xx[:, k, t0:t0 + r],
                                                        ww[:, p, k, 0:j.width], start=(k == 0 and e == 0),
                                                        stop=(k == KT - 1 and e == 2 and j.bias is None))
                        if j.bias is not None:
                            last = nc.tensor.matmul(ps[0:r, bank, 0:j.width], w_ones[:, 0:r], j.bias,
                                                    start=False, stop=True)
                    last.then_inc(s.out, 1)

            @block.scalar
            def _(act):
                def split(g):
                    j = jobs[g]
                    act.wait_ge(w_sem[g % 2], 32 * (g // 2 + 1))
                    if g >= 2:
                        act.wait_ge(s.out, units_through(g - 2))
                    for k in range(0, KT, KT // 2):
                        nc.scalar.activation(w_hi[:, g % 2, k:k + KT // 2, 0:j.width],
                                             w_in[:, g % 2, k:k + KT // 2, 0:j.width], ACT.Copy, scale=W_SCALE
                                             ).then_inc(s.w_hi, 1)

                split(0)
                for n, (g, j, f) in enumerate(units):
                    if f == 0 and g + 1 < len(jobs):
                        split(g + 1)
                    act.wait_ge(s.out, n + 1)
                    dst = j.dest(f)
                    bias = j.bias[:, f:f + 1] if j.kind == "feature" and j.bias is not None else 0.0
                    width = T if j.kind == "feature" else j.width
                    nc.scalar.activation(dst, ps[0:dst.shape[0], n % 6, 0:width], j.func, bias=bias,
                                         scale=j.scale / W_SCALE).then_inc(s.out_used, 1)

            @block.vector
            def _(dve):
                for g, j in enumerate(jobs):
                    for k in range(0, KT, KT // 2):
                        dve.wait_ge(s.w_hi, 2 * g + k // (KT // 2) + 1)
                        at = (slice(None), g % 2, slice(k, k + KT // 2), slice(0, j.width))
                        nc.vector.scalar_tensor_tensor(out=w_lo[at], in0=w_in[at], scalar=W_SCALE, in1=w_hi[at],
                                                       op0=ALU.mult, op1=ALU.subtract).then_inc(s.w_lo, 1)

    def job(col, kind, dest, func=None, bias=None, scale=1.0, width=GROUP):
        return Job(col, kind, dest, func or ACT.Copy, bias, scale, width)

    def project_out(w, src, kt):
        with ExitStack() as ctx, phase("w0", "w1", "w2", "w3", "hi", "lo", "src_hi", "out") as (block, s):
            w_in = sb("w_in", [128, 4, D], ctx=ctx)
            w_hi = sb("w_hi", [128, 4, D], F16, ctx=ctx)
            w_lo = sb("w_lo", [128, 4, D], F16, ctx=ctx)
            s_hi = sb("s_hi", [128, kt, T], F16, ctx=ctx)
            s_lo = sb("s_lo", [128, kt, T], F16, ctx=ctx)
            w_sem = (s.w0, s.w1, s.w2, s.w3)

            @block.sync
            def _(sp):
                for k in range(kt):
                    if k >= 4:
                        sp.wait_ge(s.lo, k - 3)
                    sp.dma_start(w_in[:, k % 4, :], w[128 * k:128 * k + 128, :]).then_inc(w_sem[k % 4], 16)

            @block.scalar
            def _(act):
                for k in range(kt):
                    nc.scalar.copy(s_hi[:, k, :], src[:, k, :]).then_inc(s.src_hi, 1)
                    act.wait_ge(w_sem[k % 4], 16 * (k // 4 + 1))
                    if k >= 4:
                        act.wait_ge(s.out, k - 3)
                    nc.scalar.activation(w_hi[:, k % 4, :], w_in[:, k % 4, :], ACT.Copy, scale=W_SCALE
                                         ).then_inc(s.hi, 1)

            @block.vector
            def _(dve):
                for k in range(kt):
                    dve.wait_ge(s.src_hi, k + 1)
                    nc.vector.tensor_tensor(s_lo[:, k, :], src[:, k, :], s_hi[:, k, :], ALU.subtract)
                    dve.wait_ge(s.hi, k + 1)
                    nc.vector.scalar_tensor_tensor(out=w_lo[:, k % 4, :], in0=w_in[:, k % 4, :], scalar=W_SCALE,
                                                   in1=w_hi[:, k % 4, :], op0=ALU.mult, op1=ALU.subtract
                                                   ).then_inc(s.lo, 1)

            @block.tensor
            def _(pe):
                for k in range(kt):
                    pe.wait_ge(s.lo, k + 1)
                    pe.wait_ge(s.hi, k + 1)
                    for i, (t0, r) in enumerate(TILES):
                        for e, (ss, ww) in enumerate(((s_hi, w_hi), (s_hi, w_lo), (s_lo, w_hi))):
                            for n in range(2):
                                last = nc.tensor.matmul(ps[0:r, 2 * i + n, :], ss[:, k, t0:t0 + r],
                                                        ww[:, k % 4, 512 * n:512 * n + 512],
                                                        start=(k == 0 and e == 0), stop=(k == kt - 1 and e == 2))
                    last.then_inc(s.out, 1)

    def residual_norm(layer, which):
        with ExitStack() as ctx, phase("loaded", "step", "var", "std", "affine", "gain", "ready",
                                       "tp", "tp_used", "hi") as (block, s):
            g_row = sb("g_row", [128, D], ctx=ctx)
            b_row = sb("b_row", [128, D], ctx=ctx)
            st = sb("st", [128, 3, 2, 6], ctx=ctx)
            mv = sb("mv", [128, 3, 2], ctx=ctx)
            sd = sb("sd", [128, 3], ctx=ctx)
            rs = sb("rs", [128, 3], ctx=ctx)

            @block.sync
            def _(sp):
                sp.dma_start(g_row[:], io["ln_g"][layer, which:which + 1, :].partition_broadcast(128)
                             ).then_inc(s.loaded, 16)
                sp.dma_start(b_row[:], io["ln_b"][layer, which:which + 1, :].partition_broadcast(128)
                             ).then_inc(s.loaded, 16)

            @block.vector
            def _(dve):
                link = linker(dve, s.step)
                for i, (t0, r) in enumerate(TILES):
                    x = x_tok[0:r, i, :]
                    link(nc.vector.scalar_tensor_tensor(out=x, in0=x, scalar=ALPHA * W_SCALE,
                                                        in1=ps[0:r, 2 * i:2 * i + 2, :].rearrange("p a b -> p (a b)"),
                                                        op0=ALU.mult, op1=ALU.add))
                    nc.vector.bn_stats(out=st[0:r, i, 0, :], in_=x[:, 0:512])
                    link(nc.vector.bn_stats(out=st[0:r, i, 1, :], in_=x[:, 512:1024]))
                    nc.vector.bn_aggr(out=mv[0:r, i, :], in_=st[0:r, i, :, :].rearrange("p a b -> p (a b)")
                                      ).then_inc(s.var, 1)
                for i, (t0, r) in enumerate(TILES):
                    x = x_tok[0:r, i, :]
                    dve.wait_ge(s.var, 3)
                    dve.wait_ge(s.std, i + 1)
                    link(nc.vector.reciprocal(rs[0:r, i:i + 1], sd[0:r, i:i + 1]))
                    link(nc.vector.tensor_scalar(x, x, mv[0:r, i, 0:1], rs[0:r, i:i + 1], ALU.subtract, ALU.mult))
                    if i == 0:
                        dve.wait_ge(s.loaded, 32)
                    nc.vector.tensor_tensor(x, x, g_row[0:r, :], ALU.mult).then_inc(s.gain, 1)
                emit_low_parts(dve, s)

            @block.gpsimd
            def _(pool):
                for i, (t0, r) in enumerate(TILES):
                    pool.wait_ge(s.gain, i + 1)
                    nc.gpsimd.tensor_tensor(x_tok[0:r, i, :], x_tok[0:r, i, :], b_row[0:r, :], ALU.add
                                            ).then_inc(s.ready, 1)

            @block.tensor
            def _(pe):
                emit_transposes(pe, s, (6, 7), lambda i: pe.wait_ge(s.ready, i + 1))

            @block.scalar
            def _(act):
                for i, (t0, r) in enumerate(TILES):
                    act.wait_ge(s.var, i + 1)
                    nc.scalar.activation(sd[0:r, i:i + 1], mv[0:r, i, 1:2], ACT.Sqrt, bias=w_eps[0:r, :]
                                         ).then_inc(s.std, 1)
                emit_transpose_copies(act, s, (6, 7))
                emit_high_parts(act, s)

    def sgu(j, layer):
        w_in, w_out = io["sgu_w_in"][j], io["sgu_w_out"][j]
        with ExitStack() as ctx:
            u_T = sb("u_T", [128, KT, T], ctx=ctx)
            v = sb("v", [128, 3, D], ctx=ctx)
            b_col = sb("b_col", [128, 16], ctx=ctx)
            b_row = sb("b_row", [1, 2 * D], ctx=ctx)
            w_m = sb("w_m", [128, 4, 128], ctx=ctx)
            w_ms = sb("w_ms", [SAMPLE, 4, SAMPLE], ctx=ctx)
            b_s = sb("b_s", [1, 4, T], ctx=ctx)
            vg = sb("vg", [128, D], ctx=ctx)
            vb = sb("vb", [128, D], ctx=ctx)
            with phase("loaded", "zero", "spread") as (block, s):
                @block.sync
                def _(sp):
                    for dst, src in ((b_col[:], io["sgu_b_col"][j]), (b_row[:], io["sgu_b_in"][j:j + 1, :]),
                                     (w_m[:], io["sgu_w_sT"][j].rearrange("g s t -> s g t")),
                                     (vg[:], io["sgu_v_g"][j:j + 1, :].partition_broadcast(128)),
                                     (vb[:], io["sgu_v_b"][j:j + 1, :].partition_broadcast(128))):
                        sp.dma_start(dst, src).then_inc(s.loaded, 16)
                    for q in range(2):
                        sp.dma_start(b_s[:, :, 128 * q:128 * q + 128], io["sgu_b_s"][j:j + 1, :, :]
                                     ).then_inc(s.loaded, 16)
                    for b in range(NB):
                        sp.dma_start(b_s[:, :, PROMPT + LS * b:PROMPT + LS * b + LS],
                                     io["sgu_b_s"][j:j + 1, :, 0:LS]).then_inc(s.loaded, 16)
                    sp.wait_ge(s.zero, 1)
                    for b in range(NB):
                        c = slice(LS * b, LS * b + LS)
                        sp.dma_start(w_ms[c, :, c], io["sgu_w_sT"][j].rearrange("g s t -> s g t")[0:LS, :, 0:LS]
                                     ).then_inc(s.spread, 16)
                    sp.wait_ge(s.loaded, 16 * 15)

                @block.gpsimd
                def _(pool):
                    nc.gpsimd.memset(w_ms[:], 0.0).then_inc(s.zero, 1)
                    pool.wait_ge(s.loaded, 16 * 15)
                    nc.gpsimd.affine_select(out=w_m[:], in_=w_m[:], compare_op=ALU.is_ge, fill=0.0, base=0,
                                            pattern=[[0, 4], [1, 128]], channel_multiplier=-1)
                    pool.wait_ge(s.spread, 16 * NB)
                    nc.gpsimd.affine_select(out=w_ms[:], in_=w_ms[:], compare_op=ALU.is_ge, fill=0.0, base=0,
                                            pattern=[[0, 4], [1, SAMPLE]], channel_multiplier=-1)

            jobs = [job(GROUP * g, "feature", lambda f, g=g: u_T[:, 4 * g + f, :], ACT.Gelu_apprx_tanh,
                        b_col[:, 4 * g:4 * g + 4]) for g in range(2)]
            jobs += [job(D + GROUP * g, "token", lambda i, g=g: v[0:ROWS[i], i, GROUP * g:GROUP * g + GROUP],
                         ACT.Gelu_apprx_tanh, b_row[:, D + GROUP * g:D + GROUP * g + GROUP]) for g in range(2)]
            project_in(w_in, jobs)

            with phase("step", "var", "std", "gain", "ready", "mix", "mix_used", "stored") as (block, s):
                st = sb("st", [128, 3, 2, 6], ctx=ctx)
                mv = sb("mv", [128, 3, 2], ctx=ctx)
                sd = sb("sd", [128, 3], ctx=ctx)
                rs = sb("rs", [128, 3], ctx=ctx)

                @block.vector
                def _(dve):
                    link = linker(dve, s.step)
                    for i, (t0, r) in enumerate(TILES):
                        nc.vector.bn_stats(out=st[0:r, i, 0, :], in_=v[0:r, i, 0:512])
                        link(nc.vector.bn_stats(out=st[0:r, i, 1, :], in_=v[0:r, i, 512:1024]))
                        nc.vector.bn_aggr(out=mv[0:r, i, :], in_=st[0:r, i, :, :].rearrange("p a b -> p (a b)")
                                          ).then_inc(s.var, 1)
                    for i, (t0, r) in enumerate(TILES):
                        row = v[0:r, i, :]
                        dve.wait_ge(s.var, 3)
                        dve.wait_ge(s.std, i + 1)
                        link(nc.vector.reciprocal(rs[0:r, i:i + 1], sd[0:r, i:i + 1]))
                        link(nc.vector.tensor_scalar(row, row, mv[0:r, i, 0:1], rs[0:r, i:i + 1],
                                                     ALU.subtract, ALU.mult))
                        nc.vector.tensor_tensor(row, row, vg[0:r, :], ALU.mult).then_inc(s.gain, 1)
                    for f in range(KT):
                        dve.wait_ge(s.mix, f + 1)
                        nc.vector.tensor_tensor(u_T[:, f, :], u_T[:, f, :], ps[:, f % 6, 0:T], ALU.mult
                                                ).then_inc(s.mix_used, 1)

                @block.gpsimd
                def _(pool):
                    for i, (t0, r) in enumerate(TILES):
                        pool.wait_ge(s.gain, i + 1)
                        nc.gpsimd.tensor_tensor(v[0:r, i, :], v[0:r, i, :], vb[0:r, :], ALU.add
                                                ).then_inc(s.ready, 1)

                @block.scalar
                def _(act):
                    for i, (t0, r) in enumerate(TILES):
                        act.wait_ge(s.var, i + 1)
                        nc.scalar.activation(sd[0:r, i:i + 1], mv[0:r, i, 1:2], ACT.Sqrt, bias=eps[0:r, :]
                                             ).then_inc(s.std, 1)

                @block.tensor
                def _(pe):
                    pe.wait_ge(s.ready, 3)
                    for f in range(KT):
                        if f >= 6:
                            pe.wait_ge(s.mix_used, f - 5)
                        for i, (t0, r) in enumerate(TILES):
                            w = w_m[:, f // 2, :] if i < 2 else w_ms[:, f // 2, :]
                            nc.tensor.matmul(ps[:, f % 6, t0:t0 + r], v[0:r, i, 128 * f:128 * f + 128], w,
                                             start=(i == 0), stop=False, skip_group_check=True)
                        last = nc.tensor.matmul(ps[:, f % 6, 0:T], ones[:], b_s[:, f // 2, :], start=False,
                                                stop=True, skip_group_check=True)
                        last.then_inc(s.mix, 1)

                @block.sync
                def _(sp):
                    sp.wait_ge(s.ready, 3)
                    sp.dma_start(out[6][j].rearrange("b l d -> (b l) d"), v[0:SAMPLE, 2, :]).then_inc(s.stored, 16)
                    sp.wait_ge(s.stored, 16)

            project_out(w_out, u_T, KT)
        residual_norm(layer, 0)

    def recurrent(kd, width, chunks, att, qc, qm, kp, km, dec, v, gate_T, gain, centre, state_in, state_out_p,
                  state_out_s):
        nchunk = len(chunks)
        units = []
        for h in range(H):
            units += [(h, "p", c, k) for c in range(nchunk) for k in range(kd)]
            units += [(h, "s", b, k) for b in range(NB) for k in range(kd)]
        at = {u: n for n, u in enumerate(units)}
        et = width // 128
        S0, S1 = 3, 3
        with ExitStack() as ctx, phase("in0", "in1", "in2", "o0", "o1", "o2", "p_out", "kv", "state",
                                       "heads", "step", "var", "std", "norm", "tp", "tp_used") as (block, s):
            st_p = sb("st_p", [128, 2, kd, width], ctx=ctx)
            s_in = sb("s_in", [128, S0, kd, width], ctx=ctx)
            s_new = sb("s_new", [128, S1, kd, width], ctx=ctx)
            o_n = sb("o_n", [128, 3, width], ctx=ctx)
            bst = sb("bst", [128, 3, 6], ctx=ctx)
            mv = sb("mv", [128, H, 3, 2], ctx=ctx)
            ms = sb("ms", [128, H, 3], ctx=ctx)
            sd = sb("sd", [128, H, 3], ctx=ctx)
            rs = sb("rs", [128, H, 3], ctx=ctx)
            sin = (s.in0, s.in1, s.in2)
            sout = (s.o0, s.o1, s.o2)
            KV, TP = (3, 4), (5, 6)

            @block.sync
            def _(sp):
                def load(n):
                    h, b = divmod(n, NB)
                    sp.dma_start(s_in[:, n % S0], state_in[b, h].rearrange("(k p) e -> p k e", p=128)
                                 ).then_inc(sin[n % S0], 16)
                for n in range(S0):
                    load(n)
                for h in range(H):
                    sp.wait_ge(s.state, at[(h, "p", nchunk - 1, kd - 1)] + 1)
                    sp.dma_start(state_out_p[0, h].rearrange("(k p) e -> p k e", p=128),
                                 st_p[:, (nchunk - 1) % 2]).then_inc(s.p_out, 16)
                    for b in range(NB):
                        n = h * NB + b
                        sp.wait_ge(s.state, at[(h, "s", b, kd - 1)] + 1)
                        sp.dma_start(state_out_s[b, h].rearrange("(k p) e -> p k e", p=128), s_new[:, n % S1]
                                     ).then_inc(sout[n % S1], 16)
                        if n + S0 < H * NB:
                            load(n + S0)
                sp.wait_ge(s.p_out, 16 * H)
                for m, q in enumerate(sout):
                    sp.wait_ge(q, 16 * len(range(m, H * NB, S1)))

            @block.tensor
            def _(pe):
                def update(u, lhs, rhs):
                    n = at[u]
                    if n >= 2:
                        pe.wait_ge(s.state, n - 1)
                    nc.tensor.matmul(ps[:, KV[n % 2], 0:width], lhs, rhs, start=True, stop=True).then_inc(s.kv, 1)

                def turn(h):
                    pe.wait_ge(s.norm, 3 * (h + 1))
                    for f in range(et):
                        n = h * et + f
                        if n >= 2:
                            pe.wait_ge(s.tp_used, n - 1)
                        for i, (t0, r) in enumerate(TILES):
                            last = nc.tensor.transpose(ps[:, TP[n % 2], t0:t0 + r],
                                                       o_n[0:r, i, 128 * f:128 * f + 128], ident[0:r, 0:r])
                        last.then_inc(s.tp, 1)

                for h in range(H):
                    ve = slice(h * width, (h + 1) * width)
                    if h:
                        turn(h - 1)
                    for i in range(2):
                        mine = [c for c in range(nchunk) if chunks[c][0] == i]
                        crossing = [c for c in mine if c > 0]
                        nc.tensor.matmul(ps[:, i, 0:width], att[:, h, i, :], v[:, i, ve], start=True,
                                         stop=not crossing)
                        for c in mine:
                            lo, hi = chunks[c][1:]
                            if c > 0:
                                pe.wait_ge(s.state, at[(h, "p", c - 1, kd - 1)] + 1)
                                for k in range(kd):
                                    nc.tensor.matmul(ps[:, i, 0:width], qc[:, h, k, c - 1, :],
                                                     st_p[:, (c - 1) % 2, k, :], start=False,
                                                     stop=(c == crossing[-1] and k == kd - 1))
                            for k in range(kd):
                                update((h, "p", c, k), kp[lo:hi, i, h, 128 * k:128 * k + 128], v[lo:hi, i, ve])
                    nc.tensor.matmul(ps[0:SAMPLE, 2, 0:width], att[0:SAMPLE, h, 2, 0:SAMPLE], v[0:SAMPLE, 2, ve],
                                     start=True, stop=False)
                    for b in range(NB):
                        n = h * NB + b
                        pe.wait_ge(sin[n % S0], 16 * (n // S0 + 1))
                        for k in range(kd):
                            last = nc.tensor.matmul(ps[0:SAMPLE, 2, 0:width], qm[:, h, k, b, :],
                                                    s_in[:, n % S0, k, :], start=False,
                                                    stop=(b == NB - 1 and k == kd - 1))
                        if b == NB - 1:
                            last.then_inc(s.heads, 1)
                        for k in range(kd):
                            update((h, "s", b, k), km[:, b, h, 128 * k:128 * k + 128], v[0:SAMPLE, 2, ve])
                turn(H - 1)

            @block.vector
            def _(dve):
                link = linker(dve, s.step)
                for h in range(H):
                    for c in range(nchunk):
                        for k in range(kd):
                            n = at[(h, "p", c, k)]
                            dve.wait_ge(s.kv, n + 1)
                            if c == (nchunk - 1) % 2 and h and k == 0:
                                dve.wait_ge(s.p_out, 16 * h)
                            dst = st_p[:, c % 2, k, :]
                            if c == 0:
                                nc.vector.tensor_copy(dst, ps[:, KV[n % 2], 0:width]).then_inc(s.state, 1)
                            else:
                                dve.wait_ge(s.state, at[(h, "p", c - 1, k)] + 1)
                                nc.vector.scalar_tensor_tensor(out=dst, in0=st_p[:, (c - 1) % 2, k, :],
                                                               scalar=dec[:, h, c:c + 1],
                                                               in1=ps[:, KV[n % 2], 0:width], op0=ALU.mult,
                                                               op1=ALU.add).then_inc(s.state, 1)
                    for b in range(NB):
                        m = h * NB + b
                        dve.wait_ge(sin[m % S0], 16 * (m // S0 + 1))
                        if m >= S1:
                            dve.wait_ge(sout[m % S1], 16 * (m // S1))
                        for k in range(kd):
                            n = at[(h, "s", b, k)]
                            dve.wait_ge(s.kv, n + 1)
                            nc.vector.scalar_tensor_tensor(out=s_new[:, m % S1, k, :], in0=s_in[:, m % S0, k, :],
                                                           scalar=dec[:, h, nchunk + b:nchunk + b + 1],
                                                           in1=ps[:, KV[n % 2], 0:width], op0=ALU.mult,
                                                           op1=ALU.add).then_inc(s.state, 1)
                    dve.wait_ge(s.heads, h + 1)
                    for i, (t0, r) in enumerate(TILES):
                        link(nc.vector.bn_stats(out=bst[0:r, i, :], in_=ps[0:r, i, 0:width]))
                        link(nc.vector.bn_aggr(out=mv[0:r, h, i, :], in_=bst[0:r, i, :]))
                        if centre:
                            ins = nc.vector.tensor_copy(ms[0:r, h, i:i + 1], mv[0:r, h, i, 1:2])
                        else:
                            ins = nc.vector.scalar_tensor_tensor(out=ms[0:r, h, i:i + 1], in0=mv[0:r, h, i, 0:1],
                                                                 scalar=mv[0:r, h, i, 0:1], in1=mv[0:r, h, i, 1:2],
                                                                 op0=ALU.mult, op1=ALU.add)
                        ins.then_inc(s.var, 1)
                    if h:
                        dve.wait_ge(s.tp, h * et)
                    for i, (t0, r) in enumerate(TILES):
                        dve.wait_ge(s.std, 3 * h + i + 1)
                        link(nc.vector.reciprocal(rs[0:r, h, i:i + 1], sd[0:r, h, i:i + 1]))
                        if centre:
                            ins = nc.vector.tensor_scalar(o_n[0:r, i, :], ps[0:r, i, 0:width], mv[0:r, h, i, 0:1],
                                                          rs[0:r, h, i:i + 1], ALU.subtract, ALU.mult)
                        else:
                            ins = nc.vector.tensor_scalar(o_n[0:r, i, :], ps[0:r, i, 0:width],
                                                          rs[0:r, h, i:i + 1], None, ALU.mult)
                        ins.then_inc(s.norm, 1)
                    for f in range(et):
                        n = h * et + f
                        dve.wait_ge(s.tp, n + 1)
                        nc.vector.scalar_tensor_tensor(out=gate_T[:, n, :], in0=ps[:, TP[n % 2], 0:T],
                                                       scalar=gain[:, n:n + 1], in1=gate_T[:, n, :], op0=ALU.mult,
                                                       op1=ALU.mult).then_inc(s.tp_used, 1)

            @block.scalar
            def _(act):
                for h in range(H):
                    for i, (t0, r) in enumerate(TILES):
                        act.wait_ge(s.var, 3 * h + i + 1)
                        nc.scalar.activation(sd[0:r, h, i:i + 1], ms[0:r, h, i:i + 1], ACT.Sqrt, bias=eps[0:r, :]
                                             ).then_inc(s.std, 1)

    def retention(j, layer):
        with ExitStack() as cg:
            g_T = sb("g_T", [128, 16, T], ctx=cg)
            with ExitStack() as ctx:
                v = sb("v", [128, 3, 2048], ctx=ctx)
                q_T = sb("q_T", [128, H, 2, T], ctx=ctx)
                k_T = sb("k_T", [128, H, 2, T], ctx=ctx)
                jobs = [job(GROUP * g, "feature",
                            lambda f, g=g: (q_T if g < 2 else k_T)[:, (4 * g + f) % 8 // 2, f % 2, :])
                        for g in range(4)]
                jobs += [job(2048 + GROUP * g, "token", lambda i, g=g: v[0:ROWS[i], i, GROUP * g:GROUP * g + GROUP])
                         for g in range(4)]
                jobs += [job(4096 + GROUP * g, "feature", lambda f, g=g: g_T[:, 4 * g + f, :], ACT.Silu)
                         for g in range(4)]
                project_in(io["ret_w_in"][j], jobs)

                att = sb("att", [128, H, 3, 128], ctx=ctx)
                qc = sb("qc", [128, H, 2, 1, 128], ctx=ctx)
                qm = sb("qm", [128, H, 2, NB, SAMPLE], ctx=ctx)
                kp = sb("kp", [128, 2, H, 256], ctx=ctx)
                dec = sb("dec", [128, H, 2 + NB], ctx=ctx)
                gain = sb("gain", [128, 16], ctx=ctx)
                km = sb("km", [SAMPLE, NB, H, 256], ctx=ctx)
                with ExitStack() as cq:
                    with phase("loaded", "step", "pstep", "q_rot", "k_rot", "sc", "sc_used", "kt", "kt_used", "qs"
                               ) as (block, s):
                        cos = sb("cos", [128, T], ctx=cq)
                        sin = sb("sin", [128, T], ctx=cq)
                        cross = sb("cross", [128, H, T], ctx=cq)
                        decay = sb("decay", [128, H, 128], ctx=cq)
                        decay_s = sb("decay_s", [SAMPLE, H, SAMPLE], ctx=cq)
                        keep = sb("keep", [128, 3, H], ctx=cq)
                        keep_s = sb("keep_s", [SAMPLE, NB, H], ctx=cq)
                        memcol = sb("memcol", [128, NB, SAMPLE], ctx=cq)
                        tmp_q = sb("tmp_q", [128, 2, H, T], ctx=cq)
                        tmp_k = sb("tmp_k", [128, 2, H, T], ctx=cq)
                        n_load = 10

                        @block.sync
                        def _(sp):
                            for dst, src in ((cos, "c_cos"), (sin, "c_sin"), (cross, "c_cross"), (decay, "c_decay"),
                                             (decay_s, "c_decay_s"), (keep, "c_kd"), (keep_s, "c_kdm"),
                                             (memcol, "c_memcol"), (dec, "c_dec")):
                                sp.dma_start(dst[:], io[src]).then_inc(s.loaded, 16)
                            sp.dma_start(gain[:], io["ret_gain"][j]).then_inc(s.loaded, 16)

                        def rotate(tt, link, a, tmp):
                            a0, a1 = a[:, :, 0, :], a[:, :, 1, :]
                            c = cos[:].rearrange("p (o t) -> p o t", o=1).to_broadcast([128, H, T])
                            n = sin[:].rearrange("p (o t) -> p o t", o=1).to_broadcast([128, H, T])
                            tt(tmp[:, 0], a1, n, ALU.mult)
                            link(tt(tmp[:, 1], a0, n, ALU.mult))
                            tt(a0, a0, c, ALU.mult)
                            link(tt(a1, a1, c, ALU.mult))
                            tt(a0, a0, tmp[:, 0], ALU.subtract)
                            return tt(a1, a1, tmp[:, 1], ALU.add)

                        @block.vector
                        def _(dve):
                            link = linker(dve, s.step)
                            dve.wait_ge(s.loaded, 16 * n_load)
                            rotate(nc.vector.tensor_tensor, link, q_T, tmp_q).then_inc(s.q_rot, 1)
                            dve.wait_ge(s.q_rot, 1)
                            for k in range(2):
                                nc.vector.tensor_tensor(qc[:, :, k, 0, :], q_T[:, :, k, 128:256], cross[:, :, 128:256],
                                                        ALU.mult)
                                nc.vector.tensor_tensor(tmp_q[:, k, :, 0:SAMPLE], q_T[:, :, k, PROMPT:T],
                                                        cross[:, :, PROMPT:T], ALU.mult).then_inc(s.qs, 1)
                            dve.wait_ge(s.qs, 2)
                            for h in range(H):
                                for k in range(2):
                                    nc.vector.tensor_tensor(
                                        qm[:, h, k, :, :],
                                        tmp_q[:, k, h, 0:SAMPLE].rearrange("p (o t) -> p o t", o=1)
                                        .to_broadcast([128, NB, SAMPLE]), memcol[:], ALU.mult)
                            for h in range(H):
                                for i in range(3):
                                    r = ROWS[i]
                                    n = 3 * h + i
                                    dve.wait_ge(s.sc, n + 1)
                                    nc.vector.tensor_tensor(att[0:r, h, i, 0:r], ps[0:r, n % 2, 0:r],
                                                            (decay if i < 2 else decay_s)[:, h, :], ALU.mult
                                                            ).then_inc(s.sc_used, 1)
                            for i in range(3):
                                r = ROWS[i]
                                for q in range(2):
                                    n = 2 * i + q
                                    dve.wait_ge(s.kt, n + 1)
                                    for e in range(2):
                                        h = 2 * q + e
                                        src = ps[0:r, 2 + n % 2, 256 * e:256 * e + 256]
                                        if i < 2:
                                            last = nc.vector.tensor_scalar(kp[:, i, h, :], src, keep[:, i, h:h + 1],
                                                                           None, ALU.mult)
                                        else:
                                            for b in range(NB):
                                                last = nc.vector.tensor_scalar(km[:, b, h, :], src,
                                                                               keep_s[:, b, h:h + 1], None, ALU.mult)
                                    last.then_inc(s.kt_used, 1)

                        @block.gpsimd
                        def _(pool):
                            link = linker(pool, s.pstep)
                            pool.wait_ge(s.loaded, 16 * n_load)
                            rotate(nc.gpsimd.tensor_tensor, link, k_T, tmp_k).then_inc(s.k_rot, 1)

                        @block.tensor
                        def _(pe):
                            pe.wait_ge(s.q_rot, 1)
                            pe.wait_ge(s.k_rot, 1)
                            for h in range(H):
                                for i, (t0, r) in enumerate(TILES):
                                    n = 3 * h + i
                                    if n >= 2:
                                        pe.wait_ge(s.sc_used, n - 1)
                                    for k in range(2):
                                        last = nc.tensor.matmul(ps[0:r, n % 2, 0:r], k_T[:, h, k, t0:t0 + r],
                                                                q_T[:, h, k, t0:t0 + r], start=(k == 0), stop=(k == 1))
                                    last.then_inc(s.sc, 1)
                            for i, (t0, r) in enumerate(TILES):
                                for q in range(2):
                                    n = 2 * i + q
                                    if n >= 2:
                                        pe.wait_ge(s.kt_used, n - 1)
                                    for e in range(4):
                                        last = nc.tensor.transpose(ps[0:r, 2 + n % 2, 128 * e:128 * e + 128],
                                                                   k_T[:, 2 * q + e // 2, e % 2, t0:t0 + r], ident[:])
                                    last.then_inc(s.kt, 1)
                recurrent(2, 512, [(0, 0, 128), (1, 0, 128)], att, qc, qm, kp, km, dec, v, g_T, gain, True,
                          io["state_ret"][j], out[2][j], out[3][j])
            project_out(io["ret_w_out"][j], g_T, 16)
        residual_norm(layer, 0)

    def gla(j, layer):
        with ExitStack() as cg:
            g_T = sb("g_T", [128, 8, T], ctx=cg)
            with ExitStack() as ctx:
                v = sb("v", [128, 3, D], ctx=ctx)
                att = sb("att", [128, H, 3, 128], ctx=ctx)
                qc = sb("qc", [128, H, 1, 3, 128], ctx=ctx)
                qm = sb("qm", [128, H, 1, NB, SAMPLE], ctx=ctx)
                kp = sb("kp", [128, 2, H, 128], ctx=ctx)
                km = sb("km", [SAMPLE, NB, H, 128], ctx=ctx)
                dec = sb("dec", [128, H, 4 + NB], ctx=ctx)
                gain = sb("gain", [128, 8], ctx=ctx)
                with ExitStack() as cq:
                    q_T = sb("q_T", [128, H, T], ctx=cq)
                    k_T = sb("k_T", [128, H, T], ctx=cq)
                    a_T = sb("a_T", [16, T], ctx=cq)
                    jobs = [job(0, "feature", lambda f: q_T[:, f, :], scale=128 ** -0.5),
                            job(GROUP, "feature", lambda f: k_T[:, f, :])]
                    jobs += [job(1024 + GROUP * g, "token", lambda i, g=g: v[0:ROWS[i], i, GROUP * g:GROUP * g + GROUP])
                             for g in range(2)]
                    jobs += [job(2048 + GROUP * g, "feature", lambda f, g=g: g_T[:, 4 * g + f, :], ACT.Silu)
                             for g in range(2)]
                    jobs += [job(3072, "feature", lambda f: a_T[:], width=16)]
                    project_in(io["gla_w_in"][j], jobs)

                    with phase("loaded", "step", "z", "z_sb", "az", "ez", "l1", "cum", "dif", "mag", "ex", "lev", "sc",
                               "sc_used", "acc", "qe", "kt", "kt_used", "kdec", "zero") as (block, s):
                        w_a2 = sb("w_a2", [16, 512], ctx=cq)
                        b_a = sb("b_a", [128, H], ctx=cq)
                        start = sb("start", [128, T], ctx=cq)
                        levels = sb("levels", [128, LEVELS, 128], ctx=cq)
                        memcol = sb("memcol", [128, NB, SAMPLE], ctx=cq)
                        member = sb("member", [SAMPLE, NB], ctx=cq)
                        z = sb("z", [128, H, T], ctx=cq)
                        az = sb("az", [128, H, T], ctx=cq)
                        cum = sb("cum", [128, H, T], ctx=cq)
                        dif = sb("dif", [128, H, T], ctx=cq)
                        ex = sb("ex", [128, H, T], ctx=cq)
                        ql = sb("ql", [128, 2, H, T], ctx=cq)
                        kl = sb("kl", [128, 2, H, T], ctx=cq)
                        tmp = sb("tmp", [128, H, 128], ctx=cq)
                        last_b = sb("last_b", [128, H, 4 + NB], ctx=cq)
                        units = [(lv, i) for lv in range(LEVELS) for i in range(3) if i < 2 or lv <= 3]

                        @block.sync
                        def _(sp):
                            for dst, src in ((w_a2, io["gla_w_a2"][j]), (b_a, io["gla_b_col"][j]), (start, io["c_start"]),
                                             (levels, io["c_levels"]), (memcol, io["c_memcol"]),
                                             (member, io["c_member"]), (gain, io["gla_gain"][j])):
                                sp.dma_start(dst[:], src).then_inc(s.loaded, 16)

                        @block.tensor
                        def _(pe):
                            pe.wait_ge(s.loaded, 16 * 7)
                            for h in range(H):
                                nc.tensor.matmul(ps[:, h, 0:T], w_a2[:, 128 * h:128 * h + 128], a_T[:], start=True,
                                                 stop=True).then_inc(s.z, 1)
                            for n, (lv, i) in enumerate(units):
                                t0, r = TILES[i]
                                pe.wait_ge(s.lev, lv + 1)
                                if n >= 2:
                                    pe.wait_ge(s.sc_used, n - 1)
                                q, k = (q_T, k_T) if lv == 0 else (ql[:, lv % 2], kl[:, lv % 2])
                                for h in range(H):
                                    last = nc.tensor.matmul(ps[0:r, 4 + n % 2, 128 * h:128 * h + r], k[:, h, t0:t0 + r],
                                                            q[:, h, t0:t0 + r], start=True, stop=True)
                                last.then_inc(s.sc, 1)
                            pe.wait_ge(s.kdec, 1)
                            for i, (t0, r) in enumerate(TILES):
                                if i >= 2:
                                    pe.wait_ge(s.kt_used, 1)
                                for h in range(H):
                                    last = nc.tensor.transpose(ps[0:r, 6 + i % 2, 128 * h:128 * h + 128],
                                                               az[:, h, t0:t0 + r], ident[:])
                                last.then_inc(s.kt, 1)

                        @block.scalar
                        def _(act):
                            for h in range(H):
                                act.wait_ge(s.z, h + 1)
                                nc.scalar.activation(z[:, h, :], ps[:, h, 0:T], ACT.Identity, bias=b_a[:, h:h + 1]
                                                     ).then_inc(s.z_sb, 1)
                            act.wait_ge(s.z_sb, H)
                            nc.scalar.activation(az[:], z[:], ACT.Abs).then_inc(s.az, 1)
                            act.wait_ge(s.az, 1)
                            nc.scalar.activation(ex[:], az[:], ACT.Exp, scale=-1.0).then_inc(s.ez, 1)
                            act.wait_ge(s.ez, 1)
                            nc.scalar.activation(dif[:], ex[:], ACT.Ln, bias=1.0).then_inc(s.l1, 1)
                            for lv in range(1, LEVELS):
                                act.wait_ge(s.dif, lv)
                                nc.scalar.activation(dif[:], dif[:], ACT.Abs).then_inc(s.mag, 1)
                                act.wait_ge(s.mag, lv)
                                if lv > 1:
                                    act.wait_ge(s.lev, lv)
                                nc.scalar.activation(ex[:], dif[:], ACT.Exp, scale=-1.0 / 16).then_inc(s.ex, 1)
                            act.wait_ge(s.dif, LEVELS)
                            act.wait_ge(s.lev, LEVELS)
                            nc.scalar.activation(ex[:], dif[:], ACT.Exp, scale=-1.0 / 16).then_inc(s.ex, 1)
                            act.wait_ge(s.kdec, 1)
                            nc.scalar.activation(dif[:], cum[:], ACT.Exp, scale=1.0 / 16).then_inc(s.ex, 1)
                            nc.scalar.activation(dec[:], last_b[:], ACT.Exp, scale=1.0 / 16)

                        @block.gpsimd
                        def _(pool):
                            nc.gpsimd.memset(qc[:], 0.0).then_inc(s.zero, 1)

                        @block.vector
                        def _(dve):
                            link = linker(dve, s.step)
                            dve.wait_ge(s.z_sb, H)
                            dve.wait_ge(s.az, 1)
                            link(nc.vector.tensor_scalar_min(z[:], z[:], 0.0))
                            dve.wait_ge(s.l1, 1)
                            link(nc.vector.tensor_tensor(z[:], z[:], dif[:], ALU.subtract))
                            for h in range(H):
                                nc.vector.tensor_tensor_scan(cum[:, h, :], start[:], z[:, h, :], 0.0, ALU.mult, ALU.add
                                                             ).then_inc(s.cum, 1)
                            dve.wait_ge(s.cum, H)
                            nc.vector.tensor_copy(last_b[:, :, 0:4], cum[:, :, 63:PROMPT:64])
                            nc.vector.tensor_copy(last_b[:, :, 4:4 + NB], cum[:, :, PROMPT + LS - 1:T:LS]
                                                  ).then_inc(s.lev, 1)

                            def spread(b):
                                size = 2 ** b
                                a = cum[:].rearrange("p h (n c) -> p (h n) c", c=size)
                                o = dif[:].rearrange("p h (n c) -> p (h n) c", c=size)
                                mid = a[:, :, size // 2 - 1:size // 2].to_broadcast([128, H * T // size, size])
                                return nc.vector.tensor_tensor(o, a, mid, ALU.subtract)

                            n = 0
                            for lv in range(LEVELS):
                                if lv:
                                    if lv > 1:
                                        dve.wait_ge(s.ex, lv - 1)
                                    spread(lv).then_inc(s.dif, 1)
                                    dve.wait_ge(s.ex, lv)
                                    if lv > 2:
                                        dve.wait_ge(s.sc, [m for m, u in enumerate(units) if u[0] == lv - 2][-1] + 1)
                                    nc.vector.tensor_tensor(ql[:, lv % 2], q_T[:], ex[:], ALU.mult)
                                    nc.vector.tensor_tensor(kl[:, lv % 2], k_T[:], ex[:], ALU.mult).then_inc(s.lev, 1)
                                for (l2, i) in units:
                                    if l2 != lv:
                                        continue
                                    t0, r = TILES[i]
                                    dve.wait_ge(s.sc, n + 1)
                                    src = ps[0:r, 4 + n % 2, :].rearrange("p (h t) -> p h t", h=H)[:, :, 0:r]
                                    mask = levels[0:r, lv:lv + 1, 0:r].to_broadcast([r, H, r])
                                    if lv == 0:
                                        nc.vector.tensor_tensor(att[0:r, :, i, 0:r], src, mask, ALU.mult
                                                                ).then_inc(s.sc_used, 1)
                                    else:
                                        nc.vector.tensor_tensor(tmp[0:r, :, 0:r], src, mask, ALU.mult
                                                                ).then_inc(s.sc_used, 1)
                                        dve.wait_ge(s.sc_used, n + 1)
                                        link(nc.vector.tensor_tensor(att[0:r, :, i, 0:r], att[0:r, :, i, 0:r],
                                                                     tmp[0:r, :, 0:r], ALU.add))
                                    n += 1
                            dve.wait_ge(s.ex, LEVELS - 1)
                            for c in range(4):
                                cc = slice(64 * c, 64 * c + 64)
                                nc.vector.tensor_tensor(dif[:, :, cc], cum[:, :, cc],
                                                        cum[:, :, 64 * c + 63:64 * c + 64].to_broadcast([128, H, 64]),
                                                        ALU.subtract)
                            for h in range(H):
                                a = cum[:, h, PROMPT:T].rearrange("p (n c) -> p n c", c=LS)
                                ins = nc.vector.tensor_tensor(dif[:, h, PROMPT:T].rearrange("p (n c) -> p n c", c=LS), a,
                                                              a[:, :, LS - 1:LS].to_broadcast([128, NB, LS]),
                                                              ALU.subtract)
                            ins.then_inc(s.dif, 1)
                            dve.wait_ge(s.ex, LEVELS)
                            nc.vector.tensor_tensor(az[:], k_T[:], ex[:], ALU.mult).then_inc(s.kdec, 1)
                            dve.wait_ge(s.ex, LEVELS + 1)
                            link(nc.vector.tensor_tensor(z[:], q_T[:], dif[:], ALU.mult))
                            dve.wait_ge(s.zero, 1)
                            for c in range(1, 4):
                                o = 64 * (c % 2)
                                nc.vector.tensor_copy(qc[:, :, 0, c - 1, o:o + 64], z[:, :, 64 * c:64 * c + 64])
                            for h in range(H):
                                nc.vector.tensor_tensor(
                                    qm[:, h, 0, :, :], z[:, h, PROMPT:T].rearrange("p (o t) -> p o t", o=1)
                                    .to_broadcast([128, NB, SAMPLE]), memcol[:], ALU.mult)
                            for i in range(3):
                                dve.wait_ge(s.kt, i + 1)
                                src = ps[0:ROWS[i], 6 + i % 2, :]
                                if i < 2:
                                    nc.vector.tensor_copy(kp[:, i, :, :], src.rearrange("p (h d) -> p h d", h=H)
                                                          ).then_inc(s.kt_used, 1)
                                else:
                                    for b in range(NB):
                                        nc.vector.tensor_scalar(km[:, b, :, :], src.rearrange("p (h d) -> p h d", h=H),
                                                                member[:, b:b + 1], None, ALU.mult)
                recurrent(1, 256, [(0, 0, 64), (0, 64, 128), (1, 0, 64), (1, 64, 128)], att, qc, qm, kp, km, dec, v, g_T,
                          gain, False, io["state_gla"][j], out[4][j], out[5][j])
            project_out(io["gla_w_out"][j], g_T, 8)
        residual_norm(layer, 0)

    def peer(layer):
        with ExitStack() as ctx:
            ea_T = sb("ea_T", [128, T], ctx=ctx)
            eb_T = sb("eb_T", [128, T], ctx=ctx)
            gh_T = sb("gh_T", [128, T], F16, ctx=ctx)
            gl_T = sb("gl_T", [128, T], F16, ctx=ctx)
            iota = sb("iota", [128, NK], ctx=ctx)
            with ExitStack() as cr:
                q_T = sb("q_T", [128, 2 * PH, T], ctx=cr)
                project_in(io["peer_w_q"][layer],
                           [job(GROUP * g, "feature", lambda f, g=g: q_T[:, 4 * g + f, :]) for g in range(4)])
                peer_route(layer, q_T, ea_T, eb_T, gh_T, gl_T, iota, cr)
            peer_experts(layer, ea_T, eb_T, gh_T, gl_T, iota)
            y_T = sb("y_T", [128, KT, T], ctx=ctx)
            with phase("moved", "x") as (block, s):
                @block.scalar
                def _(act):
                    scale = W_SCALE / (V_SCALE * G_SCALE)
                    nc.scalar.activation(y_T[:, :, 0:PROMPT], ps[:, 0:4, :].rearrange("p a (b t) -> p (a b) t", b=2),
                                         ACT.Copy, scale=scale)
                    nc.scalar.activation(y_T[:, :, PROMPT:T], ps[:, 4, :].rearrange("p (b t) -> p b t", b=KT),
                                         ACT.Copy, scale=scale)
            with phase("x") as (block, s):
                @block.tensor
                def _(pe):
                    for i, (t0, r) in enumerate(TILES):
                        for f in range(KT):
                            nc.tensor.transpose(ps[0:r, 2 * i + f // 4, 128 * (f % 4):128 * (f % 4) + 128],
                                                y_T[:, f, t0:t0 + r], ident[:])
        residual_norm(layer, 1)

    def peer_route(layer, q_T, ea_T, eb_T, gh_T, gl_T, iota, ctx):
        with phase("loaded", "sc", "sc_sb", "free", "step", "shift", "exp", "ready", "tp", "tp_used", "hi") as (block, s):
            keys = sb("keys", [128, 2, NK], ctx=ctx)
            sc = sb("sc", [128, 2 * PH, NK], ctx=ctx)
            sc2 = sb("sc2", [128, 2 * PH, NK], ctx=ctx)
            val = sb("val", [128, PH, 2, PK], ctx=ctx)
            idx = sb("idx", [128, PH, 2, PK], U32, ctx=ctx)
            idf = sb("idf", [128, PH, 2, PK], ctx=ctx)
            cand = sb("cand", [128, PH, PK, PK], ctx=ctx)
            cand2 = sb("cand2", [128, PH, PK, PK], ctx=ctx)
            best = sb("best", [128, PH, PK], ctx=ctx)
            ci = sb("ci", [128, PH, PK], U32, ctx=ctx)
            ij = sb("ij", [128, 2, PH, PK], U32, ctx=ctx)
            ijf = sb("ijf", [128, 2, PH, PK], ctx=ctx)
            pick = sb("pick", [128, 3, PH, PK], ctx=ctx)
            tot = sb("tot", [128, PH], ctx=ctx)
            inv = sb("inv", [128, PH], ctx=ctx)
            gt_T = sb("gt_T", [128, T], ctx=ctx)
            dsts = (ea_T, eb_T, gt_T)

            @block.sync
            def _(sp):
                sp.dma_start(keys[:, 0, :], io["peer_keys_aT"][layer]).then_inc(s.loaded, 16)
                sp.dma_start(keys[:, 1, :], io["peer_keys_bT"][layer]).then_inc(s.loaded, 16)
                sp.dma_start(iota[:], io["c_iota"]).then_inc(s.loaded, 16)

            @block.tensor
            def _(pe):
                pe.wait_ge(s.loaded, 48)

                def turn(i):
                    r = ROWS[i]
                    t0 = TILES[i][0]
                    pe.wait_ge(s.ready, i + 1)
                    if i:
                        pe.wait_ge(s.tp_used, 3 * i)
                    for m in range(3):
                        last = nc.tensor.transpose(ps[:, 4, 128 * m:128 * m + r],
                                                   pick[0:r, m].rearrange("p h k -> p (h k)"), ident[0:r, 0:r])
                    last.then_inc(s.tp, 1)

                def scores(i):
                    t0, r = TILES[i]
                    if i:
                        pe.wait_ge(s.sc_sb, 4 * i)
                    for b in range(4):
                        for e in range(4):
                            jj = 4 * b + e
                            last = nc.tensor.matmul(ps[0:r, b, 128 * e:128 * e + 128], q_T[:, jj, t0:t0 + r],
                                                    keys[:, jj % 2, :], start=True, stop=True)
                        last.then_inc(s.sc, 1)

                scores(0)
                scores(1)
                turn(0)
                scores(2)
                turn(1)
                turn(2)

            @block.scalar
            def _(act):
                def take(i):
                    r = ROWS[i]
                    if i:
                        act.wait_ge(s.free, i)
                    for b in range(4):
                        act.wait_ge(s.sc, 4 * i + b + 1)
                        nc.scalar.copy(sc[0:r, 4 * b:4 * b + 4, :],
                                       ps[0:r, b, :].rearrange("p (e n) -> p e n", e=4)).then_inc(s.sc_sb, 1)

                def finish(i):
                    t0, r = TILES[i]
                    act.wait_ge(s.shift, i + 1)
                    nc.scalar.activation(pick[0:r, 2], pick[0:r, 2], ACT.Exp).then_inc(s.exp, 1)
                    act.wait_ge(s.tp, i + 1)
                    for m in range(3):
                        nc.scalar.copy(dsts[m][:, t0:t0 + r], ps[:, 4, 128 * m:128 * m + r]).then_inc(s.tp_used, 1)

                take(0)
                take(1)
                finish(0)
                take(2)
                finish(1)
                finish(2)
                act.wait_ge(s.tp_used, 9)
                nc.scalar.copy(gh_T[:], gt_T[:]).then_inc(s.hi, 1)

            @block.vector
            def _(dve):
                link = linker(dve, s.step)

                def top16(n, src, scratch, v_of, i_of, freed=None):
                    for jj in range(n):
                        last = nc.vector.max(out=v_of(jj)[:, 0:8], in_=src(jj))
                    link(last)
                    for jj in range(n):
                        nc.vector.max_index(out=i_of(jj)[:, 0:8], in_max=v_of(jj)[:, 0:8], in_values=src(jj))
                    for jj in range(n):
                        last = nc.vector.match_replace(out=scratch(jj), in_to_replace=v_of(jj)[:, 0:8],
                                                       in_values=src(jj), imm_value=LOWEST)
                    link(last)
                    for jj in range(n):
                        last = nc.vector.max(out=v_of(jj)[:, 8:16], in_=scratch(jj))
                    link(last)
                    for jj in range(n):
                        last = nc.vector.max_index(out=i_of(jj)[:, 8:16], in_max=v_of(jj)[:, 8:16],
                                                   in_values=scratch(jj))
                    link(last)

                for i, (t0, r) in enumerate(TILES):
                    dve.wait_ge(s.sc_sb, 4 * i + 4)
                    top16(2 * PH, lambda jj: sc[0:r, jj, :], lambda jj: sc2[0:r, jj, :],
                          lambda jj: val[0:r, jj // 2, jj % 2, :], lambda jj: idx[0:r, jj // 2, jj % 2, :])
                    nc.vector.tensor_copy(idf[0:r], idx[0:r]).then_inc(s.free, 1)
                    dve.wait_ge(s.free, i + 1)
                    link(nc.vector.tensor_tensor(
                        cand[0:r], val[0:r, :, 0, :].rearrange("p h (k o) -> p h k o", o=1).to_broadcast([r, PH, PK, PK]),
                        val[0:r, :, 1:2, :].to_broadcast([r, PH, PK, PK]), ALU.add))
                    top16(PH, lambda h: cand[0:r, h].rearrange("p a b -> p (a b)"),
                          lambda h: cand2[0:r, h].rearrange("p a b -> p (a b)"),
                          lambda h: best[0:r, h, :], lambda h: ci[0:r, h, :])
                    nc.vector.tensor_single_scalar(ij[0:r, 0], ci[0:r], 4, ALU.logical_shift_right)
                    link(nc.vector.tensor_single_scalar(ij[0:r, 1], ci[0:r], PK - 1, ALU.bitwise_and))
                    link(nc.vector.tensor_copy(ijf[0:r], ij[0:r]))
                    if i:
                        dve.wait_ge(s.tp, i)
                    nc.vector.tensor_tensor(pick[0:r, 2], best[0:r], best[0:r, :, 0:1].to_broadcast([r, PH, PK]),
                                            ALU.subtract).then_inc(s.shift, 1)
                    row16 = iota[0:r, 0:PK].rearrange("p (o k) -> p o k", o=1).to_broadcast([r, PH * PK, PK])
                    if i == 0:
                        dve.wait_ge(s.loaded, 48)
                    for m in range(2):
                        link(nc.vector.tensor_tensor(
                            cand[0:r].rearrange("p h a b -> p (h a) b"),
                            ijf[0:r, m].rearrange("p h (k o) -> p (h k) o", o=1).to_broadcast([r, PH * PK, PK]),
                            row16, ALU.is_equal))
                        link(nc.vector.tensor_tensor(cand[0:r], cand[0:r],
                                                     idf[0:r, :, m:m + 1, :].to_broadcast([r, PH, PK, PK]), ALU.mult))
                        link(nc.vector.tensor_reduce(pick[0:r, m].rearrange("p h k -> p (h k)"),
                                                     cand[0:r].rearrange("p h a b -> p (h a) b"), AX, ALU.add))
                    dve.wait_ge(s.exp, i + 1)
                    link(nc.vector.tensor_reduce(tot[0:r], pick[0:r, 2], AX, ALU.add))
                    link(nc.vector.reciprocal(inv[0:r], tot[0:r]))
                    nc.vector.scalar_tensor_tensor(out=pick[0:r, 2], in0=pick[0:r, 2], scalar=G_SCALE,
                                                   in1=inv[0:r].rearrange("p (h o) -> p h o", o=1)
                                                   .to_broadcast([r, PH, PK]), op0=ALU.mult, op1=ALU.mult
                                                   ).then_inc(s.ready, 1)
                dve.wait_ge(s.hi, 1)
                nc.vector.tensor_tensor(gl_T[:], gt_T[:], gh_T[:], ALU.subtract)

    def peer_experts(layer, ea_T, eb_T, gh_T, gl_T, iota):
        u_tab, v_tab = io["peer_uT"], io["peer_v"]
        with ExitStack() as ctx, phase("u0", "u1", "v0", "v1", "uh", "ul", "vh", "vl", "h", "gelu", "w", "wh", "wl",
                                       "y", "eq", "rows", "cols", "g", "g_used") as (block, s):
            gates = sb("gates", [128, 2, QUARTER, T], ctx=ctx)
            u_in = sb("u_in", [128, 2, KT, 128], ctx=ctx)
            v_in = sb("v_in", [128, 2, D], ctx=ctx)
            u_hi = sb("u_hi", [128, 2, KT, 128], F16, ctx=ctx)
            u_lo = sb("u_lo", [128, 2, KT, 128], F16, ctx=ctx)
            v_hi = sb("v_hi", [128, 2, D], F16, ctx=ctx)
            v_lo = sb("v_lo", [128, 2, D], F16, ctx=ctx)
            ge = sb("ge", [128, 2, T], ctx=ctx)
            w = sb("w", [128, 2, T], ctx=ctx)
            w_hi = sb("w_hi", [128, 2, T], F16, ctx=ctx)
            w_lo = sb("w_lo", [128, 2, T], F16, ctx=ctx)
            hot_b = sb("hot_b", [128, 2, GT, NK], F16, ctx=ctx)
            hot = sb("hot", [128, 2, GT, QUARTER], F16, ctx=ctx)
            hot_hi = sb("hot_hi", [128, 2, GT, QUARTER], F16, ctx=ctx)
            hot_lo = sb("hot_lo", [128, 2, GT, QUARTER], F16, ctx=ctx)
            u_sem, v_sem = (s.u0, s.u1), (s.v0, s.v1)
            H_BANK, G_BANK = 5, 7

            def number(q, c):
                return c + QUARTER * q

            def later(q, c):
                return not (q == 0 and isinstance(c, int) and c < 2)

            def loads(q, c, p):
                return (number(q, c) - p) * 8 + 16

            def spread(x, width, t):
                return x[:, t].rearrange("p (t o) -> p t o", o=1).to_broadcast([128, GT, width])

            def scatter_vector(dve, q, c, p):
                n = number(q, c)
                t = bass.ds(c * GT, GT)
                if later(q, c):
                    dve.wait_ge(s.g, n - 1)
                wide = [128, GT, QUARTER]
                nc.vector.tensor_tensor(hot[:, p], iota[:, QUARTER * q:QUARTER * q + QUARTER]
                                        .rearrange("p (o a) -> p o a", o=1).to_broadcast(wide),
                                        spread(ea_T, QUARTER, t), ALU.is_equal).then_inc(s.eq, 1)
                nc.vector.tensor_tensor(hot_b[:, p], iota[:].rearrange("p (o b) -> p o b", o=1)
                                        .to_broadcast([128, GT, NK]), spread(eb_T, NK, t), ALU.is_equal
                                        ).then_inc(s.rows, 1)

            def scatter_pool(pool, q, c, p):
                n = number(q, c)
                t = bass.ds(c * GT, GT)
                pool.wait_ge(s.eq, n + 1)
                nc.gpsimd.tensor_tensor(hot_hi[:, p], hot[:, p], spread(gh_T, QUARTER, t), ALU.mult)
                nc.gpsimd.tensor_tensor(hot_lo[:, p], hot[:, p], spread(gl_T, QUARTER, t), ALU.mult
                                        ).then_inc(s.cols, 1)

            def scatter_tensor(pe, q, c, p):
                n = number(q, c)
                pe.wait_ge(s.rows, n + 1)
                pe.wait_ge(s.cols, n + 1)
                if not (q == 0 and isinstance(c, int) and c < 1):
                    pe.wait_ge(s.g_used, n)
                for e in range(GT):
                    dst = ps[:, G_BANK, QUARTER * e:QUARTER * e + QUARTER]
                    nc.tensor.matmul(dst, hot_b[:, p, e, :], hot_hi[:, p, e, :], start=True, stop=False)
                    last = nc.tensor.matmul(dst, hot_b[:, p, e, :], hot_lo[:, p, e, :], start=False, stop=True)
                last.then_inc(s.g, 1)

            def scatter_scalar(act, q, c, p):
                n = number(q, c)
                act.wait_ge(s.g, n + 1)
                if q >= 2:
                    act.wait_ge(s.w, QUARTER * (q - 1))
                nc.scalar.copy(gates[:, q % 2, :, bass.ds(c * GT, GT)],
                               ps[:, G_BANK, 0:GT * QUARTER].rearrange("p (t a) -> p a t", a=QUARTER)
                               ).then_inc(s.g_used, 1)

            def load_u(sp, q, c, p):
                if later(q, c):
                    sp.wait_ge(s.ul, number(q, c) - 1)
                sp.dma_start(u_in[:, p], u_tab[bass.ds(c + (layer * NK + QUARTER * q), 1)]
                             .rearrange("o p k e -> p (o k) e")).then_inc(u_sem[p], 16)

            def load_v(sp, q, c, p):
                if later(q, c):
                    sp.wait_ge(s.vl, number(q, c) - 1)
                sp.dma_start(v_in[:, p], v_tab[bass.ds(c + (layer * NK + QUARTER * q), 1)]
                             .rearrange("o e d -> e (o d)")).then_inc(v_sem[p], 16)

            def u_high(act, q, c, p):
                act.wait_ge(u_sem[p], loads(q, c, p))
                if later(q, c):
                    act.wait_ge(s.h, number(q, c) - 1)
                nc.scalar.activation(u_hi[:, p], u_in[:, p], ACT.Copy, scale=U_SCALE).then_inc(s.uh, 1)

            def v_high(act, q, c, p):
                act.wait_ge(v_sem[p], loads(q, c, p))
                if later(q, c):
                    act.wait_ge(s.y, number(q, c) - 1)
                nc.scalar.activation(v_hi[:, p], v_in[:, p], ACT.Copy, scale=V_SCALE).then_inc(s.vh, 1)

            def u_low(dve, q, c, p):
                dve.wait_ge(s.uh, number(q, c) + 1)
                nc.vector.scalar_tensor_tensor(out=u_lo[:, p].rearrange("p k e -> p (k e)"),
                                               in0=u_in[:, p].rearrange("p k e -> p (k e)"), scalar=U_SCALE,
                                               in1=u_hi[:, p].rearrange("p k e -> p (k e)"), op0=ALU.mult,
                                               op1=ALU.subtract).then_inc(s.ul, 1)

            def v_low(dve, q, c, p):
                dve.wait_ge(s.vh, number(q, c) + 1)
                nc.vector.scalar_tensor_tensor(out=v_lo[:, p], in0=v_in[:, p], scalar=V_SCALE, in1=v_hi[:, p],
                                               op0=ALU.mult, op1=ALU.subtract).then_inc(s.vl, 1)

            def gelu(act, q, c, p):
                n = number(q, c)
                act.wait_ge(s.h, n + 1)
                if later(q, c):
                    act.wait_ge(s.w, n - 1)
                nc.scalar.activation(ge[:, p], ps[:, H_BANK + p, 0:T], ACT.Gelu_apprx_tanh, scale=1.0 / U_SCALE
                                     ).then_inc(s.gelu, 1)
                act.wait_ge(s.w, n + 1)
                if later(q, c):
                    act.wait_ge(s.y, n - 1)
                nc.scalar.copy(w_hi[:, p], w[:, p]).then_inc(s.wh, 1)

            def gate(dve, q, c, p):
                n = number(q, c)
                dve.wait_ge(s.gelu, n + 1)
                dve.wait_ge(s.g_used, QUARTER * (q + 1))
                if later(q, c):
                    dve.wait_ge(s.wl, n - 1)
                nc.vector.tensor_tensor(w[:, p], ge[:, p],
                                        gates[:, q % 2, bass.ds(c, 1), :].rearrange("p o t -> p (o t)"), ALU.mult
                                        ).then_inc(s.w, 1)

            def w_low(pool, q, c, p):
                pool.wait_ge(s.wh, number(q, c) + 1)
                nc.gpsimd.tensor_tensor(w_lo[:, p], w[:, p], w_hi[:, p], ALU.subtract).then_inc(s.wl, 1)

            def product_u(pe, q, c, p):
                n = number(q, c)
                pe.wait_ge(s.uh, n + 1)
                pe.wait_ge(s.ul, n + 1)
                if later(q, c):
                    pe.wait_ge(s.gelu, n - 1)
                for k in range(KT):
                    dst = ps[:, H_BANK + p, 0:T]
                    nc.tensor.matmul(dst, u_hi[:, p, k, :], x_hi[:, k, :], start=(k == 0), stop=False)
                    nc.tensor.matmul(dst, u_hi[:, p, k, :], x_lo[:, k, :], start=False, stop=False)
                    last = nc.tensor.matmul(dst, u_lo[:, p, k, :], x_hi[:, k, :], start=False, stop=(k == KT - 1))
                last.then_inc(s.h, 1)

            def product_v(pe, q, c, p):
                n = number(q, c)
                begin = isinstance(n, int) and n == 0
                end = isinstance(n, int) and n == NK - 1
                pe.wait_ge(s.vl, n + 1)
                pe.wait_ge(s.wl, n + 1)
                for f in range(KT):
                    for m, (vv, ww) in enumerate(((v_hi, w_hi), (v_hi, w_lo), (v_lo, w_hi))):
                        lhs = vv[:, p, 128 * f:128 * f + 128]
                        nc.tensor.matmul(ps[:, f // 2, 256 * (f % 2):256 * (f % 2) + 256], lhs, ww[:, p, 0:PROMPT],
                                         start=(begin and m == 0 and f % 2 == 0), stop=(end and m == 2),
                                         skip_group_check=True)
                        last = nc.tensor.matmul(ps[:, 4, SAMPLE * f:SAMPLE * f + SAMPLE], lhs, ww[:, p, PROMPT:T],
                                                start=(begin and m == 0 and f == 0), stop=(end and m == 2),
                                                skip_group_check=True)
                last.then_inc(s.y, 1)

            def pairs(eng, q, first, last, pair):
                if first:
                    pair(q, 0)
                with eng.Fori(1 if first else 0, QUARTER // 2 - (1 if last else 0)) as n:
                    pair(q, n * 2)
                if last:
                    pair(q, QUARTER - 2)

            def each_pair(eng, pair):
                for q in range(4):
                    pairs(eng, q, q == 0, q == 3, pair)

            @block.sync
            def _(sp):
                def pair(q, c):
                    for p in range(2):
                        load_u(sp, q, c + p, p)
                        load_v(sp, q, c + p, p)
                each_pair(sp, pair)

            @block.scalar
            def _(act):
                u_high(act, 0, 0, 0)
                u_high(act, 0, 1, 1)
                v_high(act, 0, 0, 0)

                def opening(q, c):
                    scatter_scalar(act, 0, c, 0)
                    scatter_scalar(act, 0, c + 1, 1)
                pairs(act, 0, True, False, opening)

                def pair(q, c):
                    done = q == 3 and isinstance(c, int)
                    for p in range(2):
                        gelu(act, q, c + p, p)
                        if not done:
                            u_high(act, q, c + p + 2, p)
                        if not (done and p):
                            v_high(act, q, c + p + 1, 1 - p)
                        if q < 3:
                            scatter_scalar(act, q + 1, c + p, p)
                each_pair(act, pair)

            @block.vector
            def _(dve):
                u_low(dve, 0, 0, 0)
                u_low(dve, 0, 1, 1)
                v_low(dve, 0, 0, 0)

                def opening(q, c):
                    scatter_vector(dve, 0, c, 0)
                    scatter_vector(dve, 0, c + 1, 1)
                pairs(dve, 0, True, False, opening)

                def pair(q, c):
                    done = q == 3 and isinstance(c, int)
                    for p in range(2):
                        gate(dve, q, c + p, p)
                        if q < 3:
                            scatter_vector(dve, q + 1, c + p, p)
                        if not done:
                            u_low(dve, q, c + p + 2, p)
                        if not (done and p):
                            v_low(dve, q, c + p + 1, 1 - p)
                each_pair(dve, pair)

            @block.gpsimd
            def _(pool):
                def opening(q, c):
                    scatter_pool(pool, 0, c, 0)
                    scatter_pool(pool, 0, c + 1, 1)
                pairs(pool, 0, True, False, opening)

                def pair(q, c):
                    for p in range(2):
                        w_low(pool, q, c + p, p)
                        if q < 3:
                            scatter_pool(pool, q + 1, c + p, p)
                each_pair(pool, pair)

            @block.tensor
            def _(pe):
                product_u(pe, 0, 0, 0)

                def opening(q, c):
                    scatter_tensor(pe, 0, c, 0)
                    scatter_tensor(pe, 0, c + 1, 1)
                pairs(pe, 0, True, False, opening)

                def pair(q, c):
                    done = q == 3 and isinstance(c, int)
                    for p in range(2):
                        if not (done and p):
                            product_u(pe, q, c + p + 1, 1 - p)
                        if q < 3:
                            scatter_tensor(pe, q + 1, c + p, p)
                        product_v(pe, q, c + p, p)
                each_pair(pe, pair)

    with root:
        yield_layers = (sgu, retention, gla)
        for layer in range(DEPTH):
            yield_layers[layer % 3](layer // 3, layer)
            peer(layer)
        with phase("stored") as (block, s):
            @block.sync
            def _(sp):
                sp.dma_start(out[0].rearrange("b (i p) d -> p (b i) d", p=128), x_tok[:, 0:2, :]
                             ).then_inc(s.stored, 16)
                sp.dma_start(out[1].rearrange("b l d -> (b l) d"), x_tok[0:SAMPLE, 2, :]).then_inc(s.stored, 16)
                sp.wait_ge(s.stored, 32)


_PLAIN = ["x_prompt", "x_sample", "state_ret", "state_gla", "sgu_w_in", "sgu_b_in", "sgu_v_g", "sgu_v_b", "sgu_b_s",
          "sgu_w_out", "ret_w_in", "ret_w_out", "gla_w_in", "gla_w_a2", "gla_w_out", "peer_w_q", "ln_g", "ln_b"]
_OUTS = [(1, PROMPT, D), (NB, LS, D), (1, 1, H, 256, 512), (1, NB, H, 256, 512), (1, 1, H, 128, 256),
         (1, NB, H, 128, 256), (2, NB, LS, D)]


def kernel(**inputs):
    import concourse.bacc as bacc
    from concourse.bass_utils import run_bass_kernel_spmd

    a = {k: np.asarray(v) for k, v in inputs.items()}
    arrays = {n: a[n] for n in _PLAIN}
    arrays["sgu_b_col"] = a["sgu_b_in"].reshape(2, 16, 128).transpose(0, 2, 1)
    arrays["ret_gain"] = a["ret_gn_g"].reshape(1, 16, 128).transpose(0, 2, 1)
    arrays["gla_b_col"] = a["gla_b_a"].reshape(1, 4, 128).transpose(0, 2, 1)
    arrays["gla_gain"] = np.tile(a["gla_rms_g"].reshape(1, 2, 128).transpose(0, 2, 1), (1, 1, H))
    arrays["sgu_w_sT"] = a["sgu_w_s"].transpose(0, 1, 3, 2)
    arrays["peer_keys_aT"] = a["peer_keys_a"].transpose(0, 2, 1)
    arrays["peer_keys_bT"] = a["peer_keys_b"].transpose(0, 2, 1)
    arrays["peer_uT"] = a["peer_u"].reshape(DEPTH * NK, 128, KT, 128).transpose(0, 3, 2, 1)
    arrays["peer_v"] = a["peer_v"].reshape(DEPTH * NK, 128, D)
    arrays.update(shape_constants())
    arrays = {f"in_{n}": np.ascontiguousarray(v) for n, v in arrays.items()}
    nc = bacc.Bacc("TRN2", target_bir_lowering=False, num_devices=1)
    io = {n[3:]: nc.dram_tensor(n, v.shape, mybir.dt.from_np(v.dtype), kind="ExternalInput").ap()
          for n, v in arrays.items()}
    out = [nc.dram_tensor(f"out_{i}", shape, F32, kind="ExternalOutput").ap() for i, shape in enumerate(_OUTS)]
    build(nc, io, out)
    r = run_bass_kernel_spmd(nc, [arrays], core_ids=[0])
    return tuple(r.results[0][f"out_{i}"] for i in range(len(_OUTS)))
```

```python
from collections import namedtuple
from contextlib import ExitStack, contextmanager

import numpy as np
import concourse.bass as bass
from concourse import mybir

F32 = mybir.dt.float32
F16 = mybir.dt.float16
U32 = mybir.dt.uint32
ALU = mybir.AluOpType
ACT = mybir.ActivationFunctionType
AX = mybir.AxisListType.X

D = 1024
KT = D // 128
PROMPT, NB, LS = 256, 8, 8
SAMPLE = NB * LS
T = PROMPT + SAMPLE
ROWS = [128, 128, SAMPLE]
TILES = [(0, 128), (128, 128), (256, SAMPLE)]
DEPTH = 4
PAST = 2048
H = 4
EPS = 1e-5
ALPHA = (2.0 * DEPTH) ** 0.25
GROUP = 512
LEVELS = 7
PH, PK, NK = 8, 16, 128
QUARTER = NK // 4
UNDER = QUARTER - 4
SPLIT = UNDER + 2
GT = T // QUARTER
U_SCALE, V_SCALE, G_SCALE = 64.0, 16.0, 16.0
W_SCALE = 64.0
LOWEST = -3.0e38

Job = namedtuple("Job", "col kind dest func bias scale width")


def ret_log_decay():
    return np.log1p(-np.exp2(-5.0 - np.arange(H))).astype(np.float32)


def shape_constants():
    f = np.float32

    def exp(x):
        return np.exp(x.astype(np.float64)).astype(f)
    pos = np.concatenate([np.arange(PROMPT), np.tile(PAST + np.arange(LS), NB)]).astype(f)
    inv = (10000.0 ** (-np.arange(0, 256, 2) / 256)).astype(f)
    ang = (pos[None, :] * inv[:, None]).astype(f)
    lg = ret_log_decay()
    step = np.concatenate([np.arange(128), np.arange(128), np.tile(np.arange(LS), NB)]).astype(f)
    size = np.concatenate([np.full(PROMPT, 128), np.full(SAMPLE, LS)]).astype(f)
    cross = exp((step + 1)[None, :] * lg[:, None])
    keep = exp((size - 1 - step)[None, :] * lg[:, None]) / f(16)
    rel = np.arange(128)[None, :] - np.arange(128)[:, None]
    decay = np.where(rel >= 0, exp(np.maximum(rel, 0).astype(f)[None] * lg[:, None, None]) / f(16), 0).astype(f)
    seq = np.arange(SAMPLE) // LS
    same = seq[None, :] == seq[:, None]
    decay_s = np.where(same, decay[:, :SAMPLE, :SAMPLE], 0).astype(f)
    member = (seq[:, None] == np.arange(NB)[None, :]).astype(f)
    kd = np.zeros((128, 3, H), f)
    for i, (t0, n) in enumerate(TILES):
        kd[:n, i] = keep[:, t0:t0 + n].T
    kdm = np.einsum("sb,sh->sbh", member, kd[:SAMPLE, 2]).astype(f)
    s, t = np.arange(128)[:, None], np.arange(128)[None, :]
    levels = [s == t] + [(s // b == t // b) & (s % b < b // 2) & (t % b >= b // 2) for b in (2, 4, 8, 16, 32, 64)]
    start = np.ones(T, f)
    start[0:PROMPT:64] = 0
    start[PROMPT::LS] = 0
    dec = np.concatenate([np.repeat(exp(128 * lg)[:, None], 2, 1), np.repeat(exp(LS * lg)[:, None], NB, 1)], 1)
    rows = np.ones((128, 1), f)
    return {
        "c_cos": np.cos(ang.astype(np.float64)).astype(f),
        "c_sin": np.sin(ang.astype(np.float64)).astype(f),
        "c_cross": (rows[:, None] * cross[None]).astype(f),
        "c_decay": np.ascontiguousarray(decay.transpose(1, 0, 2)),
        "c_decay_s": np.ascontiguousarray(decay_s.transpose(1, 0, 2)),
        "c_kd": kd,
        "c_kdm": kdm,
        "c_member": member,
        "c_memcol": (rows[:, None] * member.T[None]).astype(f),
        "c_levels": np.ascontiguousarray(np.stack(levels).astype(f).transpose(1, 0, 2)),
        "c_start": (rows * start[None]).astype(f),
        "c_dec": (rows[:, None] * dec[None]).astype(f),
        "c_ident": np.eye(128, dtype=f),
        "c_iota": (rows * np.arange(NK)[None]).astype(f),
        "c_ones": np.ones((1, 128), f),
    }


def build(nc, io, out):

    @contextmanager
    def phase(*names):
        handles = [nc.alloc_semaphore(f"{n}_{nc.next_id()}") for n in names]
        with nc.Block() as block:
            yield block, namedtuple("Signals", names)(*handles)
        nc.clear_and_free_semaphores(handles)
        nc.all_engine_barrier()

    def linker(eng, sem):
        n = [0]

        def link(ins):
            n[0] += 1
            ins.then_inc(sem, 1)
            eng.wait_ge(sem, n[0])
        return link

    root = ExitStack()

    def sb(name, shape, dt=F32, ctx=root):
        return ctx.enter_context(nc.sbuf_tensor(f"{name}_{nc.next_id()}", shape, dt))

    ps = root.enter_context(nc.psum_tensor("ps", [128, 8, 512], F32))
    x_tok = sb("x_tok", [128, 3, D])
    x_T = sb("x_T", [128, KT, T])
    x_hi = sb("x_hi", [128, KT, T], F16)
    x_lo = sb("x_lo", [128, KT, T], F16)
    ident = sb("ident", [128, 128])
    ones = sb("ones", [1, 128])
    w_ones = sb("w_ones", [1, 128])
    eps = sb("eps", [128, 1])
    w_eps = sb("w_eps", [128, 1])

    def emit_transposes(pe, s, banks, wait_first):
        n = 0
        for i, (t0, r) in enumerate(TILES):
            wait_first(i)
            for q in range(KT // 4):
                if n >= 2:
                    pe.wait_ge(s.tp_used, n - 1)
                for j in range(4):
                    last = nc.tensor.transpose(ps[:, banks[n % 2], j * 128:j * 128 + r],
                                               x_tok[0:r, i, (4 * q + j) * 128:(4 * q + j + 1) * 128],
                                               ident[0:r, 0:r])
                last.then_inc(s.tp, 1)
                n += 1

    def emit_transpose_copies(act, s, banks):
        n = 0
        for i, (t0, r) in enumerate(TILES):
            for q in range(KT // 4):
                act.wait_ge(s.tp, n + 1)
                nc.scalar.copy(x_T[:, 4 * q:4 * q + 4, t0:t0 + r],
                               ps[:, banks[n % 2], :].rearrange("p (j t) -> p j t", j=4)[:, :, 0:r]
                               ).then_inc(s.tp_used, 1)
                n += 1

    def emit_high_parts(act, s):
        act.wait_ge(s.tp_used, 3 * KT // 4)
        for q in range(KT // 4):
            nc.scalar.copy(x_hi[:, 4 * q:4 * q + 4, :], x_T[:, 4 * q:4 * q + 4, :]).then_inc(s.hi, 1)

    def emit_low_parts(dve, s):
        for q in range(KT // 4):
            dve.wait_ge(s.hi, q + 1)
            nc.vector.tensor_tensor(x_lo[:, 4 * q:4 * q + 4, :], x_T[:, 4 * q:4 * q + 4, :],
                                    x_hi[:, 4 * q:4 * q + 4, :], ALU.subtract)

    with phase("loaded", "tp", "tp_used", "hi") as (block, s):
        @block.sync
        def _(sp):
            sp.dma_start(x_tok[:, 0:2, :], io["x_prompt"].rearrange("b (i p) d -> p (b i) d", p=128)
                         ).then_inc(s.loaded, 16)
            sp.dma_start(x_tok[0:SAMPLE, 2, :], io["x_sample"].rearrange("b l d -> (b l) d")
                         ).then_inc(s.loaded, 16)
            sp.dma_start(ident[:], io["c_ident"]).then_inc(s.loaded, 16)
            sp.dma_start(ones[:], io["c_ones"]).then_inc(s.loaded, 16)

        @block.vector
        def _(dve):
            nc.vector.memset(eps[:], EPS)
            nc.vector.memset(w_eps[:], EPS * W_SCALE ** 2)
            nc.vector.memset(w_ones[:], W_SCALE)
            emit_low_parts(dve, s)

        @block.tensor
        def _(pe):
            emit_transposes(pe, s, (0, 1), lambda i: pe.wait_ge(s.loaded, 64) if i == 0 else None)

        @block.scalar
        def _(act):
            emit_transpose_copies(act, s, (0, 1))
            emit_high_parts(act, s)

    def project_in(w, jobs):
        units = []
        for g, j in enumerate(jobs):
            for f in range(-(-j.width // 128) if j.kind == "feature" else 3):
                units.append((g, j, f))

        def units_through(g):
            return sum(u[0] <= g for u in units)

        with ExitStack() as ctx, phase("w0", "w1", "w_hi", "w_lo", "out", "out_used") as (block, s):
            w_in = sb("w_in", [128, 2, KT, GROUP], ctx=ctx)
            w_hi = sb("w_hi", [128, 2, KT, GROUP], F16, ctx=ctx)
            w_lo = sb("w_lo", [128, 2, KT, GROUP], F16, ctx=ctx)
            w_sem = (s.w0, s.w1)

            @block.sync
            def _(sp):
                for g, j in enumerate(jobs):
                    if g >= 2:
                        sp.wait_ge(s.w_lo, 2 * (g - 1))
                    for k in range(0, KT, KT // 2):
                        sp.dma_start(w_in[:, g % 2, k:k + KT // 2, 0:j.width],
                                     w[128 * k:128 * (k + KT // 2), j.col:j.col + j.width]
                                     .rearrange("(k p) n -> p k n", p=128)).then_inc(w_sem[g % 2], 16)

            @block.tensor
            def _(pe):
                for n, (g, j, f) in enumerate(units):
                    if f == 0:
                        pe.wait_ge(s.w_lo, 2 * (g + 1))
                        pe.wait_ge(s.w_hi, 2 * (g + 1))
                    if n >= 6:
                        pe.wait_ge(s.out_used, n - 5)
                    bank, p = n % 6, g % 2
                    parts = ((w_hi, x_hi), (w_hi, x_lo), (w_lo, x_hi))
                    if j.kind == "feature":
                        m = min(128, j.width - 128 * f)
                        for k in range(KT):
                            for e, (ww, xx) in enumerate(parts):
                                last = nc.tensor.matmul(ps[0:m, bank, 0:T], ww[:, p, k, 128 * f:128 * f + m],
                                                        xx[:, k, :], start=(k == 0 and e == 0),
                                                        stop=(k == KT - 1 and e == 2))
                    else:
                        t0, r = TILES[f]
                        for k in range(KT):
                            for e, (ww, xx) in enumerate(parts):
                                last = nc.tensor.matmul(ps[0:r, bank, 0:j.width], xx[:, k, t0:t0 + r],
                                                        ww[:, p, k, 0:j.width], start=(k == 0 and e == 0),
                                                        stop=(k == KT - 1 and e == 2 and j.bias is None))
                        if j.bias is not None:
                            last = nc.tensor.matmul(ps[0:r, bank, 0:j.width], w_ones[:, 0:r], j.bias,
                                                    start=False, stop=True)
                    last.then_inc(s.out, 1)

            @block.scalar
            def _(act):
                def split(g):
                    j = jobs[g]
                    act.wait_ge(w_sem[g % 2], 32 * (g // 2 + 1))
                    if g >= 2:
                        act.wait_ge(s.out, units_through(g - 2))
                    for k in range(0, KT, KT // 2):
                        nc.scalar.activation(w_hi[:, g % 2, k:k + KT // 2, 0:j.width],
                                             w_in[:, g % 2, k:k + KT // 2, 0:j.width], ACT.Copy, scale=W_SCALE
                                             ).then_inc(s.w_hi, 1)

                split(0)
                for n, (g, j, f) in enumerate(units):
                    if f == 0 and g + 1 < len(jobs):
                        split(g + 1)
                    act.wait_ge(s.out, n + 1)
                    dst = j.dest(f)
                    bias = j.bias[:, f:f + 1] if j.kind == "feature" and j.bias is not None else 0.0
                    width = T if j.kind == "feature" else j.width
                    nc.scalar.activation(dst, ps[0:dst.shape[0], n % 6, 0:width], j.func, bias=bias,
                                         scale=j.scale / W_SCALE).then_inc(s.out_used, 1)

            @block.vector
            def _(dve):
                for g, j in enumerate(jobs):
                    for k in range(0, KT, KT // 2):
                        dve.wait_ge(s.w_hi, 2 * g + k // (KT // 2) + 1)
                        at = (slice(None), g % 2, slice(k, k + KT // 2), slice(0, j.width))
                        nc.vector.scalar_tensor_tensor(out=w_lo[at], in0=w_in[at], scalar=W_SCALE, in1=w_hi[at],
                                                       op0=ALU.mult, op1=ALU.subtract).then_inc(s.w_lo, 1)

    def job(col, kind, dest, func=None, bias=None, scale=1.0, width=GROUP):
        return Job(col, kind, dest, func or ACT.Copy, bias, scale, width)

    def project_out(w, src, kt):
        with ExitStack() as ctx, phase("w0", "w1", "w2", "w3", "hi", "lo", "src_hi", "out") as (block, s):
            w_in = sb("w_in", [128, 4, D], ctx=ctx)
            w_hi = sb("w_hi", [128, 4, D], F16, ctx=ctx)
            w_lo = sb("w_lo", [128, 4, D], F16, ctx=ctx)
            s_hi = sb("s_hi", [128, kt, T], F16, ctx=ctx)
            s_lo = sb("s_lo", [128, kt, T], F16, ctx=ctx)
            w_sem = (s.w0, s.w1, s.w2, s.w3)

            @block.sync
            def _(sp):
                for k in range(kt):
                    if k >= 4:
                        sp.wait_ge(s.lo, k - 3)
                    sp.dma_start(w_in[:, k % 4, :], w[128 * k:128 * k + 128, :]).then_inc(w_sem[k % 4], 16)

            @block.scalar
            def _(act):
                for k in range(kt):
                    nc.scalar.copy(s_hi[:, k, :], src[:, k, :]).then_inc(s.src_hi, 1)
                    act.wait_ge(w_sem[k % 4], 16 * (k // 4 + 1))
                    if k >= 4:
                        act.wait_ge(s.out, k - 3)
                    nc.scalar.activation(w_hi[:, k % 4, :], w_in[:, k % 4, :], ACT.Copy, scale=W_SCALE
                                         ).then_inc(s.hi, 1)

            @block.vector
            def _(dve):
                for k in range(kt):
                    dve.wait_ge(s.src_hi, k + 1)
                    nc.vector.tensor_tensor(s_lo[:, k, :], src[:, k, :], s_hi[:, k, :], ALU.subtract)
                    dve.wait_ge(s.hi, k + 1)
                    nc.vector.scalar_tensor_tensor(out=w_lo[:, k % 4, :], in0=w_in[:, k % 4, :], scalar=W_SCALE,
                                                   in1=w_hi[:, k % 4, :], op0=ALU.mult, op1=ALU.subtract
                                                   ).then_inc(s.lo, 1)

            @block.tensor
            def _(pe):
                for k in range(kt):
                    pe.wait_ge(s.lo, k + 1)
                    pe.wait_ge(s.hi, k + 1)
                    for i, (t0, r) in enumerate(TILES):
                        for e, (ss, ww) in enumerate(((s_hi, w_hi), (s_hi, w_lo), (s_lo, w_hi))):
                            for n in range(2):
                                last = nc.tensor.matmul(ps[0:r, 2 * i + n, :], ss[:, k, t0:t0 + r],
                                                        ww[:, k % 4, 512 * n:512 * n + 512],
                                                        start=(k == 0 and e == 0), stop=(k == kt - 1 and e == 2))
                    last.then_inc(s.out, 1)

    def residual_norm(layer, which):
        with ExitStack() as ctx, phase("loaded", "step", "var", "std", "affine", "gain", "ready",
                                       "tp", "tp_used", "hi") as (block, s):
            g_row = sb("g_row", [128, D], ctx=ctx)
            b_row = sb("b_row", [128, D], ctx=ctx)
            st = sb("st", [128, 3, 2, 6], ctx=ctx)
            mv = sb("mv", [128, 3, 2], ctx=ctx)
            sd = sb("sd", [128, 3], ctx=ctx)
            rs = sb("rs", [128, 3], ctx=ctx)

            @block.sync
            def _(sp):
                sp.dma_start(g_row[:], io["ln_g"][layer, which:which + 1, :].partition_broadcast(128)
                             ).then_inc(s.loaded, 16)
                sp.dma_start(b_row[:], io["ln_b"][layer, which:which + 1, :].partition_broadcast(128)
                             ).then_inc(s.loaded, 16)

            @block.vector
            def _(dve):
                link = linker(dve, s.step)
                for i, (t0, r) in enumerate(TILES):
                    x = x_tok[0:r, i, :]
                    link(nc.vector.scalar_tensor_tensor(out=x, in0=x, scalar=ALPHA * W_SCALE,
                                                        in1=ps[0:r, 2 * i:2 * i + 2, :].rearrange("p a b -> p (a b)"),
                                                        op0=ALU.mult, op1=ALU.add))
                    nc.vector.bn_stats(out=st[0:r, i, 0, :], in_=x[:, 0:512])
                    link(nc.vector.bn_stats(out=st[0:r, i, 1, :], in_=x[:, 512:1024]))
                    nc.vector.bn_aggr(out=mv[0:r, i, :], in_=st[0:r, i, :, :].rearrange("p a b -> p (a b)")
                                      ).then_inc(s.var, 1)
                for i, (t0, r) in enumerate(TILES):
                    x = x_tok[0:r, i, :]
                    dve.wait_ge(s.var, 3)
                    dve.wait_ge(s.std, i + 1)
                    link(nc.vector.reciprocal(rs[0:r, i:i + 1], sd[0:r, i:i + 1]))
                    link(nc.vector.tensor_scalar(x, x, mv[0:r, i, 0:1], rs[0:r, i:i + 1], ALU.subtract, ALU.mult))
                    if i == 0:
                        dve.wait_ge(s.loaded, 32)
                    nc.vector.tensor_tensor(x, x, g_row[0:r, :], ALU.mult).then_inc(s.gain, 1)
                emit_low_parts(dve, s)

            @block.gpsimd
            def _(pool):
                for i, (t0, r) in enumerate(TILES):
                    pool.wait_ge(s.gain, i + 1)
                    nc.gpsimd.tensor_tensor(x_tok[0:r, i, :], x_tok[0:r, i, :], b_row[0:r, :], ALU.add
                                            ).then_inc(s.ready, 1)

            @block.tensor
            def _(pe):
                emit_transposes(pe, s, (6, 7), lambda i: pe.wait_ge(s.ready, i + 1))

            @block.scalar
            def _(act):
                for i, (t0, r) in enumerate(TILES):
                    act.wait_ge(s.var, i + 1)
                    nc.scalar.activation(sd[0:r, i:i + 1], mv[0:r, i, 1:2], ACT.Sqrt, bias=w_eps[0:r, :]
                                         ).then_inc(s.std, 1)
                emit_transpose_copies(act, s, (6, 7))
                emit_high_parts(act, s)

    def sgu(j, layer):
        w_in, w_out = io["sgu_w_in"][j], io["sgu_w_out"][j]
        with ExitStack() as ctx:
            u_T = sb("u_T", [128, KT, T], ctx=ctx)
            v = sb("v", [128, 3, D], ctx=ctx)
            b_col = sb("b_col", [128, 16], ctx=ctx)
            b_row = sb("b_row", [1, 2 * D], ctx=ctx)
            w_m = sb("w_m", [128, 4, 128], ctx=ctx)
            w_ms = sb("w_ms", [SAMPLE, 4, SAMPLE], ctx=ctx)
            b_s = sb("b_s", [1, 4, T], ctx=ctx)
            vg = sb("vg", [128, D], ctx=ctx)
            vb = sb("vb", [128, D], ctx=ctx)
            with phase("loaded", "zero", "spread") as (block, s):
                @block.sync
                def _(sp):
                    for dst, src in ((b_col[:], io["sgu_b_col"][j]), (b_row[:], io["sgu_b_in"][j:j + 1, :]),
                                     (w_m[:], io["sgu_w_sT"][j].rearrange("g s t -> s g t")),
                                     (vg[:], io["sgu_v_g"][j:j + 1, :].partition_broadcast(128)),
                                     (vb[:], io["sgu_v_b"][j:j + 1, :].partition_broadcast(128))):
                        sp.dma_start(dst, src).then_inc(s.loaded, 16)
                    for q in range(2):
                        sp.dma_start(b_s[:, :, 128 * q:128 * q + 128], io["sgu_b_s"][j:j + 1, :, :]
                                     ).then_inc(s.loaded, 16)
                    for b in range(NB):
                        sp.dma_start(b_s[:, :, PROMPT + LS * b:PROMPT + LS * b + LS],
                                     io["sgu_b_s"][j:j + 1, :, 0:LS]).then_inc(s.loaded, 16)
                    sp.wait_ge(s.zero, 1)
                    for b in range(NB):
                        c = slice(LS * b, LS * b + LS)
                        sp.dma_start(w_ms[c, :, c], io["sgu_w_sT"][j].rearrange("g s t -> s g t")[0:LS, :, 0:LS]
                                     ).then_inc(s.spread, 16)
                    sp.wait_ge(s.loaded, 16 * 15)

                @block.gpsimd
                def _(pool):
                    nc.gpsimd.memset(w_ms[:], 0.0).then_inc(s.zero, 1)
                    pool.wait_ge(s.loaded, 16 * 15)
                    nc.gpsimd.affine_select(out=w_m[:], in_=w_m[:], compare_op=ALU.is_ge, fill=0.0, base=0,
                                            pattern=[[0, 4], [1, 128]], channel_multiplier=-1)
                    pool.wait_ge(s.spread, 16 * NB)
                    nc.gpsimd.affine_select(out=w_ms[:], in_=w_ms[:], compare_op=ALU.is_ge, fill=0.0, base=0,
                                            pattern=[[0, 4], [1, SAMPLE]], channel_multiplier=-1)

            jobs = [job(GROUP * g, "feature", lambda f, g=g: u_T[:, 4 * g + f, :], ACT.Gelu_apprx_tanh,
                        b_col[:, 4 * g:4 * g + 4]) for g in range(2)]
            jobs += [job(D + GROUP * g, "token", lambda i, g=g: v[0:ROWS[i], i, GROUP * g:GROUP * g + GROUP],
                         ACT.Gelu_apprx_tanh, b_row[:, D + GROUP * g:D + GROUP * g + GROUP]) for g in range(2)]
            project_in(w_in, jobs)

            with phase("step", "var", "std", "gain", "ready", "mix", "mix_used", "stored") as (block, s):
                st = sb("st", [128, 3, 2, 6], ctx=ctx)
                mv = sb("mv", [128, 3, 2], ctx=ctx)
                sd = sb("sd", [128, 3], ctx=ctx)
                rs = sb("rs", [128, 3], ctx=ctx)

                @block.vector
                def _(dve):
                    link = linker(dve, s.step)
                    for i, (t0, r) in enumerate(TILES):
                        nc.vector.bn_stats(out=st[0:r, i, 0, :], in_=v[0:r, i, 0:512])
                        link(nc.vector.bn_stats(out=st[0:r, i, 1, :], in_=v[0:r, i, 512:1024]))
                        nc.vector.bn_aggr(out=mv[0:r, i, :], in_=st[0:r, i, :, :].rearrange("p a b -> p (a b)")
                                          ).then_inc(s.var, 1)
                    for i, (t0, r) in enumerate(TILES):
                        row = v[0:r, i, :]
                        dve.wait_ge(s.var, 3)
                        dve.wait_ge(s.std, i + 1)
                        link(nc.vector.reciprocal(rs[0:r, i:i + 1], sd[0:r, i:i + 1]))
                        link(nc.vector.tensor_scalar(row, row, mv[0:r, i, 0:1], rs[0:r, i:i + 1],
                                                     ALU.subtract, ALU.mult))
                        nc.vector.tensor_tensor(row, row, vg[0:r, :], ALU.mult).then_inc(s.gain, 1)
                    for f in range(KT):
                        dve.wait_ge(s.mix, f + 1)
                        nc.vector.tensor_tensor(u_T[:, f, :], u_T[:, f, :], ps[:, f % 6, 0:T], ALU.mult
                                                ).then_inc(s.mix_used, 1)

                @block.gpsimd
                def _(pool):
                    for i, (t0, r) in enumerate(TILES):
                        pool.wait_ge(s.gain, i + 1)
                        nc.gpsimd.tensor_tensor(v[0:r, i, :], v[0:r, i, :], vb[0:r, :], ALU.add
                                                ).then_inc(s.ready, 1)

                @block.scalar
                def _(act):
                    for i, (t0, r) in enumerate(TILES):
                        act.wait_ge(s.var, i + 1)
                        nc.scalar.activation(sd[0:r, i:i + 1], mv[0:r, i, 1:2], ACT.Sqrt, bias=eps[0:r, :]
                                             ).then_inc(s.std, 1)

                @block.tensor
                def _(pe):
                    pe.wait_ge(s.ready, 3)
                    for f in range(KT):
                        if f >= 6:
                            pe.wait_ge(s.mix_used, f - 5)
                        for i, (t0, r) in enumerate(TILES):
                            w = w_m[:, f // 2, :] if i < 2 else w_ms[:, f // 2, :]
                            nc.tensor.matmul(ps[:, f % 6, t0:t0 + r], v[0:r, i, 128 * f:128 * f + 128], w,
                                             start=(i == 0), stop=False, skip_group_check=True)
                        last = nc.tensor.matmul(ps[:, f % 6, 0:T], ones[:], b_s[:, f // 2, :], start=False,
                                                stop=True, skip_group_check=True)
                        last.then_inc(s.mix, 1)

                @block.sync
                def _(sp):
                    sp.wait_ge(s.ready, 3)
                    sp.dma_start(out[6][j].rearrange("b l d -> (b l) d"), v[0:SAMPLE, 2, :]).then_inc(s.stored, 16)
                    sp.wait_ge(s.stored, 16)

            project_out(w_out, u_T, KT)
        residual_norm(layer, 0)

    def recurrent(kd, width, chunks, att, qc, qm, kp, km, dec, v, gate_T, gain, centre, state_in, state_out_p,
                  state_out_s):
        nchunk = len(chunks)
        units = []
        for h in range(H):
            units += [(h, "p", c, k) for c in range(nchunk) for k in range(kd)]
            units += [(h, "s", b, k) for b in range(NB) for k in range(kd)]
        at = {u: n for n, u in enumerate(units)}
        et = width // 128
        S0, S1 = 3, 3
        with ExitStack() as ctx, phase("in0", "in1", "in2", "o0", "o1", "o2", "p_out", "kv", "state",
                                       "heads", "step", "var", "std", "norm", "tp", "tp_used") as (block, s):
            st_p = sb("st_p", [128, 2, kd, width], ctx=ctx)
            s_in = sb("s_in", [128, S0, kd, width], ctx=ctx)
            s_new = sb("s_new", [128, S1, kd, width], ctx=ctx)
            o_n = sb("o_n", [128, 3, width], ctx=ctx)
            bst = sb("bst", [128, 3, 6], ctx=ctx)
            mv = sb("mv", [128, H, 3, 2], ctx=ctx)
            ms = sb("ms", [128, H, 3], ctx=ctx)
            sd = sb("sd", [128, H, 3], ctx=ctx)
            rs = sb("rs", [128, H, 3], ctx=ctx)
            sin = (s.in0, s.in1, s.in2)
            sout = (s.o0, s.o1, s.o2)
            KV, TP = (3, 4), (5, 6)

            @block.sync
            def _(sp):
                def load(n):
                    h, b = divmod(n, NB)
                    sp.dma_start(s_in[:, n % S0], state_in[b, h].rearrange("(k p) e -> p k e", p=128)
                                 ).then_inc(sin[n % S0], 16)
                for n in range(S0):
                    load(n)
                for h in range(H):
                    sp.wait_ge(s.state, at[(h, "p", nchunk - 1, kd - 1)] + 1)
                    sp.dma_start(state_out_p[0, h].rearrange("(k p) e -> p k e", p=128),
                                 st_p[:, (nchunk - 1) % 2]).then_inc(s.p_out, 16)
                    for b in range(NB):
                        n = h * NB + b
                        sp.wait_ge(s.state, at[(h, "s", b, kd - 1)] + 1)
                        sp.dma_start(state_out_s[b, h].rearrange("(k p) e -> p k e", p=128), s_new[:, n % S1]
                                     ).then_inc(sout[n % S1], 16)
                        if n + S0 < H * NB:
                            load(n + S0)
                sp.wait_ge(s.p_out, 16 * H)
                for m, q in enumerate(sout):
                    sp.wait_ge(q, 16 * len(range(m, H * NB, S1)))

            @block.tensor
            def _(pe):
                def update(u, lhs, rhs):
                    n = at[u]
                    if n >= 2:
                        pe.wait_ge(s.state, n - 1)
                    nc.tensor.matmul(ps[:, KV[n % 2], 0:width], lhs, rhs, start=True, stop=True).then_inc(s.kv, 1)

                def turn(h):
                    pe.wait_ge(s.norm, 3 * (h + 1))
                    for f in range(et):
                        n = h * et + f
                        if n >= 2:
                            pe.wait_ge(s.tp_used, n - 1)
                        for i, (t0, r) in enumerate(TILES):
                            last = nc.tensor.transpose(ps[:, TP[n % 2], t0:t0 + r],
                                                       o_n[0:r, i, 128 * f:128 * f + 128], ident[0:r, 0:r])
                        last.then_inc(s.tp, 1)

                for h in range(H):
                    ve = slice(h * width, (h + 1) * width)
                    if h:
                        turn(h - 1)
                    for i in range(2):
                        mine = [c for c in range(nchunk) if chunks[c][0] == i]
                        crossing = [c for c in mine if c > 0]
                        nc.tensor.matmul(ps[:, i, 0:width], att[:, h, i, :], v[:, i, ve], start=True,
                                         stop=not crossing)
                        for c in mine:
                            lo, hi = chunks[c][1:]
                            if c > 0:
                                pe.wait_ge(s.state, at[(h, "p", c - 1, kd - 1)] + 1)
                                for k in range(kd):
                                    nc.tensor.matmul(ps[:, i, 0:width], qc[:, h, k, c - 1, :],
                                                     st_p[:, (c - 1) % 2, k, :], start=False,
                                                     stop=(c == crossing[-1] and k == kd - 1))
                            for k in range(kd):
                                update((h, "p", c, k), kp[lo:hi, i, h, 128 * k:128 * k + 128], v[lo:hi, i, ve])
                    nc.tensor.matmul(ps[0:SAMPLE, 2, 0:width], att[0:SAMPLE, h, 2, 0:SAMPLE], v[0:SAMPLE, 2, ve],
                                     start=True, stop=False)
                    for b in range(NB):
                        n = h * NB + b
                        pe.wait_ge(sin[n % S0], 16 * (n // S0 + 1))
                        for k in range(kd):
                            last = nc.tensor.matmul(ps[0:SAMPLE, 2, 0:width], qm[:, h, k, b, :],
                                                    s_in[:, n % S0, k, :], start=False,
                                                    stop=(b == NB - 1 and k == kd - 1))
                        if b == NB - 1:
                            last.then_inc(s.heads, 1)
                        for k in range(kd):
                            update((h, "s", b, k), km[:, b, h, 128 * k:128 * k + 128], v[0:SAMPLE, 2, ve])
                turn(H - 1)

            @block.vector
            def _(dve):
                link = linker(dve, s.step)
                for h in range(H):
                    for c in range(nchunk):
                        for k in range(kd):
                            n = at[(h, "p", c, k)]
                            dve.wait_ge(s.kv, n + 1)
                            if c == (nchunk - 1) % 2 and h and k == 0:
                                dve.wait_ge(s.p_out, 16 * h)
                            dst = st_p[:, c % 2, k, :]
                            if c == 0:
                                nc.vector.tensor_copy(dst, ps[:, KV[n % 2], 0:width]).then_inc(s.state, 1)
                            else:
                                dve.wait_ge(s.state, at[(h, "p", c - 1, k)] + 1)
                                nc.vector.scalar_tensor_tensor(out=dst, in0=st_p[:, (c - 1) % 2, k, :],
                                                               scalar=dec[:, h, c:c + 1],
                                                               in1=ps[:, KV[n % 2], 0:width], op0=ALU.mult,
                                                               op1=ALU.add).then_inc(s.state, 1)
                    for b in range(NB):
                        m = h * NB + b
                        dve.wait_ge(sin[m % S0], 16 * (m // S0 + 1))
                        if m >= S1:
                            dve.wait_ge(sout[m % S1], 16 * (m // S1))
                        for k in range(kd):
                            n = at[(h, "s", b, k)]
                            dve.wait_ge(s.kv, n + 1)
                            nc.vector.scalar_tensor_tensor(out=s_new[:, m % S1, k, :], in0=s_in[:, m % S0, k, :],
                                                           scalar=dec[:, h, nchunk + b:nchunk + b + 1],
                                                           in1=ps[:, KV[n % 2], 0:width], op0=ALU.mult,
                                                           op1=ALU.add).then_inc(s.state, 1)
                    dve.wait_ge(s.heads, h + 1)
                    for i, (t0, r) in enumerate(TILES):
                        link(nc.vector.bn_stats(out=bst[0:r, i, :], in_=ps[0:r, i, 0:width]))
                        link(nc.vector.bn_aggr(out=mv[0:r, h, i, :], in_=bst[0:r, i, :]))
                        if centre:
                            ins = nc.vector.tensor_copy(ms[0:r, h, i:i + 1], mv[0:r, h, i, 1:2])
                        else:
                            ins = nc.vector.scalar_tensor_tensor(out=ms[0:r, h, i:i + 1], in0=mv[0:r, h, i, 0:1],
                                                                 scalar=mv[0:r, h, i, 0:1], in1=mv[0:r, h, i, 1:2],
                                                                 op0=ALU.mult, op1=ALU.add)
                        ins.then_inc(s.var, 1)
                    if h:
                        dve.wait_ge(s.tp, h * et)
                    for i, (t0, r) in enumerate(TILES):
                        dve.wait_ge(s.std, 3 * h + i + 1)
                        link(nc.vector.reciprocal(rs[0:r, h, i:i + 1], sd[0:r, h, i:i + 1]))
                        if centre:
                            ins = nc.vector.tensor_scalar(o_n[0:r, i, :], ps[0:r, i, 0:width], mv[0:r, h, i, 0:1],
                                                          rs[0:r, h, i:i + 1], ALU.subtract, ALU.mult)
                        else:
                            ins = nc.vector.tensor_scalar(o_n[0:r, i, :], ps[0:r, i, 0:width],
                                                          rs[0:r, h, i:i + 1], None, ALU.mult)
                        ins.then_inc(s.norm, 1)
                    for f in range(et):
                        n = h * et + f
                        dve.wait_ge(s.tp, n + 1)
                        nc.vector.scalar_tensor_tensor(out=gate_T[:, n, :], in0=ps[:, TP[n % 2], 0:T],
                                                       scalar=gain[:, n:n + 1], in1=gate_T[:, n, :], op0=ALU.mult,
                                                       op1=ALU.mult).then_inc(s.tp_used, 1)

            @block.scalar
            def _(act):
                for h in range(H):
                    for i, (t0, r) in enumerate(TILES):
                        act.wait_ge(s.var, 3 * h + i + 1)
                        nc.scalar.activation(sd[0:r, h, i:i + 1], ms[0:r, h, i:i + 1], ACT.Sqrt, bias=eps[0:r, :]
                                             ).then_inc(s.std, 1)

    def retention(j, layer):
        with ExitStack() as cg:
            g_T = sb("g_T", [128, 16, T], ctx=cg)
            with ExitStack() as ctx:
                v = sb("v", [128, 3, 2048], ctx=ctx)
                q_T = sb("q_T", [128, H, 2, T], ctx=ctx)
                k_T = sb("k_T", [128, H, 2, T], ctx=ctx)
                jobs = [job(GROUP * g, "feature",
                            lambda f, g=g: (q_T if g < 2 else k_T)[:, (4 * g + f) % 8 // 2, f % 2, :])
                        for g in range(4)]
                jobs += [job(2048 + GROUP * g, "token", lambda i, g=g: v[0:ROWS[i], i, GROUP * g:GROUP * g + GROUP])
                         for g in range(4)]
                jobs += [job(4096 + GROUP * g, "feature", lambda f, g=g: g_T[:, 4 * g + f, :], ACT.Silu)
                         for g in range(4)]
                project_in(io["ret_w_in"][j], jobs)

                att = sb("att", [128, H, 3, 128], ctx=ctx)
                qc = sb("qc", [128, H, 2, 1, 128], ctx=ctx)
                qm = sb("qm", [128, H, 2, NB, SAMPLE], ctx=ctx)
                kp = sb("kp", [128, 2, H, 256], ctx=ctx)
                dec = sb("dec", [128, H, 2 + NB], ctx=ctx)
                gain = sb("gain", [128, 16], ctx=ctx)
                km = sb("km", [SAMPLE, NB, H, 256], ctx=ctx)
                with ExitStack() as cq:
                    with phase("loaded", "step", "pstep", "q_rot", "k_rot", "sc", "sc_used", "kt", "kt_used", "qs"
                               ) as (block, s):
                        cos = sb("cos", [128, T], ctx=cq)
                        sin = sb("sin", [128, T], ctx=cq)
                        cross = sb("cross", [128, H, T], ctx=cq)
                        decay = sb("decay", [128, H, 128], ctx=cq)
                        decay_s = sb("decay_s", [SAMPLE, H, SAMPLE], ctx=cq)
                        keep = sb("keep", [128, 3, H], ctx=cq)
                        keep_s = sb("keep_s", [SAMPLE, NB, H], ctx=cq)
                        memcol = sb("memcol", [128, NB, SAMPLE], ctx=cq)
                        tmp_q = sb("tmp_q", [128, 2, H, T], ctx=cq)
                        tmp_k = sb("tmp_k", [128, 2, H, T], ctx=cq)
                        n_load = 10

                        @block.sync
                        def _(sp):
                            for dst, src in ((cos, "c_cos"), (sin, "c_sin"), (cross, "c_cross"), (decay, "c_decay"),
                                             (decay_s, "c_decay_s"), (keep, "c_kd"), (keep_s, "c_kdm"),
                                             (memcol, "c_memcol"), (dec, "c_dec")):
                                sp.dma_start(dst[:], io[src]).then_inc(s.loaded, 16)
                            sp.dma_start(gain[:], io["ret_gain"][j]).then_inc(s.loaded, 16)

                        def rotate(tt, link, a, tmp):
                            a0, a1 = a[:, :, 0, :], a[:, :, 1, :]
                            c = cos[:].rearrange("p (o t) -> p o t", o=1).to_broadcast([128, H, T])
                            n = sin[:].rearrange("p (o t) -> p o t", o=1).to_broadcast([128, H, T])
                            tt(tmp[:, 0], a1, n, ALU.mult)
                            link(tt(tmp[:, 1], a0, n, ALU.mult))
                            tt(a0, a0, c, ALU.mult)
                            link(tt(a1, a1, c, ALU.mult))
                            tt(a0, a0, tmp[:, 0], ALU.subtract)
                            return tt(a1, a1, tmp[:, 1], ALU.add)

                        @block.vector
                        def _(dve):
                            link = linker(dve, s.step)
                            dve.wait_ge(s.loaded, 16 * n_load)
                            rotate(nc.vector.tensor_tensor, link, q_T, tmp_q).then_inc(s.q_rot, 1)
                            dve.wait_ge(s.q_rot, 1)
                            for k in range(2):
                                nc.vector.tensor_tensor(qc[:, :, k, 0, :], q_T[:, :, k, 128:256], cross[:, :, 128:256],
                                                        ALU.mult)
                                nc.vector.tensor_tensor(tmp_q[:, k, :, 0:SAMPLE], q_T[:, :, k, PROMPT:T],
                                                        cross[:, :, PROMPT:T], ALU.mult).then_inc(s.qs, 1)
                            dve.wait_ge(s.qs, 2)
                            for h in range(H):
                                for k in range(2):
                                    nc.vector.tensor_tensor(
                                        qm[:, h, k, :, :],
                                        tmp_q[:, k, h, 0:SAMPLE].rearrange("p (o t) -> p o t", o=1)
                                        .to_broadcast([128, NB, SAMPLE]), memcol[:], ALU.mult)
                            for h in range(H):
                                for i in range(3):
                                    r = ROWS[i]
                                    n = 3 * h + i
                                    dve.wait_ge(s.sc, n + 1)
                                    nc.vector.tensor_tensor(att[0:r, h, i, 0:r], ps[0:r, n % 2, 0:r],
                                                            (decay if i < 2 else decay_s)[:, h, :], ALU.mult
                                                            ).then_inc(s.sc_used, 1)
                            for i in range(3):
                                r = ROWS[i]
                                for q in range(2):
                                    n = 2 * i + q
                                    dve.wait_ge(s.kt, n + 1)
                                    for e in range(2):
                                        h = 2 * q + e
                                        src = ps[0:r, 2 + n % 2, 256 * e:256 * e + 256]
                                        if i < 2:
                                            last = nc.vector.tensor_scalar(kp[:, i, h, :], src, keep[:, i, h:h + 1],
                                                                           None, ALU.mult)
                                        else:
                                            for b in range(NB):
                                                last = nc.vector.tensor_scalar(km[:, b, h, :], src,
                                                                               keep_s[:, b, h:h + 1], None, ALU.mult)
                                    last.then_inc(s.kt_used, 1)

                        @block.gpsimd
                        def _(pool):
                            link = linker(pool, s.pstep)
                            pool.wait_ge(s.loaded, 16 * n_load)
                            rotate(nc.gpsimd.tensor_tensor, link, k_T, tmp_k).then_inc(s.k_rot, 1)

                        @block.tensor
                        def _(pe):
                            pe.wait_ge(s.q_rot, 1)
                            pe.wait_ge(s.k_rot, 1)
                            for h in range(H):
                                for i, (t0, r) in enumerate(TILES):
                                    n = 3 * h + i
                                    if n >= 2:
                                        pe.wait_ge(s.sc_used, n - 1)
                                    for k in range(2):
                                        last = nc.tensor.matmul(ps[0:r, n % 2, 0:r], k_T[:, h, k, t0:t0 + r],
                                                                q_T[:, h, k, t0:t0 + r], start=(k == 0), stop=(k == 1))
                                    last.then_inc(s.sc, 1)
                            for i, (t0, r) in enumerate(TILES):
                                for q in range(2):
                                    n = 2 * i + q
                                    if n >= 2:
                                        pe.wait_ge(s.kt_used, n - 1)
                                    for e in range(4):
                                        last = nc.tensor.transpose(ps[0:r, 2 + n % 2, 128 * e:128 * e + 128],
                                                                   k_T[:, 2 * q + e // 2, e % 2, t0:t0 + r], ident[:])
                                    last.then_inc(s.kt, 1)
                recurrent(2, 512, [(0, 0, 128), (1, 0, 128)], att, qc, qm, kp, km, dec, v, g_T, gain, True,
                          io["state_ret"][j], out[2][j], out[3][j])
            project_out(io["ret_w_out"][j], g_T, 16)
        residual_norm(layer, 0)

    def gla(j, layer):
        with ExitStack() as cg:
            g_T = sb("g_T", [128, 8, T], ctx=cg)
            with ExitStack() as ctx:
                v = sb("v", [128, 3, D], ctx=ctx)
                att = sb("att", [128, H, 3, 128], ctx=ctx)
                qc = sb("qc", [128, H, 1, 3, 128], ctx=ctx)
                qm = sb("qm", [128, H, 1, NB, SAMPLE], ctx=ctx)
                kp = sb("kp", [128, 2, H, 128], ctx=ctx)
                km = sb("km", [SAMPLE, NB, H, 128], ctx=ctx)
                dec = sb("dec", [128, H, 4 + NB], ctx=ctx)
                gain = sb("gain", [128, 8], ctx=ctx)
                with ExitStack() as cq:
                    q_T = sb("q_T", [128, H, T], ctx=cq)
                    k_T = sb("k_T", [128, H, T], ctx=cq)
                    a_T = sb("a_T", [16, T], ctx=cq)
                    jobs = [job(0, "feature", lambda f: q_T[:, f, :], scale=128 ** -0.5),
                            job(GROUP, "feature", lambda f: k_T[:, f, :])]
                    jobs += [job(1024 + GROUP * g, "token", lambda i, g=g: v[0:ROWS[i], i, GROUP * g:GROUP * g + GROUP])
                             for g in range(2)]
                    jobs += [job(2048 + GROUP * g, "feature", lambda f, g=g: g_T[:, 4 * g + f, :], ACT.Silu)
                             for g in range(2)]
                    jobs += [job(3072, "feature", lambda f: a_T[:], width=16)]
                    project_in(io["gla_w_in"][j], jobs)

                    with phase("loaded", "step", "z", "z_sb", "az", "ez", "l1", "cum", "dif", "mag", "ex", "lev", "sc",
                               "sc_used", "acc", "qe", "kt", "kt_used", "kdec", "zero") as (block, s):
                        w_a2 = sb("w_a2", [16, 512], ctx=cq)
                        b_a = sb("b_a", [128, H], ctx=cq)
                        start = sb("start", [128, T], ctx=cq)
                        levels = sb("levels", [128, LEVELS, 128], ctx=cq)
                        memcol = sb("memcol", [128, NB, SAMPLE], ctx=cq)
                        member = sb("member", [SAMPLE, NB], ctx=cq)
                        z = sb("z", [128, H, T], ctx=cq)
                        az = sb("az", [128, H, T], ctx=cq)
                        cum = sb("cum", [128, H, T], ctx=cq)
                        dif = sb("dif", [128, H, T], ctx=cq)
                        ex = sb("ex", [128, H, T], ctx=cq)
                        ql = sb("ql", [128, 2, H, T], ctx=cq)
                        kl = sb("kl", [128, 2, H, T], ctx=cq)
                        tmp = sb("tmp", [128, H, 128], ctx=cq)
                        last_b = sb("last_b", [128, H, 4 + NB], ctx=cq)
                        units = [(lv, i) for lv in range(LEVELS) for i in range(3) if i < 2 or lv <= 3]

                        @block.sync
                        def _(sp):
                            for dst, src in ((w_a2, io["gla_w_a2"][j]), (b_a, io["gla_b_col"][j]), (start, io["c_start"]),
                                             (levels, io["c_levels"]), (memcol, io["c_memcol"]),
                                             (member, io["c_member"]), (gain, io["gla_gain"][j])):
                                sp.dma_start(dst[:], src).then_inc(s.loaded, 16)

                        @block.tensor
                        def _(pe):
                            pe.wait_ge(s.loaded, 16 * 7)
                            for h in range(H):
                                nc.tensor.matmul(ps[:, h, 0:T], w_a2[:, 128 * h:128 * h + 128], a_T[:], start=True,
                                                 stop=True).then_inc(s.z, 1)
                            for n, (lv, i) in enumerate(units):
                                t0, r = TILES[i]
                                pe.wait_ge(s.lev, lv + 1)
                                if n >= 2:
                                    pe.wait_ge(s.sc_used, n - 1)
                                q, k = (q_T, k_T) if lv == 0 else (ql[:, lv % 2], kl[:, lv % 2])
                                for h in range(H):
                                    last = nc.tensor.matmul(ps[0:r, 4 + n % 2, 128 * h:128 * h + r], k[:, h, t0:t0 + r],
                                                            q[:, h, t0:t0 + r], start=True, stop=True)
                                last.then_inc(s.sc, 1)
                            pe.wait_ge(s.kdec, 1)
                            for i, (t0, r) in enumerate(TILES):
                                if i >= 2:
                                    pe.wait_ge(s.kt_used, 1)
                                for h in range(H):
                                    last = nc.tensor.transpose(ps[0:r, 6 + i % 2, 128 * h:128 * h + 128],
                                                               az[:, h, t0:t0 + r], ident[:])
                                last.then_inc(s.kt, 1)

                        @block.scalar
                        def _(act):
                            for h in range(H):
                                act.wait_ge(s.z, h + 1)
                                nc.scalar.activation(z[:, h, :], ps[:, h, 0:T], ACT.Identity, bias=b_a[:, h:h + 1]
                                                     ).then_inc(s.z_sb, 1)
                            act.wait_ge(s.z_sb, H)
                            nc.scalar.activation(az[:], z[:], ACT.Abs).then_inc(s.az, 1)
                            act.wait_ge(s.az, 1)
                            nc.scalar.activation(ex[:], az[:], ACT.Exp, scale=-1.0).then_inc(s.ez, 1)
                            act.wait_ge(s.ez, 1)
                            nc.scalar.activation(dif[:], ex[:], ACT.Ln, bias=1.0).then_inc(s.l1, 1)
                            for lv in range(1, LEVELS):
                                act.wait_ge(s.dif, lv)
                                nc.scalar.activation(dif[:], dif[:], ACT.Abs).then_inc(s.mag, 1)
                                act.wait_ge(s.mag, lv)
                                if lv > 1:
                                    act.wait_ge(s.lev, lv)
                                nc.scalar.activation(ex[:], dif[:], ACT.Exp, scale=-1.0 / 16).then_inc(s.ex, 1)
                            act.wait_ge(s.dif, LEVELS)
                            act.wait_ge(s.lev, LEVELS)
                            nc.scalar.activation(ex[:], dif[:], ACT.Exp, scale=-1.0 / 16).then_inc(s.ex, 1)
                            act.wait_ge(s.kdec, 1)
                            nc.scalar.activation(dif[:], cum[:], ACT.Exp, scale=1.0 / 16).then_inc(s.ex, 1)
                            nc.scalar.activation(dec[:], last_b[:], ACT.Exp, scale=1.0 / 16)

                        @block.gpsimd
                        def _(pool):
                            nc.gpsimd.memset(qc[:], 0.0).then_inc(s.zero, 1)

                        @block.vector
                        def _(dve):
                            link = linker(dve, s.step)
                            dve.wait_ge(s.z_sb, H)
                            dve.wait_ge(s.az, 1)
                            link(nc.vector.tensor_scalar_min(z[:], z[:], 0.0))
                            dve.wait_ge(s.l1, 1)
                            link(nc.vector.tensor_tensor(z[:], z[:], dif[:], ALU.subtract))
                            for h in range(H):
                                nc.vector.tensor_tensor_scan(cum[:, h, :], start[:], z[:, h, :], 0.0, ALU.mult, ALU.add
                                                             ).then_inc(s.cum, 1)
                            dve.wait_ge(s.cum, H)
                            nc.vector.tensor_copy(last_b[:, :, 0:4], cum[:, :, 63:PROMPT:64])
                            nc.vector.tensor_copy(last_b[:, :, 4:4 + NB], cum[:, :, PROMPT + LS - 1:T:LS]
                                                  ).then_inc(s.lev, 1)

                            def spread(b):
                                size = 2 ** b
                                a = cum[:].rearrange("p h (n c) -> p (h n) c", c=size)
                                o = dif[:].rearrange("p h (n c) -> p (h n) c", c=size)
                                mid = a[:, :, size // 2 - 1:size // 2].to_broadcast([128, H * T // size, size])
                                return nc.vector.tensor_tensor(o, a, mid, ALU.subtract)

                            n = 0
                            for lv in range(LEVELS):
                                if lv:
                                    if lv > 1:
                                        dve.wait_ge(s.ex, lv - 1)
                                    spread(lv).then_inc(s.dif, 1)
                                    dve.wait_ge(s.ex, lv)
                                    if lv > 2:
                                        dve.wait_ge(s.sc, [m for m, u in enumerate(units) if u[0] == lv - 2][-1] + 1)
                                    nc.vector.tensor_tensor(ql[:, lv % 2], q_T[:], ex[:], ALU.mult)
                                    nc.vector.tensor_tensor(kl[:, lv % 2], k_T[:], ex[:], ALU.mult).then_inc(s.lev, 1)
                                for (l2, i) in units:
                                    if l2 != lv:
                                        continue
                                    t0, r = TILES[i]
                                    dve.wait_ge(s.sc, n + 1)
                                    src = ps[0:r, 4 + n % 2, :].rearrange("p (h t) -> p h t", h=H)[:, :, 0:r]
                                    mask = levels[0:r, lv:lv + 1, 0:r].to_broadcast([r, H, r])
                                    if lv == 0:
                                        nc.vector.tensor_tensor(att[0:r, :, i, 0:r], src, mask, ALU.mult
                                                                ).then_inc(s.sc_used, 1)
                                    else:
                                        nc.vector.tensor_tensor(tmp[0:r, :, 0:r], src, mask, ALU.mult
                                                                ).then_inc(s.sc_used, 1)
                                        dve.wait_ge(s.sc_used, n + 1)
                                        link(nc.vector.tensor_tensor(att[0:r, :, i, 0:r], att[0:r, :, i, 0:r],
                                                                     tmp[0:r, :, 0:r], ALU.add))
                                    n += 1
                            dve.wait_ge(s.ex, LEVELS - 1)
                            for c in range(4):
                                cc = slice(64 * c, 64 * c + 64)
                                nc.vector.tensor_tensor(dif[:, :, cc], cum[:, :, cc],
                                                        cum[:, :, 64 * c + 63:64 * c + 64].to_broadcast([128, H, 64]),
                                                        ALU.subtract)
                            for h in range(H):
                                a = cum[:, h, PROMPT:T].rearrange("p (n c) -> p n c", c=LS)
                                ins = nc.vector.tensor_tensor(dif[:, h, PROMPT:T].rearrange("p (n c) -> p n c", c=LS), a,
                                                              a[:, :, LS - 1:LS].to_broadcast([128, NB, LS]),
                                                              ALU.subtract)
                            ins.then_inc(s.dif, 1)
                            dve.wait_ge(s.ex, LEVELS)
                            nc.vector.tensor_tensor(az[:], k_T[:], ex[:], ALU.mult).then_inc(s.kdec, 1)
                            dve.wait_ge(s.ex, LEVELS + 1)
                            link(nc.vector.tensor_tensor(z[:], q_T[:], dif[:], ALU.mult))
                            dve.wait_ge(s.zero, 1)
                            for c in range(1, 4):
                                o = 64 * (c % 2)
                                nc.vector.tensor_copy(qc[:, :, 0, c - 1, o:o + 64], z[:, :, 64 * c:64 * c + 64])
                            for h in range(H):
                                nc.vector.tensor_tensor(
                                    qm[:, h, 0, :, :], z[:, h, PROMPT:T].rearrange("p (o t) -> p o t", o=1)
                                    .to_broadcast([128, NB, SAMPLE]), memcol[:], ALU.mult)
                            for i in range(3):
                                dve.wait_ge(s.kt, i + 1)
                                src = ps[0:ROWS[i], 6 + i % 2, :]
                                if i < 2:
                                    nc.vector.tensor_copy(kp[:, i, :, :], src.rearrange("p (h d) -> p h d", h=H)
                                                          ).then_inc(s.kt_used, 1)
                                else:
                                    for b in range(NB):
                                        nc.vector.tensor_scalar(km[:, b, :, :], src.rearrange("p (h d) -> p h d", h=H),
                                                                member[:, b:b + 1], None, ALU.mult)
                recurrent(1, 256, [(0, 0, 64), (0, 64, 128), (1, 0, 64), (1, 64, 128)], att, qc, qm, kp, km, dec, v, g_T,
                          gain, False, io["state_gla"][j], out[4][j], out[5][j])
            project_out(io["gla_w_out"][j], g_T, 8)
        residual_norm(layer, 0)

    def peer(layer):
        with ExitStack() as ctx:
            ea_T = sb("ea_T", [128, T], F16, ctx=ctx)
            eb_T = sb("eb_T", [128, T], F16, ctx=ctx)
            gh_T = sb("gh_T", [128, T], F16, ctx=ctx)
            gl_T = sb("gl_T", [128, T], F16, ctx=ctx)
            iota = sb("iota", [128, NK, 2], F16, ctx=ctx)
            u_in = sb("u_in", [128, 2, KT, 128], ctx=ctx)
            u_hi = sb("u_hi", [128, 2, KT, 128], F16, ctx=ctx)
            u_lo = sb("u_lo", [128, 2, KT, 128], F16, ctx=ctx)
            first = sb("first", [128, QUARTER, T], ctx=ctx)
            peer_choose(layer, ea_T, eb_T, gh_T, gl_T, iota, u_in, u_hi, u_lo, first)
            peer_experts(layer, ea_T, eb_T, gh_T, gl_T, iota, u_in, u_hi, u_lo, first)
        with ExitStack() as ctx:
            y_T = sb("y_T", [128, KT, T], ctx=ctx)
            with phase("moved", "x") as (block, s):
                @block.scalar
                def _(act):
                    scale = W_SCALE / (V_SCALE * G_SCALE)
                    nc.scalar.activation(y_T[:, :, 0:PROMPT], ps[:, 0:4, :].rearrange("p a (b t) -> p (a b) t", b=2),
                                         ACT.Copy, scale=scale)
                    nc.scalar.activation(y_T[:, :, PROMPT:T], ps[:, 4, :].rearrange("p (b t) -> p b t", b=KT),
                                         ACT.Copy, scale=scale)
            with phase("x") as (block, s):
                @block.tensor
                def _(pe):
                    for i, (t0, r) in enumerate(TILES):
                        for f in range(KT):
                            nc.tensor.transpose(ps[0:r, 2 * i + f // 4, 128 * (f % 4):128 * (f % 4) + 128],
                                                y_T[:, f, t0:t0 + r], ident[:])
        residual_norm(layer, 1)

    def peer_choose(layer, ea_T, eb_T, gh_T, gl_T, iota, u_in, u_hi, u_lo, first):
        QW = 2 * NK
        RUNS = ((0, 2), (2, 5), (5, 8), (8, UNDER // 2))
        SLOTS = 6
        with ExitStack() as ctx, phase("loaded", "w0", "w1", "w_sc", "w_hi", "w_lo0", "w_lo1", "q", "q_used", "u0", "u1", "us",
                                       "uh", "ul", "h", "gelu", "sc", "sc_sb", "free", "step", "picked", "shift", "exp",
                                       "ready", "tp", "tp_used", "hi") as (block, s):
            w_in = sb("w_in", [128, 2, KT, QW], ctx=ctx)
            w_hi = sb("w_hi", [128, 2, KT, QW], F16, ctx=ctx)
            w_lo = sb("w_lo", [128, 2, KT, QW], F16, ctx=ctx)
            q_T = sb("q_T", [128, 2 * PH, T], ctx=ctx)
            keys = sb("keys", [128, 2, NK], ctx=ctx)
            sc = sb("sc", [128, SLOTS, 4, NK], ctx=ctx)
            sc2 = sb("sc2", [128, 4, NK], ctx=ctx)
            val = sb("val", [128, 2, 2, PK], ctx=ctx)
            idx = sb("idx", [128, 2, 2, PK], U32, ctx=ctx)
            idf = sb("idf", [128, 2, 2, PK], F16, ctx=ctx)
            cand = sb("cand", [128, 2, PK, PK], ctx=ctx)
            cand2 = sb("cand2", [128, 2, PK, PK], ctx=ctx)
            hot = sb("hot", [128, 2, 2, PK, PK], F16, ctx=ctx)
            keys_no = sb("keys_no", [128, NK], ctx=ctx)
            best = sb("best", [128, 2, PK], ctx=ctx)
            ci = sb("ci", [128, 2, PK], U32, ctx=ctx)
            ij = sb("ij", [128, 2, 2, PK], U32, ctx=ctx)
            ijf = sb("ijf", [128, 2, 2, PK], F16, ctx=ctx)
            pick = sb("pick", [128, 3, 3, PH, PK], ctx=ctx)
            tot = sb("tot", [128, 3, PH], ctx=ctx)
            inv = sb("inv", [128, 3, PH], ctx=ctx)
            gt_T = sb("gt_T", [128, T], ctx=ctx)
            dsts = (ea_T, eb_T, gt_T)
            w_sem, w_lo_sem, u_sem = (s.w0, s.w1), (s.w_lo0, s.w_lo1), (s.u0, s.u1)
            w_q, u_tab = io["peer_w_q"][layer], io["peer_uT"]
            Q_BANK, S_BANK, TURN, H_BANK = 0, 2, 4, 5

            def in_order(eng, blocks, heads=None, weights=None, closing=None):
                for g, (lo, hi) in enumerate(RUNS):
                    if heads:
                        heads(g)
                    if lo == 0:
                        blocks(0)
                        lo = 1
                    if hi - 1 > lo:
                        with eng.Fori(lo, hi - 1) as n:
                            blocks(n * 2)
                    if closing and g == PH // 2 - 1:
                        closing()
                    blocks(2 * hi - 2)
                    if weights:
                        weights(g)

            def by_pool(hd):
                return hd % 2 == 1 and hd > 1

            def early(c):
                return isinstance(c, int) and c < 2

            @block.sync
            def _(sp):
                def load_w(hd):
                    if hd >= 2:
                        sp.wait_ge(w_lo_sem[hd % 2], hd // 2)
                    sp.dma_start(w_in[:, hd % 2], w_q[:, QW * hd:QW * hd + QW].rearrange("(k p) n -> p k n", p=128)
                                 ).then_inc(w_sem[hd % 2], 16)

                def load_u(c, p):
                    if not early(c):
                        sp.wait_ge(s.ul, c - 1)
                    sp.dma_start(u_in[:, p], u_tab[bass.ds(c + layer * NK, 1)].rearrange("o p k e -> p (o k) e")
                                 ).then_inc(u_sem[p], 16)

                load_w(0)
                load_w(1)
                for m, name in enumerate(("peer_keys_aT", "peer_keys_bT")):
                    sp.dma_start(keys[:, m, :], io[name][layer]).then_inc(s.loaded, 16)
                sp.dma_start(keys_no[:], io["c_iota"]).then_inc(s.loaded, 16)
                load_u(0, 0)
                load_u(1, 1)
                load_w(2)
                load_w(3)

                def weights(g):
                    for hd in (2 * g + 4, 2 * g + 5):
                        if hd < PH:
                            load_w(hd)

                def blocks(c):
                    load_u(c + 2, 0)
                    load_u(c + 3, 1)
                in_order(sp, blocks, weights=weights)

            @block.scalar
            def _(act):
                def split_w(hd):
                    p = hd % 2
                    act.wait_ge(w_sem[p], 16 * (hd // 2 + 1))
                    if by_pool(hd):
                        nc.scalar.activation(w_in[:, p], w_in[:, p], ACT.Copy, scale=W_SCALE).then_inc(s.w_sc, 1)
                        act.wait_ge(s.w_sc, hd // 2)
                    if hd >= 2:
                        act.wait_ge(s.q, 2 * hd - 2)
                    nc.scalar.activation(w_hi[:, p], w_in[:, p], ACT.Copy, scale=1.0 if by_pool(hd) else W_SCALE
                                         ).then_inc(s.w_hi, 1)

                def scale_u(c, p):
                    act.wait_ge(u_sem[p], (c - p) * 8 + 16)
                    nc.scalar.activation(u_in[:, p], u_in[:, p], ACT.Copy, scale=U_SCALE).then_inc(s.us, 1)

                def high_u(c, p):
                    act.wait_ge(s.us, c + 1)
                    if not early(c):
                        act.wait_ge(s.h, c - 1)
                    nc.scalar.copy(u_hi[:, p], u_in[:, p]).then_inc(s.uh, 1)

                split_w(0)
                split_w(1)
                for c in range(2):
                    scale_u(c, c)
                    high_u(c, c)

                def heads(g):
                    more = 2 * g + 2 < PH
                    queries(2 * g)
                    if more:
                        split_w(2 * g + 2)
                    queries(2 * g + 1)
                    scores(g)
                    if more:
                        split_w(2 * g + 3)

                def queries(hd):
                    for n in (2 * hd, 2 * hd + 1):
                        act.wait_ge(s.q, n + 1)
                        nc.scalar.activation(q_T[:, n, :], ps[:, Q_BANK + n % 2, 0:T], ACT.Copy,
                                             scale=1.0 / W_SCALE).then_inc(s.q_used, 1)

                def blocks(c):
                    for p in range(2):
                        scale_u(c + p + 2, p)
                        high_u(c + p + 2, p)
                        act.wait_ge(s.h, c + p + 1)
                        nc.scalar.activation(first[:, bass.ds(c + p, 1), :].rearrange("p o t -> p (o t)"),
                                             ps[:, H_BANK + p, 0:T], ACT.Gelu_apprx_tanh, scale=1.0 / U_SCALE
                                             ).then_inc(s.gelu, 1)

                def scores(g):
                    for i, (t0, r) in enumerate(TILES):
                        m = 3 * g + i
                        act.wait_ge(s.sc, m + 1)
                        if m >= SLOTS:
                            act.wait_ge(s.free, m - SLOTS + 1)
                        nc.scalar.copy(sc[0:r, m % SLOTS], ps[0:r, S_BANK + m % 2, :].rearrange("p (e n) -> p e n", e=4)
                                       ).then_inc(s.sc_sb, 1)

                def exponentials():
                    for i, (t0, r) in enumerate(TILES):
                        act.wait_ge(s.shift, 3 * (PH // 2 - 1) + i + 1)
                        nc.scalar.activation(pick[0:r, i, 2], pick[0:r, i, 2], ACT.Exp).then_inc(s.exp, 1)
                in_order(act, blocks, heads, closing=exponentials)

                for i, (t0, r) in enumerate(TILES):
                    act.wait_ge(s.tp, i + 1)
                    for m in range(3):
                        nc.scalar.copy(dsts[m][:, t0:t0 + r], ps[:, TURN, 128 * m:128 * m + r]).then_inc(s.tp_used, 1)
                act.wait_ge(s.tp_used, 9)
                nc.scalar.copy(gh_T[:], gt_T[:]).then_inc(s.hi, 1)

            @block.gpsimd
            def _(pool):
                def low_w(hd):
                    pool.wait_ge(s.w_hi, hd + 1)
                    nc.gpsimd.tensor_tensor(w_lo[:, 1], w_in[:, 1], w_hi[:, 1], ALU.subtract).then_inc(s.w_lo1, 1)

                def low_u(c, p):
                    pool.wait_ge(s.uh, c + 1)
                    nc.gpsimd.tensor_tensor(u_lo[:, p], u_in[:, p], u_hi[:, p], ALU.subtract).then_inc(s.ul, 1)

                low_u(0, 0)
                low_u(1, 1)

                def weights(g):
                    if 2 * g + 3 < PH:
                        low_w(2 * g + 3)

                def blocks(c):
                    low_u(c + 2, 0)
                    low_u(c + 3, 1)
                in_order(pool, blocks, weights=weights)

            @block.tensor
            def _(pe):
                def heads(g):
                    queries(g)
                    scores(g)

                def queries(g):
                    for hd in (2 * g, 2 * g + 1):
                        pe.wait_ge(w_lo_sem[hd % 2], hd // 2 + 1)
                        pe.wait_ge(s.w_hi, hd + 1)
                        for n in (2 * hd, 2 * hd + 1):
                            if n >= 2:
                                pe.wait_ge(s.q_used, n - 1)
                            at = slice(NK * (n % 2), NK * (n % 2) + NK)
                            for k in range(KT):
                                for e, (ww, xx) in enumerate(((w_hi, x_hi), (w_hi, x_lo), (w_lo, x_hi))):
                                    last = nc.tensor.matmul(ps[:, Q_BANK + n % 2, 0:T], ww[:, hd % 2, k, at],
                                                            xx[:, k, :], start=(k == 0 and e == 0),
                                                            stop=(k == KT - 1 and e == 2))
                            last.then_inc(s.q, 1)

                def blocks(c):
                    for p in range(2):
                        pe.wait_ge(s.uh, c + p + 1)
                        pe.wait_ge(s.ul, c + p + 1)
                        if not early(c):
                            pe.wait_ge(s.gelu, c + p - 1)
                        for k in range(KT):
                            dst = ps[:, H_BANK + p, 0:T]
                            nc.tensor.matmul(dst, u_hi[:, p, k, :], x_hi[:, k, :], start=(k == 0), stop=False)
                            nc.tensor.matmul(dst, u_hi[:, p, k, :], x_lo[:, k, :], start=False, stop=False)
                            last = nc.tensor.matmul(dst, u_lo[:, p, k, :], x_hi[:, k, :], start=False,
                                                    stop=(k == KT - 1))
                        last.then_inc(s.h, 1)

                def scores(g):
                    if g == 0:
                        pe.wait_ge(s.loaded, 48)
                    pe.wait_ge(s.q_used, 4 * g + 4)
                    for i, (t0, r) in enumerate(TILES):
                        m = 3 * g + i
                        if m >= 2:
                            pe.wait_ge(s.sc_sb, m - 1)
                        for e in range(4):
                            last = nc.tensor.matmul(ps[0:r, S_BANK + m % 2, NK * e:NK * e + NK],
                                                    q_T[:, 4 * g + e, t0:t0 + r], keys[:, e % 2, :], start=True,
                                                    stop=True)
                        last.then_inc(s.sc, 1)
                in_order(pe, blocks, heads)

                for i, (t0, r) in enumerate(TILES):
                    pe.wait_ge(s.ready, i + 1)
                    if i:
                        pe.wait_ge(s.tp_used, 3 * i)
                    for m in range(3):
                        last = nc.tensor.transpose(ps[:, TURN, 128 * m:128 * m + r],
                                                   pick[0:r, i, m].rearrange("p h k -> p (h k)"), ident[0:r, 0:r])
                    last.then_inc(s.tp, 1)

            @block.vector
            def _(dve):
                link = linker(dve, s.step)

                def top16(n, src, scratch, v_of, i_of):
                    for jj in range(n):
                        last = nc.vector.max(out=v_of(jj)[:, 0:8], in_=src(jj))
                    link(last)
                    for jj in range(n):
                        nc.vector.max_index(out=i_of(jj)[:, 0:8], in_max=v_of(jj)[:, 0:8], in_values=src(jj))
                    for jj in range(n):
                        last = nc.vector.match_replace(out=scratch(jj), in_to_replace=v_of(jj)[:, 0:8],
                                                       in_values=src(jj), imm_value=LOWEST)
                    link(last)
                    for jj in range(n):
                        last = nc.vector.max(out=v_of(jj)[:, 8:16], in_=scratch(jj))
                    link(last)
                    for jj in range(n):
                        last = nc.vector.max_index(out=i_of(jj)[:, 8:16], in_max=v_of(jj)[:, 8:16],
                                                   in_values=scratch(jj))
                    link(last)

                def choose(g, i):
                    r, m = ROWS[i], 3 * g + i
                    heads = slice(2 * g, 2 * g + 2)
                    dve.wait_ge(s.sc_sb, m + 1)
                    top16(4, lambda e: sc[0:r, m % SLOTS, e, :], lambda e: sc2[0:r, e, :],
                          lambda e: val[0:r, e // 2, e % 2, :], lambda e: idx[0:r, e // 2, e % 2, :])
                    nc.vector.tensor_copy(idf[0:r], idx[0:r]).then_inc(s.free, 1)
                    link(nc.vector.tensor_tensor(
                        cand[0:r], val[0:r, :, 0, :].rearrange("p h (k o) -> p h k o", o=1)
                        .to_broadcast([r, 2, PK, PK]), val[0:r, :, 1:2, :].to_broadcast([r, 2, PK, PK]), ALU.add))
                    top16(2, lambda h: cand[0:r, h].rearrange("p a b -> p (a b)"),
                          lambda h: cand2[0:r, h].rearrange("p a b -> p (a b)"),
                          lambda h: best[0:r, h, :], lambda h: ci[0:r, h, :])
                    nc.vector.tensor_single_scalar(ij[0:r, 0], ci[0:r], 4, ALU.logical_shift_right)
                    link(nc.vector.tensor_single_scalar(ij[0:r, 1], ci[0:r], PK - 1, ALU.bitwise_and))
                    link(nc.vector.tensor_copy(ijf[0:r], ij[0:r]))
                    nc.vector.tensor_tensor(pick[0:r, i, 2, heads], best[0:r],
                                            best[0:r, :, 0:1].to_broadcast([r, 2, PK]), ALU.subtract
                                            ).then_inc(s.shift, 1)
                    rows = [r, 4 * PK, PK]
                    link(nc.vector.tensor_tensor(
                        hot[0:r].rearrange("p m h a b -> p (m h a) b"),
                        ijf[0:r].rearrange("p m h (k o) -> p (m h k) o", o=1).to_broadcast(rows),
                        iota[0:r, 0:PK, 0].rearrange("p (o k) -> p o k", o=1).to_broadcast(rows), ALU.is_equal))
                    for n in range(2):
                        last = nc.vector.tensor_tensor(hot[0:r, n], hot[0:r, n],
                                                       idf[0:r, :, n:n + 1, :].to_broadcast([r, 2, PK, PK]), ALU.mult)
                    link(last)
                    nc.vector.tensor_reduce(pick[0:r, i, 0:2, heads], hot[0:r], AX, ALU.add).then_inc(s.picked, 1)

                def low_w(hd):
                    p = hd % 2
                    dve.wait_ge(s.w_hi, hd + 1)
                    nc.vector.scalar_tensor_tensor(out=w_lo[:, p], in0=w_in[:, p], scalar=W_SCALE, in1=w_hi[:, p],
                                                   op0=ALU.mult, op1=ALU.subtract).then_inc(w_lo_sem[p], 1)

                low_w(0)
                low_w(1)
                dve.wait_ge(s.loaded, 48)
                link(nc.vector.tensor_copy(iota[:], keys_no[:].rearrange("p (k o) -> p k o", o=1)
                                           .to_broadcast([128, NK, 2])))
                for g in range(PH // 2):
                    for i in range(3):
                        choose(g, i)
                        if i == 0 and 2 * g + 2 < PH:
                            low_w(2 * g + 2)
                for i, (t0, r) in enumerate(TILES):
                    dve.wait_ge(s.exp, i + 1)
                    link(nc.vector.tensor_reduce(tot[0:r, i], pick[0:r, i, 2], AX, ALU.add))
                    link(nc.vector.reciprocal(inv[0:r, i], tot[0:r, i]))
                    nc.vector.scalar_tensor_tensor(out=pick[0:r, i, 2], in0=pick[0:r, i, 2], scalar=G_SCALE,
                                                   in1=inv[0:r, i].rearrange("p (h o) -> p h o", o=1)
                                                   .to_broadcast([r, PH, PK]), op0=ALU.mult, op1=ALU.mult
                                                   ).then_inc(s.ready, 1)
                dve.wait_ge(s.hi, 1)
                nc.vector.tensor_tensor(gl_T[:], gt_T[:], gh_T[:], ALU.subtract)

    def peer_experts(layer, ea_T, eb_T, gh_T, gl_T, iota, u_in, u_hi, u_lo, first):
        u_tab, v_tab = io["peer_uT"], io["peer_v"]
        with ExitStack() as ctx, phase("u0", "u1", "v0", "v1", "uh", "ul", "vh", "vl", "h", "gelu", "w", "wh", "wl",
                                       "y", "eq", "rows", "cols", "g", "g_used", "us") as (block, s):
            gates = sb("gates", [128, 2, QUARTER, T], ctx=ctx)
            v_in = sb("v_in", [128, 2, D], ctx=ctx)
            v_hi = sb("v_hi", [128, 2, D], F16, ctx=ctx)
            v_lo = sb("v_lo", [128, 2, D], F16, ctx=ctx)
            ge = sb("ge", [128, 2, T], ctx=ctx)
            w = sb("w", [128, 2, T], ctx=ctx)
            w_hi = sb("w_hi", [128, 2, T], F16, ctx=ctx)
            w_lo = sb("w_lo", [128, 2, T], F16, ctx=ctx)
            hot_b = sb("hot_b", [128, 2, GT // 2, NK, 2], F16, ctx=ctx)
            hot = sb("hot", [128, 2, GT // 2, QUARTER, 2], F16, ctx=ctx)
            hot_hi = sb("hot_hi", [128, 2, GT // 2, QUARTER, 2], F16, ctx=ctx)
            hot_lo = sb("hot_lo", [128, 2, GT // 2, QUARTER, 2], F16, ctx=ctx)
            u_sem, v_sem = (s.u0, s.u1), (s.v0, s.v1)
            H_BANK, G_BANK = 5, 7

            def number(q, c):
                return c + QUARTER * q

            def later(q, c):
                return not (q == 0 and isinstance(c, int) and c < 2)

            def u_number(q, c):
                return number(q, c) - UNDER

            def split_number(q, c):
                return number(q, c) - SPLIT

            def block_at(q, c):
                return (q + 1, c - QUARTER) if isinstance(c, int) and c >= QUARTER else (q, c)

            def no_split_before(q, c):
                return q == 0 and split_number(q, c) < 2

            def spread(x, width, t):
                return x[:, t].rearrange("p (t o e) -> p t o e", o=1, e=2).to_broadcast([128, GT // 2, width, 2])

            def numbers(k0, width):
                return iota[:, k0:k0 + width].rearrange("p (o k) e -> p o k e", o=1).to_broadcast(
                    [128, GT // 2, width, 2])

            def scatter_vector(dve, q, c, p):
                n = number(q, c)
                t = bass.ds(c * GT, GT)
                if later(q, c):
                    dve.wait_ge(s.cols, n - 1)
                nc.vector.tensor_tensor(hot[:, p], numbers(QUARTER * q, QUARTER), spread(ea_T, QUARTER, t),
                                        ALU.is_equal).then_inc(s.eq, 1)
                if later(q, c):
                    dve.wait_ge(s.g, n - 1)
                nc.vector.tensor_tensor(hot_b[:, p], numbers(0, NK), spread(eb_T, NK, t), ALU.is_equal)
                dve.wait_ge(s.eq, n + 1)
                nc.vector.tensor_tensor(hot_hi[:, p], hot[:, p], spread(gh_T, QUARTER, t), ALU.mult
                                        ).then_inc(s.rows, 1)

            def scatter_pool(pool, q, c, p):
                n = number(q, c)
                t = bass.ds(c * GT, GT)
                if later(q, c):
                    pool.wait_ge(s.g, n - 1)
                pool.wait_ge(s.eq, n + 1)
                nc.gpsimd.tensor_tensor(hot_lo[:, p], hot[:, p], spread(gl_T, QUARTER, t), ALU.mult
                                        ).then_inc(s.cols, 1)

            def scatter_tensor(pe, q, c, p):
                n = number(q, c)
                pe.wait_ge(s.rows, n + 1)
                pe.wait_ge(s.cols, n + 1)
                if not (q == 0 and isinstance(c, int) and c < 1):
                    pe.wait_ge(s.g_used, n)
                for e in range(GT):
                    dst = ps[:, G_BANK, QUARTER * e:QUARTER * e + QUARTER]
                    rows = hot_b[:, p, e // 2, :, e % 2]
                    nc.tensor.matmul(dst, rows, hot_hi[:, p, e // 2, :, e % 2], start=True, stop=False)
                    last = nc.tensor.matmul(dst, rows, hot_lo[:, p, e // 2, :, e % 2], start=False, stop=True)
                last.then_inc(s.g, 1)

            def scatter_scalar(act, q, c, p):
                n = number(q, c)
                act.wait_ge(s.g, n + 1)
                if q >= 2:
                    act.wait_ge(s.w, QUARTER * (q - 1))
                nc.scalar.copy(gates[:, q % 2, :, bass.ds(c * GT, GT)],
                               ps[:, G_BANK, 0:GT * QUARTER].rearrange("p (t a) -> p a t", a=QUARTER)
                               ).then_inc(s.g_used, 1)

            def load_u(sp, q, c, p):
                if not no_split_before(q, c):
                    sp.wait_ge(s.ul, split_number(q, c) - 1)
                sp.dma_start(u_in[:, p], u_tab[bass.ds(c + (layer * NK + QUARTER * q), 1)]
                             .rearrange("o p k e -> p (o k) e")).then_inc(u_sem[p], 16)

            def load_v(sp, q, c, p):
                if later(q, c):
                    sp.wait_ge(s.vl, number(q, c) - 1)
                sp.dma_start(v_in[:, p], v_tab[bass.ds(c + (layer * NK + QUARTER * q), 1)]
                             .rearrange("o e d -> e (o d)")).then_inc(v_sem[p], 16)

            def u_high(act, q, c, p):
                act.wait_ge(u_sem[p], (split_number(q, c) - p) * 8 + 16)
                act.wait_ge(s.h, u_number(q, c) - 1)
                nc.scalar.activation(u_hi[:, p], u_in[:, p], ACT.Copy, scale=U_SCALE).then_inc(s.uh, 1)

            def u_opening_scalar(act, c, p):
                n = split_number(0, c)
                act.wait_ge(u_sem[p], (n - p) * 8 + 16)
                nc.scalar.activation(u_in[:, p], u_in[:, p], ACT.Copy, scale=U_SCALE).then_inc(s.us, 1)
                act.wait_ge(s.us, n + 1)
                act.wait_ge(s.h, u_number(0, c) - 1)
                nc.scalar.copy(u_hi[:, p], u_in[:, p]).then_inc(s.uh, 1)

            def gelu_opening(act, c, p):
                act.wait_ge(s.h, u_number(0, c) + 1)
                nc.scalar.activation(first[:, c, :], ps[:, H_BANK + p, 0:T], ACT.Gelu_apprx_tanh, scale=1.0 / U_SCALE
                                     ).then_inc(s.gelu, 1)

            def u_opening_pool(pool, c, p):
                pool.wait_ge(s.uh, split_number(0, c) + 1)
                nc.gpsimd.tensor_tensor(u_lo[:, p], u_in[:, p], u_hi[:, p], ALU.subtract).then_inc(s.ul, 1)

            def v_high(act, q, c, p):
                act.wait_ge(v_sem[p], (number(q, c) - p) * 8 + 16)
                if later(q, c):
                    act.wait_ge(s.y, number(q, c) - 1)
                nc.scalar.activation(v_hi[:, p], v_in[:, p], ACT.Copy, scale=V_SCALE).then_inc(s.vh, 1)

            def u_low(dve, q, c, p):
                dve.wait_ge(s.uh, split_number(q, c) + 1)
                nc.vector.scalar_tensor_tensor(out=u_lo[:, p].rearrange("p k e -> p (k e)"),
                                               in0=u_in[:, p].rearrange("p k e -> p (k e)"), scalar=U_SCALE,
                                               in1=u_hi[:, p].rearrange("p k e -> p (k e)"), op0=ALU.mult,
                                               op1=ALU.subtract).then_inc(s.ul, 1)

            def v_low(dve, q, c, p):
                dve.wait_ge(s.vh, number(q, c) + 1)
                nc.vector.scalar_tensor_tensor(out=v_lo[:, p], in0=v_in[:, p], scalar=V_SCALE, in1=v_hi[:, p],
                                               op0=ALU.mult, op1=ALU.subtract).then_inc(s.vl, 1)

            def gelu(act, q, c, p):
                if q > 0:
                    n = number(q, c)
                    act.wait_ge(s.h, u_number(q, c) + 1)
                    if later(q, c):
                        act.wait_ge(s.w, n - 1)
                    nc.scalar.activation(ge[:, p], ps[:, H_BANK + p, 0:T], ACT.Gelu_apprx_tanh, scale=1.0 / U_SCALE
                                         ).then_inc(s.gelu, 1)

            def w_high(act, q, c, p):
                n = number(q, c)
                act.wait_ge(s.w, n + 1)
                if later(q, c):
                    act.wait_ge(s.y, n - 1)
                nc.scalar.copy(w_hi[:, p], w[:, p]).then_inc(s.wh, 1)

            def gate(dve, q, c, p):
                n = number(q, c)
                if q > 0:
                    dve.wait_ge(s.gelu, u_number(q, c) + 1)
                elif isinstance(c, int) and c == 0:
                    dve.wait_ge(s.gelu, QUARTER - UNDER)
                dve.wait_ge(s.g_used, QUARTER * (q + 1))
                if later(q, c):
                    dve.wait_ge(s.wl, n - 1)
                src = ge[:, p] if q > 0 else first[:, bass.ds(c, 1), :].rearrange("p o t -> p (o t)")
                nc.vector.tensor_tensor(w[:, p], src,
                                        gates[:, q % 2, bass.ds(c, 1), :].rearrange("p o t -> p (o t)"), ALU.mult
                                        ).then_inc(s.w, 1)

            def w_low(pool, q, c, p):
                pool.wait_ge(s.wh, number(q, c) + 1)
                nc.gpsimd.tensor_tensor(w_lo[:, p], w[:, p], w_hi[:, p], ALU.subtract).then_inc(s.wl, 1)

            def u_ready(pe, q, c):
                n = u_number(q, c)
                if not (q == 0 and c < SPLIT):
                    pe.wait_ge(s.uh, split_number(q, c) + 1)
                    pe.wait_ge(s.ul, split_number(q, c) + 1)
                if not (q == 0 and n < 2):
                    pe.wait_ge(s.gelu, n - 1)

            def u_part(p, k, start, stop):
                dst = ps[:, H_BANK + p, 0:T]
                at = slice(k, k + 1) if isinstance(k, int) else bass.ds(k, 1)
                high, low = (u[:, p, at, :].rearrange("p o e -> p (o e)") for u in (u_hi, u_lo))
                x_high, x_low = (x[:, at, :].rearrange("p o t -> p (o t)") for x in (x_hi, x_lo))
                nc.tensor.matmul(dst, high, x_high, start=start, stop=False)
                nc.tensor.matmul(dst, high, x_low, start=False, stop=False)
                return nc.tensor.matmul(dst, low, x_high, start=False, stop=stop)

            def product_u(pe, q, c, p):
                u_ready(pe, q, c)
                for k in range(KT):
                    last = u_part(p, k, k == 0, k == KT - 1)
                last.then_inc(s.h, 1)

            def product_v(pe, q, c, p):
                n = number(q, c)
                begin = isinstance(n, int) and n == 0
                end = isinstance(n, int) and n == NK - 1
                pe.wait_ge(s.vl, n + 1)
                pe.wait_ge(s.wl, n + 1)
                for f in range(KT):
                    for m, (vv, ww) in enumerate(((v_hi, w_hi), (v_hi, w_lo), (v_lo, w_hi))):
                        lhs = vv[:, p, 128 * f:128 * f + 128]
                        nc.tensor.matmul(ps[:, f // 2, 256 * (f % 2):256 * (f % 2) + 256], lhs, ww[:, p, 0:PROMPT],
                                         start=(begin and m == 0 and f % 2 == 0), stop=(end and m == 2),
                                         skip_group_check=True)
                        last = nc.tensor.matmul(ps[:, 4, SAMPLE * f:SAMPLE * f + SAMPLE], lhs, ww[:, p, PROMPT:T],
                                                start=(begin and m == 0 and f == 0), stop=(end and m == 2),
                                                skip_group_check=True)
                last.then_inc(s.y, 1)

            def pairs(eng, q, head, tail, pair):
                if head:
                    pair(q, 0)
                with eng.Fori(1 if head else 0, QUARTER // 2 - (1 if tail else 0)) as n:
                    pair(q, n * 2)
                if tail:
                    pair(q, QUARTER - 2)

            def each_pair(eng, pair, begin=None):
                for q in range(4):
                    if begin:
                        begin(q)
                    pairs(eng, q, q <= 1, True, pair)

            def opening(eng, step, begin=None, middle=None, end=None):
                for b in range(UNDER, QUARTER):
                    c = KT * (b - UNDER)
                    if begin:
                        begin(b)
                    step(c, 0)
                    if middle:
                        middle(b)
                    with eng.Fori(1, KT // 2 - 1) as n:
                        step(n * 2 + c, n * 2)
                    step(c + KT - 2, KT - 2)
                    if end:
                        end(b)

            def w_next(c, p):
                return not (isinstance(c, int) and c + p == QUARTER - 1)

            def u_ahead(q, c, p, by):
                at_end = isinstance(c, int) and c + p + by >= QUARTER
                return at_end if q == 0 else not (q == 3 and at_end)

            @block.sync
            def _(sp):
                for c in range(SPLIT, QUARTER):
                    load_u(sp, 0, c, c % 2)

                def pair(q, c):
                    for p in range(2):
                        if q > 0:
                            load_u(sp, q, c + p, p)
                        load_v(sp, q, c + p, p)
                each_pair(sp, pair)

            @block.scalar
            def _(act):
                def step(c, k):
                    scatter_scalar(act, 0, c, 0)
                    scatter_scalar(act, 0, c + 1, 1)

                def end(b):
                    if b + 2 < QUARTER:
                        u_opening_scalar(act, b + 2, b % 2)
                    gelu_opening(act, b, b % 2)
                    if b == UNDER:
                        v_high(act, 0, 0, 0)
                opening(act, step, end=end)

                def pair(q, c):
                    done = q == 3 and isinstance(c, int) and c == QUARTER - 2
                    for p in range(2):
                        if w_next(c, p):
                            gelu(act, q, c + p + 1, 1 - p)
                        if u_ahead(q, c, p, 2):
                            u_high(act, *block_at(q, c + p + 2), p)
                        if not (done and p):
                            v_high(act, q, c + p + 1, 1 - p)
                        if w_next(c, p):
                            w_high(act, q, c + p + 1, 1 - p)
                        if q < 3:
                            scatter_scalar(act, q + 1, c + p, p)

                def begin(q):
                    gelu(act, q, 0, 0)
                    w_high(act, q, 0, 0)
                each_pair(act, pair, begin)

            @block.vector
            def _(dve):
                def step(c, k):
                    scatter_vector(dve, 0, c, 0)
                    scatter_vector(dve, 0, c + 1, 1)
                opening(dve, step)

                def begin(q):
                    gate(dve, q, 0, 0)
                    if q == 0:
                        v_low(dve, 0, 0, 0)

                def pair(q, c):
                    done = q == 3 and isinstance(c, int) and c == QUARTER - 2
                    for p in range(2):
                        if q < 3:
                            scatter_vector(dve, q + 1, c + p, p)
                        if w_next(c, p):
                            gate(dve, q, c + p + 1, 1 - p)
                        if u_ahead(q, c, p, 2):
                            u_low(dve, *block_at(q, c + p + 2), p)
                        if not (done and p):
                            v_low(dve, q, c + p + 1, 1 - p)
                each_pair(dve, pair, begin)

            @block.gpsimd
            def _(pool):
                def step(c, k):
                    scatter_pool(pool, 0, c, 0)
                    scatter_pool(pool, 0, c + 1, 1)

                def middle(b):
                    if SPLIT <= b + 1 < QUARTER:
                        u_opening_pool(pool, b + 1, (b + 1) % 2)
                opening(pool, step, middle=middle)

                def pair(q, c):
                    for p in range(2):
                        if q < 3:
                            scatter_pool(pool, q + 1, c + p, p)
                        if w_next(c, p):
                            w_low(pool, q, c + p + 1, 1 - p)
                each_pair(pool, pair, lambda q: w_low(pool, q, 0, 0))

            @block.tensor
            def _(pe):
                at = {}

                def begin(b):
                    at["block"] = b
                    u_ready(pe, 0, b)

                def step(c, k):
                    p = at["block"] % 2
                    for m in range(2):
                        scatter_tensor(pe, 0, c + m, m)
                        first_k, last_k = isinstance(k, int) and k + m == 0, isinstance(k, int) and k + m == KT - 1
                        last = u_part(p, k + m, first_k, last_k)
                    if last_k:
                        last.then_inc(s.h, 1)
                opening(pe, step, begin=begin)

                def pair(q, c):
                    for p in range(2):
                        if u_ahead(q, c, p, 1):
                            product_u(pe, *block_at(q, c + p + 1), 1 - p)
                        if q < 3:
                            scatter_tensor(pe, q + 1, c + p, p)
                        product_v(pe, q, c + p, p)
                each_pair(pe, pair)

    with root:
        yield_layers = (sgu, retention, gla)
        for layer in range(DEPTH):
            yield_layers[layer % 3](layer // 3, layer)
            peer(layer)
        with phase("stored") as (block, s):
            @block.sync
            def _(sp):
                sp.dma_start(out[0].rearrange("b (i p) d -> p (b i) d", p=128), x_tok[:, 0:2, :]
                             ).then_inc(s.stored, 16)
                sp.dma_start(out[1].rearrange("b l d -> (b l) d"), x_tok[0:SAMPLE, 2, :]).then_inc(s.stored, 16)
                sp.wait_ge(s.stored, 32)


_PLAIN = ["x_prompt", "x_sample", "state_ret", "state_gla", "sgu_w_in", "sgu_b_in", "sgu_v_g", "sgu_v_b", "sgu_b_s",
          "sgu_w_out", "ret_w_in", "ret_w_out", "gla_w_in", "gla_w_a2", "gla_w_out", "peer_w_q", "ln_g", "ln_b"]
_OUTS = [(1, PROMPT, D), (NB, LS, D), (1, 1, H, 256, 512), (1, NB, H, 256, 512), (1, 1, H, 128, 256),
         (1, NB, H, 128, 256), (2, NB, LS, D)]


def kernel(**inputs):
    import concourse.bacc as bacc
    from concourse.bass_utils import run_bass_kernel_spmd

    a = {k: np.asarray(v) for k, v in inputs.items()}
    arrays = {n: a[n] for n in _PLAIN}
    arrays["sgu_b_col"] = a["sgu_b_in"].reshape(2, 16, 128).transpose(0, 2, 1)
    arrays["ret_gain"] = a["ret_gn_g"].reshape(1, 16, 128).transpose(0, 2, 1)
    arrays["gla_b_col"] = a["gla_b_a"].reshape(1, 4, 128).transpose(0, 2, 1)
    arrays["gla_gain"] = np.tile(a["gla_rms_g"].reshape(1, 2, 128).transpose(0, 2, 1), (1, 1, H))
    arrays["sgu_w_sT"] = a["sgu_w_s"].transpose(0, 1, 3, 2)
    arrays["peer_keys_aT"] = a["peer_keys_a"].transpose(0, 2, 1)
    arrays["peer_keys_bT"] = a["peer_keys_b"].transpose(0, 2, 1)
    arrays["peer_uT"] = a["peer_u"].reshape(DEPTH * NK, 128, KT, 128).transpose(0, 3, 2, 1)
    arrays["peer_v"] = a["peer_v"].reshape(DEPTH * NK, 128, D)
    arrays.update(shape_constants())
    arrays = {f"in_{n}": np.ascontiguousarray(v) for n, v in arrays.items()}
    nc = bacc.Bacc("TRN2", target_bir_lowering=False, num_devices=1)
    io = {n[3:]: nc.dram_tensor(n, v.shape, mybir.dt.from_np(v.dtype), kind="ExternalInput").ap()
          for n, v in arrays.items()}
    out = [nc.dram_tensor(f"out_{i}", shape, F32, kind="ExternalOutput").ap() for i, shape in enumerate(_OUTS)]
    build(nc, io, out)
    r = run_bass_kernel_spmd(nc, [arrays], core_ids=[0])
    return tuple(r.results[0][f"out_{i}"] for i in range(len(_OUTS)))
```

```python
from collections import namedtuple
from contextlib import ExitStack, contextmanager

import numpy as np
import concourse.bass as bass
from concourse import mybir

F32 = mybir.dt.float32
F16 = mybir.dt.float16
U32 = mybir.dt.uint32
ALU = mybir.AluOpType
ACT = mybir.ActivationFunctionType
AX = mybir.AxisListType.X

D = 1024
KT = D // 128
PROMPT, NB, LS = 256, 8, 8
SAMPLE = NB * LS
T = PROMPT + SAMPLE
ROWS = [128, 128, SAMPLE]
TILES = [(0, 128), (128, 128), (256, SAMPLE)]
DEPTH = 4
PAST = 2048
H = 4
EPS = 1e-5
ALPHA = (2.0 * DEPTH) ** 0.25
GROUP = 512
LEVELS = 7
PH, PK, NK = 8, 16, 128
QUARTER = NK // 4
UNDER = QUARTER - 4
SPLIT = UNDER + 2
GT = T // QUARTER
U_SCALE, V_SCALE, G_SCALE = 64.0, 16.0, 16.0
W_SCALE = 64.0
LOWEST = -3.0e38

Job = namedtuple("Job", "col kind dest func bias scale width")
Side = namedtuple("Side", "signals load mask biases")


def ret_log_decay():
    return np.log1p(-np.exp2(-5.0 - np.arange(H))).astype(np.float32)


def shape_constants():
    f = np.float32

    def exp(x):
        return np.exp(x.astype(np.float64)).astype(f)
    pos = np.concatenate([np.arange(PROMPT), np.tile(PAST + np.arange(LS), NB)]).astype(f)
    inv = (10000.0 ** (-np.arange(0, 256, 2) / 256)).astype(f)
    ang = (pos[None, :] * inv[:, None]).astype(f)
    lg = ret_log_decay()
    step = np.concatenate([np.arange(128), np.arange(128), np.tile(np.arange(LS), NB)]).astype(f)
    size = np.concatenate([np.full(PROMPT, 128), np.full(SAMPLE, LS)]).astype(f)
    cross = exp((step + 1)[None, :] * lg[:, None])
    keep = exp((size - 1 - step)[None, :] * lg[:, None]) / f(16)
    rel = np.arange(128)[None, :] - np.arange(128)[:, None]
    decay = np.where(rel >= 0, exp(np.maximum(rel, 0).astype(f)[None] * lg[:, None, None]) / f(16), 0).astype(f)
    seq = np.arange(SAMPLE) // LS
    same = seq[None, :] == seq[:, None]
    decay_s = np.where(same, decay[:, :SAMPLE, :SAMPLE], 0).astype(f)
    member = (seq[:, None] == np.arange(NB)[None, :]).astype(f)
    kd = np.zeros((128, 3, H), f)
    for i, (t0, n) in enumerate(TILES):
        kd[:n, i] = keep[:, t0:t0 + n].T
    kdm = np.einsum("sb,sh->sbh", member, kd[:SAMPLE, 2]).astype(f)
    s, t = np.arange(128)[:, None], np.arange(128)[None, :]
    levels = [s == t] + [(s // b == t // b) & (s % b < b // 2) & (t % b >= b // 2) for b in (2, 4, 8, 16, 32, 64)]
    start = np.ones(T, f)
    start[0:PROMPT:64] = 0
    start[PROMPT::LS] = 0
    dec = np.concatenate([np.repeat(exp(128 * lg)[:, None], 2, 1), np.repeat(exp(LS * lg)[:, None], NB, 1)], 1)
    rows = np.ones((128, 1), f)
    return {
        "c_cos": np.cos(ang.astype(np.float64)).astype(f),
        "c_sin": np.sin(ang.astype(np.float64)).astype(f),
        "c_cross": (rows[:, None] * cross[None]).astype(f),
        "c_decay": np.ascontiguousarray(decay.transpose(1, 0, 2)),
        "c_decay_s": np.ascontiguousarray(decay_s.transpose(1, 0, 2)),
        "c_kd": kd,
        "c_kdm": kdm,
        "c_member": member,
        "c_memcol": (rows[:, None] * member.T[None]).astype(f),
        "c_levels": np.ascontiguousarray(np.stack(levels).astype(f).transpose(1, 0, 2)),
        "c_start": (rows * start[None]).astype(f),
        "c_dec": (rows[:, None] * dec[None]).astype(f),
        "c_ident": np.eye(128, dtype=f),
        "c_iota": (rows * np.arange(NK)[None]).astype(f),
        "c_ones": np.ones((1, 128), f),
    }


def build(nc, io, out):

    @contextmanager
    def phase(*names):
        handles = [nc.alloc_semaphore(f"{n}_{nc.next_id()}") for n in names]
        with nc.Block() as block:
            yield block, namedtuple("Signals", names)(*handles)
        nc.clear_and_free_semaphores(handles)
        nc.all_engine_barrier()

    def linker(eng, sem):
        n = [0]

        def link(ins):
            n[0] += 1
            ins.then_inc(sem, 1)
            eng.wait_ge(sem, n[0])
        return link

    root = ExitStack()

    def sb(name, shape, dt=F32, ctx=root):
        return ctx.enter_context(nc.sbuf_tensor(f"{name}_{nc.next_id()}", shape, dt))

    ps = root.enter_context(nc.psum_tensor("ps", [128, 8, 512], F32))
    x_tok = sb("x_tok", [128, 3, D])
    x_T = sb("x_T", [128, KT, T])
    x_hi = sb("x_hi", [128, KT, T], F16)
    x_lo = sb("x_lo", [128, KT, T], F16)
    ident = sb("ident", [128, 128])
    ones = sb("ones", [1, 128])
    w_ones = sb("w_ones", [1, 128])
    eps = sb("eps", [128, 1])
    w_eps = sb("w_eps", [128, 1])

    def emit_transposes(pe, s, banks, wait_first):
        n = 0
        for i, (t0, r) in enumerate(TILES):
            wait_first(i)
            for q in range(KT // 4):
                if n >= 2:
                    pe.wait_ge(s.tp_used, n - 1)
                for j in range(4):
                    last = nc.tensor.transpose(ps[:, banks[n % 2], j * 128:j * 128 + r],
                                               x_tok[0:r, i, (4 * q + j) * 128:(4 * q + j + 1) * 128],
                                               ident[0:r, 0:r])
                last.then_inc(s.tp, 1)
                n += 1

    def emit_transpose_copies(act, s, banks):
        n = 0
        for i, (t0, r) in enumerate(TILES):
            for q in range(KT // 4):
                act.wait_ge(s.tp, n + 1)
                nc.scalar.copy(x_T[:, 4 * q:4 * q + 4, t0:t0 + r],
                               ps[:, banks[n % 2], :].rearrange("p (j t) -> p j t", j=4)[:, :, 0:r]
                               ).then_inc(s.tp_used, 1)
                n += 1
            act.wait_ge(s.tp_used, n)
            nc.scalar.copy(x_hi[:, :, t0:t0 + r], x_T[:, :, t0:t0 + r]).then_inc(s.hi, 1)

    def emit_low_parts(dve, s):
        for i, (t0, r) in enumerate(TILES):
            dve.wait_ge(s.hi, i + 1)
            nc.vector.tensor_tensor(x_lo[:, :, t0:t0 + r], x_T[:, :, t0:t0 + r], x_hi[:, :, t0:t0 + r],
                                    ALU.subtract)

    with phase("loaded", "tp", "tp_used", "hi") as (block, s):
        @block.sync
        def _(sp):
            sp.dma_start(x_tok[:, 0:2, :], io["x_prompt"].rearrange("b (i p) d -> p (b i) d", p=128)
                         ).then_inc(s.loaded, 16)
            sp.dma_start(x_tok[0:SAMPLE, 2, :], io["x_sample"].rearrange("b l d -> (b l) d")
                         ).then_inc(s.loaded, 16)
            sp.dma_start(ident[:], io["c_ident"]).then_inc(s.loaded, 16)
            sp.dma_start(ones[:], io["c_ones"]).then_inc(s.loaded, 16)

        @block.vector
        def _(dve):
            nc.vector.memset(eps[:], EPS)
            nc.vector.memset(w_eps[:], EPS * W_SCALE ** 2)
            nc.vector.memset(w_ones[:], W_SCALE)
            emit_low_parts(dve, s)

        @block.tensor
        def _(pe):
            emit_transposes(pe, s, (0, 1), lambda i: pe.wait_ge(s.loaded, 64) if i == 0 else None)

        @block.scalar
        def _(act):
            emit_transpose_copies(act, s, (0, 1))

    def project_in(w, jobs, side=None):
        units = []
        for g, j in enumerate(jobs):
            for f in range(-(-j.width // 128) if j.kind == "feature" else 3):
                units.append((g, j, f))

        def units_through(g):
            return sum(u[0] <= g for u in units)

        PARTS, PK_T = 4, KT // 4
        arrivals = [f"w{p}_{m}" for p in range(2) for m in range(PARTS)]
        with ExitStack() as ctx, phase(*arrivals, "w_hi", "w_lo", "out", "out_used",
                                       *(side.signals if side else ())) as (block, s):
            w_in = sb("w_in", [128, 2, KT, GROUP], ctx=ctx)
            w_hi = sb("w_hi", [128, 2, KT, GROUP], F16, ctx=ctx)
            w_lo = sb("w_lo", [128, 2, KT, GROUP], F16, ctx=ctx)
            w_sem = (s[0:PARTS], s[PARTS:2 * PARTS])

            def tiles_of(m):
                return slice(PK_T * m, PK_T * m + PK_T)

            @block.sync
            def _(sp):
                for g, j in enumerate(jobs):
                    for m in range(PARTS):
                        if g >= 2:
                            sp.wait_ge(s.w_lo, PARTS * (g - 2) + m + 1)
                        sp.dma_start(w_in[:, g % 2, tiles_of(m), 0:j.width],
                                     w[128 * PK_T * m:128 * PK_T * (m + 1), j.col:j.col + j.width]
                                     .rearrange("(k p) n -> p k n", p=128)).then_inc(w_sem[g % 2][m], 16)
                    if g == 0 and side:
                        side.load(sp, s)

            if side:
                @block.gpsimd
                def _(pool):
                    side.mask(pool, s)

            @block.tensor
            def _(pe):
                if side:
                    pe.wait_ge(s.bias, side.biases)

                def part_ready(g, f, k):
                    if f == 0 and k % PK_T == 0:
                        pe.wait_ge(s.w_hi, PARTS * g + k // PK_T + 1)
                        pe.wait_ge(s.w_lo, PARTS * g + k // PK_T + 1)

                for n, (g, j, f) in enumerate(units):
                    if n >= 6:
                        pe.wait_ge(s.out_used, n - 5)
                    bank, p = n % 6, g % 2
                    parts = ((w_hi, x_hi), (w_hi, x_lo), (w_lo, x_hi))
                    if j.kind == "feature":
                        m = min(128, j.width - 128 * f)
                        for k in range(KT):
                            part_ready(g, f, k)
                            for e, (ww, xx) in enumerate(parts):
                                last = nc.tensor.matmul(ps[0:m, bank, 0:T], ww[:, p, k, 128 * f:128 * f + m],
                                                        xx[:, k, :], start=(k == 0 and e == 0),
                                                        stop=(k == KT - 1 and e == 2))
                    else:
                        t0, r = TILES[f]
                        for k in range(KT):
                            part_ready(g, f, k)
                            for e, (ww, xx) in enumerate(parts):
                                last = nc.tensor.matmul(ps[0:r, bank, 0:j.width], xx[:, k, t0:t0 + r],
                                                        ww[:, p, k, 0:j.width], start=(k == 0 and e == 0),
                                                        stop=(k == KT - 1 and e == 2 and j.bias is None))
                        if j.bias is not None:
                            last = nc.tensor.matmul(ps[0:r, bank, 0:j.width], w_ones[:, 0:r], j.bias,
                                                    start=False, stop=True)
                    last.then_inc(s.out, 1)

            @block.scalar
            def _(act):
                def split(g):
                    j = jobs[g]
                    if g >= 2:
                        act.wait_ge(s.out, units_through(g - 2))
                    for m in range(PARTS):
                        act.wait_ge(w_sem[g % 2][m], 16 * (g // 2 + 1))
                        nc.scalar.activation(w_hi[:, g % 2, tiles_of(m), 0:j.width],
                                             w_in[:, g % 2, tiles_of(m), 0:j.width], ACT.Copy, scale=W_SCALE
                                             ).then_inc(s.w_hi, 1)

                split(0)
                if side:
                    act.wait_ge(s.bias, side.biases)
                for n, (g, j, f) in enumerate(units):
                    if f == 0 and g + 1 < len(jobs):
                        split(g + 1)
                    act.wait_ge(s.out, n + 1)
                    dst = j.dest(f)
                    bias = j.bias[:, f:f + 1] if j.kind == "feature" and j.bias is not None else 0.0
                    width = T if j.kind == "feature" else j.width
                    nc.scalar.activation(dst, ps[0:dst.shape[0], n % 6, 0:width], j.func, bias=bias,
                                         scale=j.scale / W_SCALE).then_inc(s.out_used, 1)

            @block.vector
            def _(dve):
                for g, j in enumerate(jobs):
                    for m in range(PARTS):
                        dve.wait_ge(s.w_hi, PARTS * g + m + 1)
                        at = (slice(None), g % 2, tiles_of(m), slice(0, j.width))
                        nc.vector.scalar_tensor_tensor(out=w_lo[at], in0=w_in[at], scalar=W_SCALE, in1=w_hi[at],
                                                       op0=ALU.mult, op1=ALU.subtract).then_inc(s.w_lo, 1)

    def job(col, kind, dest, func=None, bias=None, scale=1.0, width=GROUP):
        return Job(col, kind, dest, func or ACT.Copy, bias, scale, width)

    def project_out(w, src, kt):
        with ExitStack() as ctx, phase("w0", "w1", "w2", "w3", "hi", "lo", "src_hi", "out") as (block, s):
            w_in = sb("w_in", [128, 4, D], ctx=ctx)
            w_hi = sb("w_hi", [128, 4, D], F16, ctx=ctx)
            w_lo = sb("w_lo", [128, 4, D], F16, ctx=ctx)
            s_hi = sb("s_hi", [128, kt, T], F16, ctx=ctx)
            s_lo = sb("s_lo", [128, kt, T], F16, ctx=ctx)
            w_sem = (s.w0, s.w1, s.w2, s.w3)

            @block.sync
            def _(sp):
                for k in range(kt):
                    if k >= 4:
                        sp.wait_ge(s.lo, k - 3)
                    sp.dma_start(w_in[:, k % 4, :], w[128 * k:128 * k + 128, :]).then_inc(w_sem[k % 4], 16)

            @block.scalar
            def _(act):
                for k in range(kt):
                    nc.scalar.copy(s_hi[:, k, :], src[:, k, :]).then_inc(s.src_hi, 1)
                    act.wait_ge(w_sem[k % 4], 16 * (k // 4 + 1))
                    if k >= 4:
                        act.wait_ge(s.out, k - 3)
                    nc.scalar.activation(w_hi[:, k % 4, :], w_in[:, k % 4, :], ACT.Copy, scale=W_SCALE
                                         ).then_inc(s.hi, 1)

            @block.vector
            def _(dve):
                for k in range(kt):
                    dve.wait_ge(s.src_hi, k + 1)
                    nc.vector.tensor_tensor(s_lo[:, k, :], src[:, k, :], s_hi[:, k, :], ALU.subtract)
                    dve.wait_ge(s.hi, k + 1)
                    nc.vector.scalar_tensor_tensor(out=w_lo[:, k % 4, :], in0=w_in[:, k % 4, :], scalar=W_SCALE,
                                                   in1=w_hi[:, k % 4, :], op0=ALU.mult, op1=ALU.subtract
                                                   ).then_inc(s.lo, 1)

            @block.tensor
            def _(pe):
                for k in range(kt):
                    pe.wait_ge(s.lo, k + 1)
                    pe.wait_ge(s.hi, k + 1)
                    for i, (t0, r) in enumerate(TILES):
                        for e, (ss, ww) in enumerate(((s_hi, w_hi), (s_hi, w_lo), (s_lo, w_hi))):
                            for n in range(2):
                                last = nc.tensor.matmul(ps[0:r, 2 * i + n, :], ss[:, k, t0:t0 + r],
                                                        ww[:, k % 4, 512 * n:512 * n + 512],
                                                        start=(k == 0 and e == 0), stop=(k == kt - 1 and e == 2))
                    last.then_inc(s.out, 1)

    def residual_norm(layer, which, q_in=None, q_hi=None):
        with ExitStack() as ctx, phase("loaded", "step", "var", "std", "rs", "norm", "gain", "ready0", "ready", "ahead",
                                       "tp", "tp_used", "hi") as (block, s):
            g_row = sb("g_row", [128, D], ctx=ctx)
            b_row = sb("b_row", [128, D], ctx=ctx)
            st = sb("st", [128, 3, 2, 6], ctx=ctx)
            mv = sb("mv", [128, 3, 2], ctx=ctx)
            sd = sb("sd", [128, 3], ctx=ctx)
            rs = sb("rs", [128, 3], ctx=ctx)
            shift = sb("shift", [128, 3], ctx=ctx)
            rows = [x_tok[0:r, i, :] for i, (t0, r) in enumerate(TILES)]

            @block.sync
            def _(sp):
                sp.dma_start(g_row[:], io["ln_g"][layer, which:which + 1, :].partition_broadcast(128)
                             ).then_inc(s.loaded, 16)
                sp.dma_start(b_row[:], io["ln_b"][layer, which:which + 1, :].partition_broadcast(128)
                             ).then_inc(s.loaded, 16)
                if q_in is not None:
                    sp.dma_start(q_in[:], io["peer_w_q"][layer][:, 0:2 * NK].rearrange("(k p) n -> p k n", p=128)
                                 ).then_inc(s.ahead, 16)

            @block.vector
            def _(dve):
                link = linker(dve, s.step)

                def moments(i):
                    x, r = rows[i], ROWS[i]
                    link(nc.vector.scalar_tensor_tensor(out=x, in0=x, scalar=ALPHA * W_SCALE,
                                                        in1=ps[0:r, 2 * i:2 * i + 2, :].rearrange("p a b -> p (a b)"),
                                                        op0=ALU.mult, op1=ALU.add))
                    nc.vector.bn_stats(out=st[0:r, i, 0, :], in_=x[:, 0:512])
                    link(nc.vector.bn_stats(out=st[0:r, i, 1, :], in_=x[:, 512:1024]))
                    nc.vector.bn_aggr(out=mv[0:r, i, :], in_=st[0:r, i, :, :].rearrange("p a b -> p (a b)")
                                      ).then_inc(s.var, 1)

                def factors(i):
                    at = (slice(0, ROWS[i]), slice(i, i + 1))
                    dve.wait_ge(s.var, i + 1)
                    dve.wait_ge(s.std, i + 1)
                    link(nc.vector.reciprocal(rs[at], sd[at]))
                    nc.vector.scalar_tensor_tensor(out=shift[at], in0=mv[0:ROWS[i], i, 0:1], scalar=-1.0, in1=rs[at],
                                                   op0=ALU.mult, op1=ALU.mult).then_inc(s.rs, 1)

                def gain(i):
                    dve.wait_ge(s.norm, i + 1)
                    nc.vector.tensor_tensor(rows[i], rows[i], g_row[0:ROWS[i], :], ALU.mult).then_inc(s.gain, 1)

                def offset(i):
                    dve.wait_ge(s.gain, i + 1)
                    nc.vector.tensor_tensor(rows[i], rows[i], b_row[0:ROWS[i], :], ALU.add).then_inc(s.ready, 1)

                moments(0)
                moments(1)
                factors(0)
                factors(1)
                moments(2)
                dve.wait_ge(s.loaded, 32)
                gain(0)
                factors(2)
                gain(1)
                offset(1)
                gain(2)
                offset(2)
                emit_low_parts(dve, s)

            @block.gpsimd
            def _(pool):
                pool.wait_ge(s.gain, 1)
                nc.gpsimd.tensor_tensor(rows[0], rows[0], b_row[:], ALU.add).then_inc(s.ready0, 1)

            @block.tensor
            def _(pe):
                emit_transposes(pe, s, (6, 7),
                                lambda i: pe.wait_ge(s.ready, i) if i else pe.wait_ge(s.ready0, 1))

            @block.scalar
            def _(act):
                def deviation(i):
                    r = ROWS[i]
                    act.wait_ge(s.var, i + 1)
                    nc.scalar.activation(sd[0:r, i:i + 1], mv[0:r, i, 1:2], ACT.Sqrt, bias=w_eps[0:r, :]
                                         ).then_inc(s.std, 1)

                def normalise(i):
                    r = ROWS[i]
                    act.wait_ge(s.rs, i + 1)
                    nc.scalar.activation(rows[i], rows[i], ACT.Identity, scale=rs[0:r, i:i + 1],
                                         bias=shift[0:r, i:i + 1]).then_inc(s.norm, 1)

                deviation(0)
                deviation(1)
                normalise(0)
                normalise(1)
                deviation(2)
                normalise(2)
                if q_in is not None:
                    act.wait_ge(s.ahead, 16)
                    nc.scalar.activation(q_hi[:], q_in[:], ACT.Copy, scale=W_SCALE)
                emit_transpose_copies(act, s, (6, 7))

    def sgu(j, layer):
        w_in, w_out = io["sgu_w_in"][j], io["sgu_w_out"][j]
        with ExitStack() as ctx:
            u_T = sb("u_T", [128, KT, T], ctx=ctx)
            v = sb("v", [128, 3, D], ctx=ctx)
            b_col = sb("b_col", [128, 16], ctx=ctx)
            b_row = sb("b_row", [1, 2 * D], ctx=ctx)
            w_m = sb("w_m", [128, 4, 128], ctx=ctx)
            w_ms = sb("w_ms", [SAMPLE, 4, SAMPLE], ctx=ctx)
            b_s = sb("b_s", [1, 4, T], ctx=ctx)
            vg = sb("vg", [128, D], ctx=ctx)
            vb = sb("vb", [128, D], ctx=ctx)
            def load(sp, s):
                sp.dma_start(b_col[:], io["sgu_b_col"][j]).then_inc(s.bias, 16)
                sp.dma_start(b_row[:], io["sgu_b_in"][j:j + 1, :]).then_inc(s.bias, 16)
                for dst, src in ((w_m[:], io["sgu_w_sT"][j].rearrange("g s t -> s g t")),
                                 (vg[:], io["sgu_v_g"][j:j + 1, :].partition_broadcast(128)),
                                 (vb[:], io["sgu_v_b"][j:j + 1, :].partition_broadcast(128))):
                    sp.dma_start(dst, src).then_inc(s.loaded, 16)
                for q in range(2):
                    sp.dma_start(b_s[:, :, 128 * q:128 * q + 128], io["sgu_b_s"][j:j + 1, :, :]
                                 ).then_inc(s.loaded, 16)
                for b in range(NB):
                    sp.dma_start(b_s[:, :, PROMPT + LS * b:PROMPT + LS * b + LS],
                                 io["sgu_b_s"][j:j + 1, :, 0:LS]).then_inc(s.loaded, 16)
                sp.wait_ge(s.zero, 1)
                for b in range(NB):
                    c = slice(LS * b, LS * b + LS)
                    sp.dma_start(w_ms[c, :, c], io["sgu_w_sT"][j].rearrange("g s t -> s g t")[0:LS, :, 0:LS]
                                 ).then_inc(s.spread, 16)

            def mask(pool, s):
                nc.gpsimd.memset(w_ms[:], 0.0).then_inc(s.zero, 1)
                pool.wait_ge(s.loaded, 16 * 13)
                nc.gpsimd.affine_select(out=w_m[:], in_=w_m[:], compare_op=ALU.is_ge, fill=0.0, base=0,
                                        pattern=[[0, 4], [1, 128]], channel_multiplier=-1)
                pool.wait_ge(s.spread, 16 * NB)
                nc.gpsimd.affine_select(out=w_ms[:], in_=w_ms[:], compare_op=ALU.is_ge, fill=0.0, base=0,
                                        pattern=[[0, 4], [1, SAMPLE]], channel_multiplier=-1)

            jobs = [job(GROUP * g, "feature", lambda f, g=g: u_T[:, 4 * g + f, :], ACT.Gelu_apprx_tanh,
                        b_col[:, 4 * g:4 * g + 4]) for g in range(2)]
            jobs += [job(D + GROUP * g, "token", lambda i, g=g: v[0:ROWS[i], i, GROUP * g:GROUP * g + GROUP],
                         ACT.Gelu_apprx_tanh, b_row[:, D + GROUP * g:D + GROUP * g + GROUP]) for g in range(2)]
            project_in(w_in, jobs, Side(("bias", "loaded", "zero", "spread"), load, mask, 32))

            with phase("step", "var", "std", "gain", "ready", "mix", "mix_used", "stored") as (block, s):
                st = sb("st", [128, 3, 2, 6], ctx=ctx)
                mv = sb("mv", [128, 3, 2], ctx=ctx)
                sd = sb("sd", [128, 3], ctx=ctx)
                rs = sb("rs", [128, 3], ctx=ctx)

                @block.vector
                def _(dve):
                    link = linker(dve, s.step)
                    for i, (t0, r) in enumerate(TILES):
                        nc.vector.bn_stats(out=st[0:r, i, 0, :], in_=v[0:r, i, 0:512])
                        link(nc.vector.bn_stats(out=st[0:r, i, 1, :], in_=v[0:r, i, 512:1024]))
                        nc.vector.bn_aggr(out=mv[0:r, i, :], in_=st[0:r, i, :, :].rearrange("p a b -> p (a b)")
                                          ).then_inc(s.var, 1)
                    for i, (t0, r) in enumerate(TILES):
                        row = v[0:r, i, :]
                        dve.wait_ge(s.var, 3)
                        dve.wait_ge(s.std, i + 1)
                        link(nc.vector.reciprocal(rs[0:r, i:i + 1], sd[0:r, i:i + 1]))
                        link(nc.vector.tensor_scalar(row, row, mv[0:r, i, 0:1], rs[0:r, i:i + 1],
                                                     ALU.subtract, ALU.mult))
                        nc.vector.tensor_tensor(row, row, vg[0:r, :], ALU.mult).then_inc(s.gain, 1)
                    for f in range(KT):
                        dve.wait_ge(s.mix, f + 1)
                        nc.vector.tensor_tensor(u_T[:, f, :], u_T[:, f, :], ps[:, f % 6, 0:T], ALU.mult
                                                ).then_inc(s.mix_used, 1)

                @block.gpsimd
                def _(pool):
                    for i, (t0, r) in enumerate(TILES):
                        pool.wait_ge(s.gain, i + 1)
                        nc.gpsimd.tensor_tensor(v[0:r, i, :], v[0:r, i, :], vb[0:r, :], ALU.add
                                                ).then_inc(s.ready, 1)

                @block.scalar
                def _(act):
                    for i, (t0, r) in enumerate(TILES):
                        act.wait_ge(s.var, i + 1)
                        nc.scalar.activation(sd[0:r, i:i + 1], mv[0:r, i, 1:2], ACT.Sqrt, bias=eps[0:r, :]
                                             ).then_inc(s.std, 1)

                @block.tensor
                def _(pe):
                    pe.wait_ge(s.ready, 3)
                    for f in range(KT):
                        if f >= 6:
                            pe.wait_ge(s.mix_used, f - 5)
                        for i, (t0, r) in enumerate(TILES):
                            w = w_m[:, f // 2, :] if i < 2 else w_ms[:, f // 2, :]
                            nc.tensor.matmul(ps[:, f % 6, t0:t0 + r], v[0:r, i, 128 * f:128 * f + 128], w,
                                             start=(i == 0), stop=False, skip_group_check=True)
                        last = nc.tensor.matmul(ps[:, f % 6, 0:T], ones[:], b_s[:, f // 2, :], start=False,
                                                stop=True, skip_group_check=True)
                        last.then_inc(s.mix, 1)

                @block.sync
                def _(sp):
                    sp.wait_ge(s.ready, 3)
                    sp.dma_start(out[6][j].rearrange("b l d -> (b l) d"), v[0:SAMPLE, 2, :]).then_inc(s.stored, 16)
                    sp.wait_ge(s.stored, 16)

            project_out(w_out, u_T, KT)

    def recurrent(kd, width, chunks, att, qc, qm, kp, km, dec, v, gate_T, gain, centre, state_in, state_out_p,
                  state_out_s):
        nchunk = len(chunks)
        units = []
        for h in range(H):
            units += [(h, "p", c, k) for c in range(nchunk) for k in range(kd)]
            units += [(h, "s", b, k) for b in range(NB) for k in range(kd)]
        at = {u: n for n, u in enumerate(units)}
        et = width // 128
        S0, S1 = 3, 3
        with ExitStack() as ctx, phase("in0", "in1", "in2", "o0", "o1", "o2", "p_out", "kv", "state",
                                       "heads", "step", "var", "std", "norm", "tp", "tp_used") as (block, s):
            st_p = sb("st_p", [128, 2, kd, width], ctx=ctx)
            s_in = sb("s_in", [128, S0, kd, width], ctx=ctx)
            s_new = sb("s_new", [128, S1, kd, width], ctx=ctx)
            o_n = sb("o_n", [128, 3, width], ctx=ctx)
            bst = sb("bst", [128, 3, 6], ctx=ctx)
            mv = sb("mv", [128, H, 3, 2], ctx=ctx)
            ms = sb("ms", [128, H, 3], ctx=ctx)
            sd = sb("sd", [128, H, 3], ctx=ctx)
            rs = sb("rs", [128, H, 3], ctx=ctx)
            sin = (s.in0, s.in1, s.in2)
            sout = (s.o0, s.o1, s.o2)
            KV, TP = (3, 4), (5, 6)

            @block.sync
            def _(sp):
                def load(n):
                    h, b = divmod(n, NB)
                    sp.dma_start(s_in[:, n % S0], state_in[b, h].rearrange("(k p) e -> p k e", p=128)
                                 ).then_inc(sin[n % S0], 16)
                for n in range(S0):
                    load(n)
                for h in range(H):
                    sp.wait_ge(s.state, at[(h, "p", nchunk - 1, kd - 1)] + 1)
                    sp.dma_start(state_out_p[0, h].rearrange("(k p) e -> p k e", p=128),
                                 st_p[:, (nchunk - 1) % 2]).then_inc(s.p_out, 16)
                    for b in range(NB):
                        n = h * NB + b
                        sp.wait_ge(s.state, at[(h, "s", b, kd - 1)] + 1)
                        sp.dma_start(state_out_s[b, h].rearrange("(k p) e -> p k e", p=128), s_new[:, n % S1]
                                     ).then_inc(sout[n % S1], 16)
                        if n + S0 < H * NB:
                            load(n + S0)
                sp.wait_ge(s.p_out, 16 * H)
                for m, q in enumerate(sout):
                    sp.wait_ge(q, 16 * len(range(m, H * NB, S1)))

            @block.tensor
            def _(pe):
                def update(u, lhs, rhs):
                    n = at[u]
                    if n >= 2:
                        pe.wait_ge(s.state, n - 1)
                    nc.tensor.matmul(ps[:, KV[n % 2], 0:width], lhs, rhs, start=True, stop=True).then_inc(s.kv, 1)

                def turn(h):
                    pe.wait_ge(s.norm, 3 * (h + 1))
                    for f in range(et):
                        n = h * et + f
                        if n >= 2:
                            pe.wait_ge(s.tp_used, n - 1)
                        for i, (t0, r) in enumerate(TILES):
                            last = nc.tensor.transpose(ps[:, TP[n % 2], t0:t0 + r],
                                                       o_n[0:r, i, 128 * f:128 * f + 128], ident[0:r, 0:r])
                        last.then_inc(s.tp, 1)

                for h in range(H):
                    ve = slice(h * width, (h + 1) * width)
                    if h:
                        turn(h - 1)
                    for i in range(2):
                        mine = [c for c in range(nchunk) if chunks[c][0] == i]
                        crossing = [c for c in mine if c > 0]
                        nc.tensor.matmul(ps[:, i, 0:width], att[:, h, i, :], v[:, i, ve], start=True,
                                         stop=not crossing)
                        for c in mine:
                            lo, hi = chunks[c][1:]
                            if c > 0:
                                pe.wait_ge(s.state, at[(h, "p", c - 1, kd - 1)] + 1)
                                for k in range(kd):
                                    nc.tensor.matmul(ps[:, i, 0:width], qc[:, h, k, c - 1, :],
                                                     st_p[:, (c - 1) % 2, k, :], start=False,
                                                     stop=(c == crossing[-1] and k == kd - 1))
                            for k in range(kd):
                                update((h, "p", c, k), kp[lo:hi, i, h, 128 * k:128 * k + 128], v[lo:hi, i, ve])
                    nc.tensor.matmul(ps[0:SAMPLE, 2, 0:width], att[0:SAMPLE, h, 2, 0:SAMPLE], v[0:SAMPLE, 2, ve],
                                     start=True, stop=False)
                    for b in range(NB):
                        n = h * NB + b
                        pe.wait_ge(sin[n % S0], 16 * (n // S0 + 1))
                        for k in range(kd):
                            last = nc.tensor.matmul(ps[0:SAMPLE, 2, 0:width], qm[:, h, k, b, :],
                                                    s_in[:, n % S0, k, :], start=False,
                                                    stop=(b == NB - 1 and k == kd - 1))
                        if b == NB - 1:
                            last.then_inc(s.heads, 1)
                        for k in range(kd):
                            update((h, "s", b, k), km[:, b, h, 128 * k:128 * k + 128], v[0:SAMPLE, 2, ve])
                turn(H - 1)

            @block.vector
            def _(dve):
                link = linker(dve, s.step)
                for h in range(H):
                    for c in range(nchunk):
                        for k in range(kd):
                            n = at[(h, "p", c, k)]
                            dve.wait_ge(s.kv, n + 1)
                            if c == (nchunk - 1) % 2 and h and k == 0:
                                dve.wait_ge(s.p_out, 16 * h)
                            dst = st_p[:, c % 2, k, :]
                            if c == 0:
                                nc.vector.tensor_copy(dst, ps[:, KV[n % 2], 0:width]).then_inc(s.state, 1)
                            else:
                                dve.wait_ge(s.state, at[(h, "p", c - 1, k)] + 1)
                                nc.vector.scalar_tensor_tensor(out=dst, in0=st_p[:, (c - 1) % 2, k, :],
                                                               scalar=dec[:, h, c:c + 1],
                                                               in1=ps[:, KV[n % 2], 0:width], op0=ALU.mult,
                                                               op1=ALU.add).then_inc(s.state, 1)
                    for b in range(NB):
                        m = h * NB + b
                        dve.wait_ge(sin[m % S0], 16 * (m // S0 + 1))
                        if m >= S1:
                            dve.wait_ge(sout[m % S1], 16 * (m // S1))
                        for k in range(kd):
                            n = at[(h, "s", b, k)]
                            dve.wait_ge(s.kv, n + 1)
                            nc.vector.scalar_tensor_tensor(out=s_new[:, m % S1, k, :], in0=s_in[:, m % S0, k, :],
                                                           scalar=dec[:, h, nchunk + b:nchunk + b + 1],
                                                           in1=ps[:, KV[n % 2], 0:width], op0=ALU.mult,
                                                           op1=ALU.add).then_inc(s.state, 1)
                    dve.wait_ge(s.heads, h + 1)
                    for i, (t0, r) in enumerate(TILES):
                        link(nc.vector.bn_stats(out=bst[0:r, i, :], in_=ps[0:r, i, 0:width]))
                        link(nc.vector.bn_aggr(out=mv[0:r, h, i, :], in_=bst[0:r, i, :]))
                        if centre:
                            ins = nc.vector.tensor_copy(ms[0:r, h, i:i + 1], mv[0:r, h, i, 1:2])
                        else:
                            ins = nc.vector.scalar_tensor_tensor(out=ms[0:r, h, i:i + 1], in0=mv[0:r, h, i, 0:1],
                                                                 scalar=mv[0:r, h, i, 0:1], in1=mv[0:r, h, i, 1:2],
                                                                 op0=ALU.mult, op1=ALU.add)
                        ins.then_inc(s.var, 1)
                    if h:
                        dve.wait_ge(s.tp, h * et)
                    for i, (t0, r) in enumerate(TILES):
                        dve.wait_ge(s.std, 3 * h + i + 1)
                        link(nc.vector.reciprocal(rs[0:r, h, i:i + 1], sd[0:r, h, i:i + 1]))
                        if centre:
                            ins = nc.vector.tensor_scalar(o_n[0:r, i, :], ps[0:r, i, 0:width], mv[0:r, h, i, 0:1],
                                                          rs[0:r, h, i:i + 1], ALU.subtract, ALU.mult)
                        else:
                            ins = nc.vector.tensor_scalar(o_n[0:r, i, :], ps[0:r, i, 0:width],
                                                          rs[0:r, h, i:i + 1], None, ALU.mult)
                        ins.then_inc(s.norm, 1)
                    for f in range(et):
                        n = h * et + f
                        dve.wait_ge(s.tp, n + 1)
                        nc.vector.scalar_tensor_tensor(out=gate_T[:, n, :], in0=ps[:, TP[n % 2], 0:T],
                                                       scalar=gain[:, n:n + 1], in1=gate_T[:, n, :], op0=ALU.mult,
                                                       op1=ALU.mult).then_inc(s.tp_used, 1)

            @block.scalar
            def _(act):
                for h in range(H):
                    for i, (t0, r) in enumerate(TILES):
                        act.wait_ge(s.var, 3 * h + i + 1)
                        nc.scalar.activation(sd[0:r, h, i:i + 1], ms[0:r, h, i:i + 1], ACT.Sqrt, bias=eps[0:r, :]
                                             ).then_inc(s.std, 1)

    def retention(j, layer):
        with ExitStack() as cg:
            g_T = sb("g_T", [128, 16, T], ctx=cg)
            with ExitStack() as ctx:
                v = sb("v", [128, 3, 2048], ctx=ctx)
                q_T = sb("q_T", [128, H, 2, T], ctx=ctx)
                k_T = sb("k_T", [128, H, 2, T], ctx=ctx)
                jobs = [job(GROUP * g, "feature",
                            lambda f, g=g: (q_T if g < 2 else k_T)[:, (4 * g + f) % 8 // 2, f % 2, :])
                        for g in range(4)]
                jobs += [job(2048 + GROUP * g, "token", lambda i, g=g: v[0:ROWS[i], i, GROUP * g:GROUP * g + GROUP])
                         for g in range(4)]
                jobs += [job(4096 + GROUP * g, "feature", lambda f, g=g: g_T[:, 4 * g + f, :], ACT.Silu)
                         for g in range(4)]
                project_in(io["ret_w_in"][j], jobs)

                att = sb("att", [128, H, 3, 128], ctx=ctx)
                qc = sb("qc", [128, H, 2, 1, 128], ctx=ctx)
                qm = sb("qm", [128, H, 2, NB, SAMPLE], ctx=ctx)
                kp = sb("kp", [128, 2, H, 256], ctx=ctx)
                dec = sb("dec", [128, H, 2 + NB], ctx=ctx)
                gain = sb("gain", [128, 16], ctx=ctx)
                km = sb("km", [SAMPLE, NB, H, 256], ctx=ctx)
                with ExitStack() as cq:
                    with phase("loaded", "step", "pstep", "q_rot", "k_rot", "sc", "sc_used", "kt", "kt_used", "qs"
                               ) as (block, s):
                        cos = sb("cos", [128, T], ctx=cq)
                        sin = sb("sin", [128, T], ctx=cq)
                        cross = sb("cross", [128, H, T], ctx=cq)
                        decay = sb("decay", [128, H, 128], ctx=cq)
                        decay_s = sb("decay_s", [SAMPLE, H, SAMPLE], ctx=cq)
                        keep = sb("keep", [128, 3, H], ctx=cq)
                        keep_s = sb("keep_s", [SAMPLE, NB, H], ctx=cq)
                        memcol = sb("memcol", [128, NB, SAMPLE], ctx=cq)
                        tmp_q = sb("tmp_q", [128, 2, H, T], ctx=cq)
                        tmp_k = sb("tmp_k", [128, 2, H, T], ctx=cq)
                        n_load = 10

                        @block.sync
                        def _(sp):
                            for dst, src in ((cos, "c_cos"), (sin, "c_sin"), (cross, "c_cross"), (decay, "c_decay"),
                                             (decay_s, "c_decay_s"), (keep, "c_kd"), (keep_s, "c_kdm"),
                                             (memcol, "c_memcol"), (dec, "c_dec")):
                                sp.dma_start(dst[:], io[src]).then_inc(s.loaded, 16)
                            sp.dma_start(gain[:], io["ret_gain"][j]).then_inc(s.loaded, 16)

                        def rotate(tt, link, a, tmp):
                            a0, a1 = a[:, :, 0, :], a[:, :, 1, :]
                            c = cos[:].rearrange("p (o t) -> p o t", o=1).to_broadcast([128, H, T])
                            n = sin[:].rearrange("p (o t) -> p o t", o=1).to_broadcast([128, H, T])
                            tt(tmp[:, 0], a1, n, ALU.mult)
                            link(tt(tmp[:, 1], a0, n, ALU.mult))
                            tt(a0, a0, c, ALU.mult)
                            link(tt(a1, a1, c, ALU.mult))
                            tt(a0, a0, tmp[:, 0], ALU.subtract)
                            return tt(a1, a1, tmp[:, 1], ALU.add)

                        @block.vector
                        def _(dve):
                            link = linker(dve, s.step)
                            dve.wait_ge(s.loaded, 16 * n_load)
                            rotate(nc.vector.tensor_tensor, link, q_T, tmp_q).then_inc(s.q_rot, 1)
                            dve.wait_ge(s.q_rot, 1)
                            for k in range(2):
                                nc.vector.tensor_tensor(qc[:, :, k, 0, :], q_T[:, :, k, 128:256], cross[:, :, 128:256],
                                                        ALU.mult)
                                nc.vector.tensor_tensor(tmp_q[:, k, :, 0:SAMPLE], q_T[:, :, k, PROMPT:T],
                                                        cross[:, :, PROMPT:T], ALU.mult).then_inc(s.qs, 1)
                            dve.wait_ge(s.qs, 2)
                            for h in range(H):
                                for k in range(2):
                                    nc.vector.tensor_tensor(
                                        qm[:, h, k, :, :],
                                        tmp_q[:, k, h, 0:SAMPLE].rearrange("p (o t) -> p o t", o=1)
                                        .to_broadcast([128, NB, SAMPLE]), memcol[:], ALU.mult)
                            for h in range(H):
                                for i in range(3):
                                    r = ROWS[i]
                                    n = 3 * h + i
                                    dve.wait_ge(s.sc, n + 1)
                                    nc.vector.tensor_tensor(att[0:r, h, i, 0:r], ps[0:r, n % 2, 0:r],
                                                            (decay if i < 2 else decay_s)[:, h, :], ALU.mult
                                                            ).then_inc(s.sc_used, 1)
                            for i in range(3):
                                r = ROWS[i]
                                for q in range(2):
                                    n = 2 * i + q
                                    dve.wait_ge(s.kt, n + 1)
                                    for e in range(2):
                                        h = 2 * q + e
                                        src = ps[0:r, 2 + n % 2, 256 * e:256 * e + 256]
                                        if i < 2:
                                            last = nc.vector.tensor_scalar(kp[:, i, h, :], src, keep[:, i, h:h + 1],
                                                                           None, ALU.mult)
                                        else:
                                            for b in range(NB):
                                                last = nc.vector.tensor_scalar(km[:, b, h, :], src,
                                                                               keep_s[:, b, h:h + 1], None, ALU.mult)
                                    last.then_inc(s.kt_used, 1)

                        @block.gpsimd
                        def _(pool):
                            link = linker(pool, s.pstep)
                            pool.wait_ge(s.loaded, 16 * n_load)
                            rotate(nc.gpsimd.tensor_tensor, link, k_T, tmp_k).then_inc(s.k_rot, 1)

                        @block.tensor
                        def _(pe):
                            pe.wait_ge(s.q_rot, 1)
                            pe.wait_ge(s.k_rot, 1)
                            for h in range(H):
                                for i, (t0, r) in enumerate(TILES):
                                    n = 3 * h + i
                                    if n >= 2:
                                        pe.wait_ge(s.sc_used, n - 1)
                                    for k in range(2):
                                        last = nc.tensor.matmul(ps[0:r, n % 2, 0:r], k_T[:, h, k, t0:t0 + r],
                                                                q_T[:, h, k, t0:t0 + r], start=(k == 0), stop=(k == 1))
                                    last.then_inc(s.sc, 1)
                            for i, (t0, r) in enumerate(TILES):
                                for q in range(2):
                                    n = 2 * i + q
                                    if n >= 2:
                                        pe.wait_ge(s.kt_used, n - 1)
                                    for e in range(4):
                                        last = nc.tensor.transpose(ps[0:r, 2 + n % 2, 128 * e:128 * e + 128],
                                                                   k_T[:, 2 * q + e // 2, e % 2, t0:t0 + r], ident[:])
                                    last.then_inc(s.kt, 1)
                recurrent(2, 512, [(0, 0, 128), (1, 0, 128)], att, qc, qm, kp, km, dec, v, g_T, gain, True,
                          io["state_ret"][j], out[2][j], out[3][j])
            project_out(io["ret_w_out"][j], g_T, 16)

    def gla(j, layer):
        with ExitStack() as cg:
            g_T = sb("g_T", [128, 8, T], ctx=cg)
            with ExitStack() as ctx:
                v = sb("v", [128, 3, D], ctx=ctx)
                att = sb("att", [128, H, 3, 128], ctx=ctx)
                qc = sb("qc", [128, H, 1, 3, 128], ctx=ctx)
                qm = sb("qm", [128, H, 1, NB, SAMPLE], ctx=ctx)
                kp = sb("kp", [128, 2, H, 128], ctx=ctx)
                km = sb("km", [SAMPLE, NB, H, 128], ctx=ctx)
                dec = sb("dec", [128, H, 4 + NB], ctx=ctx)
                gain = sb("gain", [128, 8], ctx=ctx)
                with ExitStack() as cq:
                    q_T = sb("q_T", [128, H, T], ctx=cq)
                    k_T = sb("k_T", [128, H, T], ctx=cq)
                    a_T = sb("a_T", [16, T], ctx=cq)
                    jobs = [job(0, "feature", lambda f: q_T[:, f, :], scale=128 ** -0.5),
                            job(GROUP, "feature", lambda f: k_T[:, f, :])]
                    jobs += [job(1024 + GROUP * g, "token", lambda i, g=g: v[0:ROWS[i], i, GROUP * g:GROUP * g + GROUP])
                             for g in range(2)]
                    jobs += [job(2048 + GROUP * g, "feature", lambda f, g=g: g_T[:, 4 * g + f, :], ACT.Silu)
                             for g in range(2)]
                    jobs += [job(3072, "feature", lambda f: a_T[:], width=16)]
                    project_in(io["gla_w_in"][j], jobs)

                    with phase("loaded", "step", "z", "z_sb", "az", "ez", "l1", "cum", "dif", "mag", "ex", "lev", "sc",
                               "sc_used", "kt", "kt_used", "kdec", "zero") as (block, s):
                        w_a2 = sb("w_a2", [16, 512], ctx=cq)
                        b_a = sb("b_a", [128, H], ctx=cq)
                        start = sb("start", [128, T], ctx=cq)
                        levels = sb("levels", [128, LEVELS, 128], ctx=cq)
                        memcol = sb("memcol", [128, NB, SAMPLE], ctx=cq)
                        member = sb("member", [SAMPLE, NB], ctx=cq)
                        z = sb("z", [128, H, T], ctx=cq)
                        az = sb("az", [128, H, T], ctx=cq)
                        cum = sb("cum", [128, H, T], ctx=cq)
                        dif = sb("dif", [128, 2, H, T], ctx=cq)
                        ex = sb("ex", [128, 2, H, T], ctx=cq)
                        ql = sb("ql", [128, 2, H, T], ctx=cq)
                        kl = sb("kl", [128, 2, H, T], ctx=cq)
                        tmp = sb("tmp", [128, H, 128], ctx=cq)
                        last_b = sb("last_b", [128, H, 4 + NB], ctx=cq)
                        units = [(lv, i) for lv in range(LEVELS) for i in range(3) if i < 2 or lv <= 3]

                        @block.sync
                        def _(sp):
                            for dst, src in ((w_a2, io["gla_w_a2"][j]), (b_a, io["gla_b_col"][j]), (start, io["c_start"]),
                                             (levels, io["c_levels"]), (memcol, io["c_memcol"]),
                                             (member, io["c_member"]), (gain, io["gla_gain"][j])):
                                sp.dma_start(dst[:], src).then_inc(s.loaded, 16)

                        @block.tensor
                        def _(pe):
                            pe.wait_ge(s.loaded, 16 * 7)
                            for h in range(H):
                                nc.tensor.matmul(ps[:, h, 0:T], w_a2[:, 128 * h:128 * h + 128], a_T[:], start=True,
                                                 stop=True).then_inc(s.z, 1)
                            pe.wait_ge(s.z_sb, H)
                            for n, (lv, i) in enumerate(units):
                                t0, r = TILES[i]
                                pe.wait_ge(s.lev, lv + 1)
                                if n >= 4:
                                    pe.wait_ge(s.sc_used, n - 3)
                                q, k = (q_T, k_T) if lv == 0 else (ql[:, lv % 2], kl[:, lv % 2])
                                for h in range(H):
                                    last = nc.tensor.matmul(ps[0:r, 2 + n % 4, 128 * h:128 * h + r], k[:, h, t0:t0 + r],
                                                            q[:, h, t0:t0 + r], start=True, stop=True)
                                last.then_inc(s.sc, 1)
                            pe.wait_ge(s.kdec, 1)
                            for i, (t0, r) in enumerate(TILES):
                                if i >= 2:
                                    pe.wait_ge(s.kt_used, 1)
                                for h in range(H):
                                    last = nc.tensor.transpose(ps[0:r, 6 + i % 2, 128 * h:128 * h + 128],
                                                               az[:, h, t0:t0 + r], ident[:])
                                last.then_inc(s.kt, 1)

                        @block.scalar
                        def _(act):
                            for h in range(H):
                                act.wait_ge(s.z, h + 1)
                                nc.scalar.activation(z[:, h, :], ps[:, h, 0:T], ACT.Identity, bias=b_a[:, h:h + 1]
                                                     ).then_inc(s.z_sb, 1)
                            act.wait_ge(s.z_sb, H)
                            nc.scalar.activation(az[:], z[:], ACT.Abs).then_inc(s.az, 1)
                            act.wait_ge(s.az, 1)
                            nc.scalar.activation(ex[:, 0], az[:], ACT.Exp, scale=-1.0).then_inc(s.ez, 1)
                            act.wait_ge(s.ez, 1)
                            nc.scalar.activation(dif[:, 0], ex[:, 0], ACT.Ln, bias=1.0).then_inc(s.l1, 1)
                            for lv in range(1, LEVELS):
                                p = lv % 2
                                act.wait_ge(s.dif, lv)
                                nc.scalar.activation(dif[:, p], dif[:, p], ACT.Abs).then_inc(s.mag, 1)
                                act.wait_ge(s.mag, lv)
                                if lv > 2:
                                    act.wait_ge(s.lev, lv - 1)
                                nc.scalar.activation(ex[:, p], dif[:, p], ACT.Exp, scale=-1.0 / 16).then_inc(s.ex, 1)
                            p = LEVELS % 2
                            act.wait_ge(s.dif, LEVELS)
                            act.wait_ge(s.lev, LEVELS - 1)
                            nc.scalar.activation(ex[:, p], dif[:, p], ACT.Exp, scale=-1.0 / 16).then_inc(s.ex, 1)
                            act.wait_ge(s.ex, LEVELS - 1)
                            nc.scalar.activation(dif[:, 1 - p], cum[:], ACT.Exp, scale=1.0 / 16).then_inc(s.ex, 1)
                            nc.scalar.activation(dec[:], last_b[:], ACT.Exp, scale=1.0 / 16)

                        @block.gpsimd
                        def _(pool):
                            nc.gpsimd.memset(qc[:], 0.0).then_inc(s.zero, 1)

                        @block.vector
                        def _(dve):
                            link = linker(dve, s.step)
                            dve.wait_ge(s.z_sb, H)
                            dve.wait_ge(s.az, 1)
                            link(nc.vector.tensor_scalar_min(z[:], z[:], 0.0))
                            dve.wait_ge(s.l1, 1)
                            link(nc.vector.tensor_tensor(z[:], z[:], dif[:, 0], ALU.subtract))
                            for h in range(H):
                                nc.vector.tensor_tensor_scan(cum[:, h, :], start[:], z[:, h, :], 0.0, ALU.mult, ALU.add
                                                             ).then_inc(s.cum, 1)
                            dve.wait_ge(s.cum, H)
                            nc.vector.tensor_copy(last_b[:, :, 0:4], cum[:, :, 63:PROMPT:64])
                            nc.vector.tensor_copy(last_b[:, :, 4:4 + NB], cum[:, :, PROMPT + LS - 1:T:LS]
                                                  ).then_inc(s.lev, 1)

                            def spread(lv):
                                size = 2 ** lv
                                a = cum[:].rearrange("p h (n c) -> p (h n) c", c=size)
                                o = dif[:, lv % 2].rearrange("p h (n c) -> p (h n) c", c=size)
                                mid = a[:, :, size // 2 - 1:size // 2].to_broadcast([128, H * T // size, size])
                                nc.vector.tensor_tensor(o, a, mid, ALU.subtract).then_inc(s.dif, 1)

                            def spread_last():
                                o = dif[:, LEVELS % 2]
                                for c in range(4):
                                    cc = slice(64 * c, 64 * c + 64)
                                    nc.vector.tensor_tensor(o[:, :, cc], cum[:, :, cc],
                                                            cum[:, :, 64 * c + 63:64 * c + 64]
                                                            .to_broadcast([128, H, 64]), ALU.subtract)
                                for h in range(H):
                                    a = cum[:, h, PROMPT:T].rearrange("p (n c) -> p n c", c=LS)
                                    ins = nc.vector.tensor_tensor(o[:, h, PROMPT:T].rearrange("p (n c) -> p n c", c=LS),
                                                                  a, a[:, :, LS - 1:LS].to_broadcast([128, NB, LS]),
                                                                  ALU.subtract)
                                ins.then_inc(s.dif, 1)

                            def gather(lv):
                                for n, (l2, i) in enumerate(units):
                                    if l2 != lv:
                                        continue
                                    t0, r = TILES[i]
                                    dve.wait_ge(s.sc, n + 1)
                                    src = ps[0:r, 2 + n % 4, :].rearrange("p (h t) -> p h t", h=H)[:, :, 0:r]
                                    mask = levels[0:r, lv:lv + 1, 0:r].to_broadcast([r, H, r])
                                    if lv == 0:
                                        nc.vector.tensor_tensor(att[0:r, :, i, 0:r], src, mask, ALU.mult
                                                                ).then_inc(s.sc_used, 1)
                                    else:
                                        nc.vector.tensor_tensor(tmp[0:r, :, 0:r], src, mask, ALU.mult
                                                                ).then_inc(s.sc_used, 1)
                                        dve.wait_ge(s.sc_used, n + 1)
                                        link(nc.vector.tensor_tensor(att[0:r, :, i, 0:r], att[0:r, :, i, 0:r],
                                                                     tmp[0:r, :, 0:r], ALU.add))

                            spread(1)
                            for lv in range(1, LEVELS):
                                if lv > 1:
                                    dve.wait_ge(s.ex, lv - 1)
                                if lv + 1 < LEVELS:
                                    spread(lv + 1)
                                else:
                                    spread_last()
                                dve.wait_ge(s.ex, lv)
                                nc.vector.tensor_tensor(ql[:, lv % 2], q_T[:], ex[:, lv % 2], ALU.mult)
                                nc.vector.tensor_tensor(kl[:, lv % 2], k_T[:], ex[:, lv % 2], ALU.mult
                                                        ).then_inc(s.lev, 1)
                                gather(lv - 1)
                            dve.wait_ge(s.ex, LEVELS)
                            nc.vector.tensor_tensor(az[:], k_T[:], ex[:, LEVELS % 2], ALU.mult).then_inc(s.kdec, 1)
                            gather(LEVELS - 1)
                            dve.wait_ge(s.ex, LEVELS + 1)
                            link(nc.vector.tensor_tensor(z[:], q_T[:], dif[:, 1 - LEVELS % 2], ALU.mult))
                            dve.wait_ge(s.zero, 1)
                            for c in range(1, 4):
                                o = 64 * (c % 2)
                                nc.vector.tensor_copy(qc[:, :, 0, c - 1, o:o + 64], z[:, :, 64 * c:64 * c + 64])
                            for h in range(H):
                                nc.vector.tensor_tensor(
                                    qm[:, h, 0, :, :], z[:, h, PROMPT:T].rearrange("p (o t) -> p o t", o=1)
                                    .to_broadcast([128, NB, SAMPLE]), memcol[:], ALU.mult)
                            for i in range(3):
                                dve.wait_ge(s.kt, i + 1)
                                src = ps[0:ROWS[i], 6 + i % 2, :]
                                if i < 2:
                                    nc.vector.tensor_copy(kp[:, i, :, :], src.rearrange("p (h d) -> p h d", h=H)
                                                          ).then_inc(s.kt_used, 1)
                                else:
                                    for b in range(NB):
                                        nc.vector.tensor_scalar(km[:, b, :, :], src.rearrange("p (h d) -> p h d", h=H),
                                                                member[:, b:b + 1], None, ALU.mult)
                recurrent(1, 256, [(0, 0, 64), (0, 64, 128), (1, 0, 64), (1, 64, 128)], att, qc, qm, kp, km, dec, v, g_T,
                          gain, False, io["state_gla"][j], out[4][j], out[5][j])
            project_out(io["gla_w_out"][j], g_T, 8)

    def peer(layer):
        with ExitStack() as ctx:
            ea_T = sb("ea_T", [128, T], F16, ctx=ctx)
            eb_T = sb("eb_T", [128, T], F16, ctx=ctx)
            gh_T = sb("gh_T", [128, T], F16, ctx=ctx)
            gl_T = sb("gl_T", [128, T], F16, ctx=ctx)
            iota = sb("iota", [128, NK, 2], F16, ctx=ctx)
            u_hi = sb("u_hi", [128, 2, KT, 128], F16, ctx=ctx)
            u_lo = sb("u_lo", [128, 2, KT, 128], F16, ctx=ctx)
            first = sb("first", [128, QUARTER, T], ctx=ctx)
            with ExitStack() as cq:
                q_in = sb("q_in", [128, KT, 2 * NK], ctx=cq)
                q_hi = sb("q_hi", [128, KT, 2 * NK], F16, ctx=cq)
                residual_norm(layer, 0, q_in, q_hi)
                peer_choose(layer, ea_T, eb_T, gh_T, gl_T, iota, u_hi, u_lo, first, q_in, q_hi)
            peer_experts(layer, ea_T, eb_T, gh_T, gl_T, iota, u_hi, u_lo, first)
        with ExitStack() as ctx:
            y_T = sb("y_T", [128, KT, T], ctx=ctx)
            with phase() as (block, s):
                @block.scalar
                def _(act):
                    scale = W_SCALE / (V_SCALE * G_SCALE)
                    nc.scalar.activation(y_T[:, :, 0:PROMPT], ps[:, 0:4, :].rearrange("p a (b t) -> p (a b) t", b=2),
                                         ACT.Copy, scale=scale)
                    nc.scalar.activation(y_T[:, :, PROMPT:T], ps[:, 4, :].rearrange("p (b t) -> p b t", b=KT),
                                         ACT.Copy, scale=scale)
            with phase() as (block, s):
                @block.tensor
                def _(pe):
                    for i, (t0, r) in enumerate(TILES):
                        for f in range(KT):
                            nc.tensor.transpose(ps[0:r, 2 * i + f // 4, 128 * (f % 4):128 * (f % 4) + 128],
                                                y_T[:, f, t0:t0 + r], ident[:])
        residual_norm(layer, 1)

    def peer_choose(layer, ea_T, eb_T, gh_T, gl_T, iota, u_hi, u_lo, first, q_in, q_hi):
        QW = 2 * NK
        FOUR = 4
        RUNS = ((0, 1), (1, 2), (2, 4), (4, UNDER // FOUR))
        SLOTS = 6
        with ExitStack() as ctx, phase("loaded", "w0", "w1", "w_hi", "w_lo0", "w_lo1", "q", "q_used", "u0", "u1",
                                       "u2", "u3", "us",
                                       "uh", "ul", "h", "gelu", "sc", "sc_sb", "free", "step", "picked", "shift", "exp",
                                       "ready", "tp", "tp_used", "hi") as (block, s):
            w_in = sb("w_in", [128, 2, KT, QW], ctx=ctx)
            u_in = sb("u_in", [128, FOUR, KT, 128], ctx=ctx)
            w_hi = sb("w_hi", [128, 2, KT, QW], F16, ctx=ctx)
            w_lo = sb("w_lo", [128, 2, KT, QW], F16, ctx=ctx)
            q_T = sb("q_T", [128, 2 * PH, T], ctx=ctx)
            keys = sb("keys", [128, 2, NK], ctx=ctx)
            sc = sb("sc", [128, SLOTS, 4, NK], ctx=ctx)
            sc2 = sb("sc2", [128, 4, NK], ctx=ctx)
            val = sb("val", [128, 2, 2, PK], ctx=ctx)
            idx = sb("idx", [128, 2, 2, PK], U32, ctx=ctx)
            idf = sb("idf", [128, 2, 2, PK], F16, ctx=ctx)
            cand = sb("cand", [128, 2, PK, PK], ctx=ctx)
            cand2 = sb("cand2", [128, 2, PK, PK], ctx=ctx)
            hot = sb("hot", [128, 2, 2, PK, PK], F16, ctx=ctx)
            keys_no = sb("keys_no", [128, NK], ctx=ctx)
            best = sb("best", [128, 2, PK], ctx=ctx)
            ci = sb("ci", [128, 2, PK], U32, ctx=ctx)
            ij = sb("ij", [128, 2, 2, PK], U32, ctx=ctx)
            ijf = sb("ijf", [128, 2, 2, PK], F16, ctx=ctx)
            pick = sb("pick", [128, 3, 3, PH, PK], ctx=ctx)
            tot = sb("tot", [128, 3, PH], ctx=ctx)
            inv = sb("inv", [128, 3, PH], ctx=ctx)
            gt_T = sb("gt_T", [128, T], ctx=ctx)
            dsts = (ea_T, eb_T, gt_T)
            w_sem, w_lo_sem, u_sem = (s.w0, s.w1), (s.w_lo0, s.w_lo1), (s.u0, s.u1, s.u2, s.u3)
            w_q, u_tab = io["peer_w_q"][layer], io["peer_uT"]
            Q_BANK, S_BANK, TURN, H_BANK = 0, 2, 4, 5

            def in_order(eng, blocks, heads=None, weights=None):
                for g, (lo, hi) in enumerate(RUNS):
                    if heads:
                        heads(g)
                    if lo == 0:
                        blocks(0)
                        lo = 1
                    if hi - 1 > lo:
                        with eng.Fori(lo, hi - 1) as n:
                            blocks(n * FOUR)
                    if hi > lo:
                        blocks(FOUR * (hi - 1))
                    if weights:
                        weights(g)

            def per_row(i):
                return 2 if i < 2 else 1

            def of_tile(i):
                return slice(0, per_row(i) * PH // 2)

            def early(c):
                return isinstance(c, int) and c < 2

            @block.sync
            def _(sp):
                def load_w(hd):
                    if hd > 2:
                        sp.wait_ge(w_lo_sem[hd % 2], hd // 2)
                    sp.dma_start(w_in[:, hd % 2], w_q[:, QW * hd:QW * hd + QW].rearrange("(k p) n -> p k n", p=128)
                                 ).then_inc(w_sem[hd % 2], 16)

                def load_u(c, p):
                    if not (isinstance(c, int) and c < FOUR):
                        sp.wait_ge(s.ul, c - FOUR + 1)
                    sp.dma_start(u_in[:, p], u_tab[bass.ds(c + layer * NK, 1)].rearrange("o p k e -> p (o k) e")
                                 ).then_inc(u_sem[p], 16)

                load_w(1)
                for m, name in enumerate(("peer_keys_aT", "peer_keys_bT")):
                    sp.dma_start(keys[:, m, :], io[name][layer]).then_inc(s.loaded, 16)
                sp.dma_start(keys_no[:], io["c_iota"]).then_inc(s.loaded, 16)
                for c in range(FOUR):
                    load_u(c, c)
                load_w(2)
                load_w(3)

                def weights(g):
                    for hd in (2 * g + 4, 2 * g + 5):
                        if hd < PH:
                            load_w(hd)

                def blocks(c):
                    for p in range(FOUR):
                        if not (isinstance(c, int) and c + FOUR + p >= SPLIT):
                            load_u(c + FOUR + p, p)
                in_order(sp, blocks, weights=weights)

            @block.scalar
            def _(act):
                def split_w(hd):
                    p = hd % 2
                    act.wait_ge(w_sem[p], 16 * ((hd - 1) // 2 + 1))
                    if hd >= 2:
                        act.wait_ge(s.q, 2 * hd - 2)
                    nc.scalar.activation(w_hi[:, p], w_in[:, p], ACT.Copy, scale=W_SCALE).then_inc(s.w_hi, 1)

                def scale_u(c, p):
                    act.wait_ge(u_sem[p], (c - p) * 4 + 16)
                    nc.scalar.activation(u_in[:, p], u_in[:, p], ACT.Copy, scale=U_SCALE).then_inc(s.us, 1)

                def high_u(c, p):
                    act.wait_ge(s.us, c + 1)
                    if not early(c):
                        act.wait_ge(s.h, c - 1)
                    nc.scalar.copy(u_hi[:, p % 2], u_in[:, p]).then_inc(s.uh, 1)

                split_w(1)
                for c in range(2):
                    scale_u(c, c)
                    high_u(c, c)

                def heads(g):
                    more = 2 * g + 2 < PH
                    queries(2 * g)
                    if more:
                        split_w(2 * g + 2)
                    queries(2 * g + 1)
                    scores(g)
                    if more:
                        split_w(2 * g + 3)

                def queries(hd):
                    for n in (2 * hd, 2 * hd + 1):
                        act.wait_ge(s.q, n + 1)
                        nc.scalar.activation(q_T[:, n, :], ps[:, Q_BANK + n % 2, 0:T], ACT.Copy,
                                             scale=1.0 / W_SCALE).then_inc(s.q_used, 1)

                def blocks(c):
                    for p in range(FOUR):
                        if isinstance(c, int) and c + p == UNDER - 1:
                            exponentials()
                        scale_u(c + p + 2, (p + 2) % FOUR)
                        high_u(c + p + 2, (p + 2) % FOUR)
                        act.wait_ge(s.h, c + p + 1)
                        nc.scalar.activation(first[:, bass.ds(c + p, 1), :].rearrange("p o t -> p (o t)"),
                                             ps[:, H_BANK + p % 2, 0:T], ACT.Gelu_apprx_tanh, scale=1.0 / U_SCALE
                                             ).then_inc(s.gelu, 1)

                def scores(g):
                    for i in range(3):
                        m = 3 * g + i
                        act.wait_ge(s.sc, m + 1)
                        if m >= SLOTS:
                            act.wait_ge(s.free, m - SLOTS + 1)
                        n = 2 * per_row(i)
                        nc.scalar.copy(sc[:, m % SLOTS, 0:n],
                                       ps[:, S_BANK + m % 2, 0:NK * n].rearrange("p (e n) -> p e n", e=n)
                                       ).then_inc(s.sc_sb, 1)

                def exponentials():
                    for i in range(3):
                        gate = pick[:, i, 2, of_tile(i)]
                        act.wait_ge(s.shift, 3 * (PH // 2 - 1) + i + 1)
                        nc.scalar.activation(gate, gate, ACT.Exp).then_inc(s.exp, 1)
                in_order(act, blocks, heads)

                for i, (t0, r) in enumerate(TILES):
                    act.wait_ge(s.tp, i + 1)
                    for m in range(3):
                        nc.scalar.copy(dsts[m][:, t0:t0 + r], ps[:, TURN, 128 * m:128 * m + r]).then_inc(s.tp_used, 1)
                act.wait_ge(s.tp_used, 9)
                nc.scalar.copy(gh_T[:], gt_T[:]).then_inc(s.hi, 1)

            @block.gpsimd
            def _(pool):
                def low_u(c, p):
                    pool.wait_ge(s.uh, c + 1)
                    nc.gpsimd.tensor_tensor(u_lo[:, p % 2], u_in[:, p], u_hi[:, p % 2], ALU.subtract
                                            ).then_inc(s.ul, 1)

                low_u(0, 0)
                low_u(1, 1)

                def blocks(c):
                    for p in range(FOUR):
                        low_u(c + p + 2, (p + 2) % FOUR)
                in_order(pool, blocks)

            @block.tensor
            def _(pe):
                def heads(g):
                    queries(g)
                    scores(g)

                def queries(g):
                    for hd in (2 * g, 2 * g + 1):
                        pe.wait_ge(w_lo_sem[hd % 2], hd // 2 + 1)
                        if hd:
                            pe.wait_ge(s.w_hi, hd)
                        high, low = (w_hi[:, hd % 2] if hd else q_hi), w_lo[:, hd % 2]
                        for n in (2 * hd, 2 * hd + 1):
                            if n >= 2:
                                pe.wait_ge(s.q_used, n - 1)
                            at = slice(NK * (n % 2), NK * (n % 2) + NK)
                            for k in range(KT):
                                for e, (ww, xx) in enumerate(((high, x_hi), (high, x_lo), (low, x_hi))):
                                    last = nc.tensor.matmul(ps[:, Q_BANK + n % 2, 0:T], ww[:, k, at],
                                                            xx[:, k, :], start=(k == 0 and e == 0),
                                                            stop=(k == KT - 1 and e == 2))
                            last.then_inc(s.q, 1)

                def blocks(c):
                    for m in range(FOUR):
                        p = m % 2
                        pe.wait_ge(s.uh, c + m + 1)
                        pe.wait_ge(s.ul, c + m + 1)
                        if not early(c + m):
                            pe.wait_ge(s.gelu, c + m - 1)
                        for k in range(KT):
                            dst = ps[:, H_BANK + p, 0:T]
                            nc.tensor.matmul(dst, u_hi[:, p, k, :], x_hi[:, k, :], start=(k == 0), stop=False)
                            nc.tensor.matmul(dst, u_hi[:, p, k, :], x_lo[:, k, :], start=False, stop=False)
                            last = nc.tensor.matmul(dst, u_lo[:, p, k, :], x_hi[:, k, :], start=False,
                                                    stop=(k == KT - 1))
                        last.then_inc(s.h, 1)

                def scores(g):
                    if g == 0:
                        pe.wait_ge(s.loaded, 48)
                    pe.wait_ge(s.q_used, 4 * g + 4)
                    for i, (t0, r) in enumerate(TILES):
                        m = 3 * g + i
                        if m >= 2:
                            pe.wait_ge(s.sc_sb, m - 1)
                        for e in range(4):
                            row, col = (0, NK * e) if i < 2 else (SAMPLE * (e // 2), NK * (e % 2))
                            last = nc.tensor.matmul(ps[row:row + r, S_BANK + m % 2, col:col + NK],
                                                    q_T[:, 4 * g + e, t0:t0 + r], keys[:, e % 2, :], start=True,
                                                    stop=True)
                        last.then_inc(s.sc, 1)
                in_order(pe, blocks, heads)

                for i, (t0, r) in enumerate(TILES):
                    pe.wait_ge(s.ready, i + 1)
                    if i:
                        pe.wait_ge(s.tp_used, 3 * i)
                    for m in range(3):
                        src = pick[:, i, m, of_tile(i)].rearrange("p h k -> p (h k)")
                        if i < 2:
                            last = nc.tensor.transpose(ps[:, TURN, 128 * m:128 * m + r], src, ident[:])
                            continue
                        for o in (0, SAMPLE):
                            at = slice(o, o + SAMPLE)
                            last = nc.tensor.matmul(ps[at, TURN, 128 * m:128 * m + SAMPLE], src[at], ident[at, at],
                                                    start=True, stop=True)
                    last.then_inc(s.tp, 1)

            @block.vector
            def _(dve):
                link = linker(dve, s.step)

                def top16(n, src, scratch, v_of, i_of):
                    for jj in range(n):
                        last = nc.vector.max(out=v_of(jj)[:, 0:8], in_=src(jj))
                    link(last)
                    for jj in range(n):
                        nc.vector.max_index(out=i_of(jj)[:, 0:8], in_max=v_of(jj)[:, 0:8], in_values=src(jj))
                    for jj in range(n):
                        last = nc.vector.match_replace(out=scratch(jj), in_to_replace=v_of(jj)[:, 0:8],
                                                       in_values=src(jj), imm_value=LOWEST)
                    link(last)
                    for jj in range(n):
                        last = nc.vector.max(out=v_of(jj)[:, 8:16], in_=scratch(jj))
                    link(last)
                    for jj in range(n):
                        last = nc.vector.max_index(out=i_of(jj)[:, 8:16], in_max=v_of(jj)[:, 8:16],
                                                   in_values=scratch(jj))
                    link(last)

                def choose(g, i):
                    m, nh = 3 * g + i, per_row(i)
                    heads = slice(nh * g, nh * g + nh)
                    dve.wait_ge(s.sc_sb, m + 1)
                    top16(2 * nh, lambda e: sc[:, m % SLOTS, e, :], lambda e: sc2[:, e, :],
                          lambda e: val[:, e // 2, e % 2, :], lambda e: idx[:, e // 2, e % 2, :])
                    nc.vector.tensor_copy(idf[:, 0:nh], idx[:, 0:nh]).then_inc(s.free, 1)
                    link(nc.vector.tensor_tensor(
                        cand[:, 0:nh], val[:, 0:nh, 0, :].rearrange("p h (k o) -> p h k o", o=1)
                        .to_broadcast([128, nh, PK, PK]), val[:, 0:nh, 1:2, :].to_broadcast([128, nh, PK, PK]),
                        ALU.add))
                    top16(nh, lambda h: cand[:, h].rearrange("p a b -> p (a b)"),
                          lambda h: cand2[:, h].rearrange("p a b -> p (a b)"),
                          lambda h: best[:, h, :], lambda h: ci[:, h, :])
                    nc.vector.tensor_single_scalar(ij[:, 0, 0:nh], ci[:, 0:nh], 4, ALU.logical_shift_right)
                    link(nc.vector.tensor_single_scalar(ij[:, 1, 0:nh], ci[:, 0:nh], PK - 1, ALU.bitwise_and))
                    link(nc.vector.tensor_copy(ijf[:, :, 0:nh], ij[:, :, 0:nh]))
                    nc.vector.tensor_tensor(pick[:, i, 2, heads], best[:, 0:nh],
                                            best[:, 0:nh, 0:1].to_broadcast([128, nh, PK]), ALU.subtract
                                            ).then_inc(s.shift, 1)
                    for n in range(2):
                        rows = [128, nh * PK, PK]
                        last = nc.vector.tensor_tensor(
                            hot[:, n, 0:nh].rearrange("p h a b -> p (h a) b"),
                            ijf[:, n, 0:nh].rearrange("p h (k o) -> p (h k) o", o=1).to_broadcast(rows),
                            iota[:, 0:PK, 0].rearrange("p (o k) -> p o k", o=1).to_broadcast(rows), ALU.is_equal)
                    link(last)
                    for n in range(2):
                        last = nc.vector.tensor_tensor(hot[:, n, 0:nh], hot[:, n, 0:nh],
                                                       idf[:, 0:nh, n:n + 1, :].to_broadcast([128, nh, PK, PK]),
                                                       ALU.mult)
                    link(last)
                    nc.vector.tensor_reduce(pick[:, i, 0:2, heads], hot[:, :, 0:nh], AX, ALU.add
                                            ).then_inc(s.picked, 1)

                def low_w(hd):
                    p = hd % 2
                    if hd:
                        dve.wait_ge(s.w_hi, hd)
                    full, high = (w_in[:, p], w_hi[:, p]) if hd else (q_in[:], q_hi[:])
                    nc.vector.scalar_tensor_tensor(out=w_lo[:, p], in0=full, scalar=W_SCALE, in1=high,
                                                   op0=ALU.mult, op1=ALU.subtract).then_inc(w_lo_sem[p], 1)

                low_w(0)
                low_w(1)
                dve.wait_ge(s.loaded, 48)
                link(nc.vector.tensor_copy(iota[:], keys_no[:].rearrange("p (k o) -> p k o", o=1)
                                           .to_broadcast([128, NK, 2])))
                for g in range(PH // 2):
                    for i in range(3):
                        if i < 2 and 2 * g + 2 < PH:
                            low_w(2 * g + 2 + i)
                        choose(g, i)
                for i in range(3):
                    at = of_tile(i)
                    gate = pick[:, i, 2, at]
                    dve.wait_ge(s.exp, i + 1)
                    link(nc.vector.tensor_reduce(tot[:, i, at], gate, AX, ALU.add))
                    link(nc.vector.reciprocal(inv[:, i, at], tot[:, i, at]))
                    nc.vector.scalar_tensor_tensor(out=gate, in0=gate, scalar=G_SCALE,
                                                   in1=inv[:, i, at].rearrange("p (h o) -> p h o", o=1)
                                                   .to_broadcast([128, at.stop, PK]), op0=ALU.mult, op1=ALU.mult
                                                   ).then_inc(s.ready, 1)
                dve.wait_ge(s.hi, 1)
                nc.vector.tensor_tensor(gl_T[:], gt_T[:], gh_T[:], ALU.subtract)

    def peer_experts(layer, ea_T, eb_T, gh_T, gl_T, iota, u_hi, u_lo, first):
        u_tab, v_tab = io["peer_uT"], io["peer_v"]
        with ExitStack() as ctx, phase("u0", "u1", "v0", "v1", "uh", "ul", "vh", "vl", "h", "gelu", "w", "wh", "wl",
                                       "y", "eq", "rows", "cols", "g", "g_used", "us") as (block, s):
            gates = sb("gates", [128, 2, QUARTER, T], ctx=ctx)
            u_in = sb("u_in", [128, 2, KT, 128], ctx=ctx)
            v_in = sb("v_in", [128, 2, D], ctx=ctx)
            v_hi = sb("v_hi", [128, 2, D], F16, ctx=ctx)
            v_lo = sb("v_lo", [128, 2, D], F16, ctx=ctx)
            ge = sb("ge", [128, 2, T], ctx=ctx)
            w = sb("w", [128, 2, T], ctx=ctx)
            w_hi = sb("w_hi", [128, 2, T], F16, ctx=ctx)
            w_lo = sb("w_lo", [128, 2, T], F16, ctx=ctx)
            hot_b = sb("hot_b", [128, 2, GT // 2, NK, 2], F16, ctx=ctx)
            hot = sb("hot", [128, 2, GT // 2, QUARTER, 2], F16, ctx=ctx)
            hot_hi = sb("hot_hi", [128, 2, GT // 2, QUARTER, 2], F16, ctx=ctx)
            hot_lo = sb("hot_lo", [128, 2, GT // 2, QUARTER, 2], F16, ctx=ctx)
            u_sem, v_sem = (s.u0, s.u1), (s.v0, s.v1)
            H_BANK, G_BANK = 5, 7

            def number(q, c):
                return c + QUARTER * q

            def later(q, c):
                return not (q == 0 and isinstance(c, int) and c < 2)

            def u_number(q, c):
                return number(q, c) - UNDER

            def split_number(q, c):
                return number(q, c) - SPLIT

            def block_at(q, c):
                return (q + 1, c - QUARTER) if isinstance(c, int) and c >= QUARTER else (q, c)

            def no_split_before(q, c):
                return q == 0 and split_number(q, c) < 2

            def spread(x, width, t):
                return x[:, t].rearrange("p (t o e) -> p t o e", o=1, e=2).to_broadcast([128, GT // 2, width, 2])

            def numbers(k0, width):
                return iota[:, k0:k0 + width].rearrange("p (o k) e -> p o k e", o=1).to_broadcast(
                    [128, GT // 2, width, 2])

            def scatter_vector(dve, q, c, p):
                n = number(q, c)
                t = bass.ds(c * GT, GT)
                if later(q, c):
                    dve.wait_ge(s.cols, n - 1)
                nc.vector.tensor_tensor(hot[:, p], numbers(QUARTER * q, QUARTER), spread(ea_T, QUARTER, t),
                                        ALU.is_equal).then_inc(s.eq, 1)
                if later(q, c):
                    dve.wait_ge(s.g, n - 1)
                nc.vector.tensor_tensor(hot_b[:, p], numbers(0, NK), spread(eb_T, NK, t), ALU.is_equal)
                dve.wait_ge(s.eq, n + 1)
                nc.vector.tensor_tensor(hot_hi[:, p], hot[:, p], spread(gh_T, QUARTER, t), ALU.mult
                                        ).then_inc(s.rows, 1)

            def scatter_pool(pool, q, c, p):
                n = number(q, c)
                t = bass.ds(c * GT, GT)
                if later(q, c):
                    pool.wait_ge(s.g, n - 1)
                pool.wait_ge(s.eq, n + 1)
                nc.gpsimd.tensor_tensor(hot_lo[:, p], hot[:, p], spread(gl_T, QUARTER, t), ALU.mult
                                        ).then_inc(s.cols, 1)

            def scatter_tensor(pe, q, c, p):
                n = number(q, c)
                pe.wait_ge(s.rows, n + 1)
                pe.wait_ge(s.cols, n + 1)
                if not (q == 0 and isinstance(c, int) and c < 1):
                    pe.wait_ge(s.g_used, n)
                for e in range(GT):
                    dst = ps[:, G_BANK, QUARTER * e:QUARTER * e + QUARTER]
                    rows = hot_b[:, p, e // 2, :, e % 2]
                    nc.tensor.matmul(dst, rows, hot_hi[:, p, e // 2, :, e % 2], start=True, stop=False)
                    last = nc.tensor.matmul(dst, rows, hot_lo[:, p, e // 2, :, e % 2], start=False, stop=True)
                last.then_inc(s.g, 1)

            def scatter_scalar(act, q, c, p):
                n = number(q, c)
                act.wait_ge(s.g, n + 1)
                if q >= 2:
                    act.wait_ge(s.w, QUARTER * (q - 1))
                nc.scalar.copy(gates[:, q % 2, :, bass.ds(c * GT, GT)],
                               ps[:, G_BANK, 0:GT * QUARTER].rearrange("p (t a) -> p a t", a=QUARTER)
                               ).then_inc(s.g_used, 1)

            def load_u(sp, q, c, p):
                if not no_split_before(q, c):
                    sp.wait_ge(s.ul, split_number(q, c) - 1)
                sp.dma_start(u_in[:, p], u_tab[bass.ds(c + (layer * NK + QUARTER * q), 1)]
                             .rearrange("o p k e -> p (o k) e")).then_inc(u_sem[p], 16)

            def load_v(sp, q, c, p):
                if later(q, c):
                    sp.wait_ge(s.vl, number(q, c) - 1)
                sp.dma_start(v_in[:, p], v_tab[bass.ds(c + (layer * NK + QUARTER * q), 1)]
                             .rearrange("o e d -> e (o d)")).then_inc(v_sem[p], 16)

            def u_high(act, q, c, p):
                act.wait_ge(u_sem[p], (split_number(q, c) - p) * 8 + 16)
                act.wait_ge(s.h, u_number(q, c) - 1)
                nc.scalar.activation(u_hi[:, p], u_in[:, p], ACT.Copy, scale=U_SCALE).then_inc(s.uh, 1)

            def u_opening_scalar(act, c, p):
                n = split_number(0, c)
                act.wait_ge(u_sem[p], (n - p) * 8 + 16)
                nc.scalar.activation(u_in[:, p], u_in[:, p], ACT.Copy, scale=U_SCALE).then_inc(s.us, 1)
                act.wait_ge(s.us, n + 1)
                act.wait_ge(s.h, u_number(0, c) - 1)
                nc.scalar.copy(u_hi[:, p], u_in[:, p]).then_inc(s.uh, 1)

            def gelu_opening(act, c, p):
                act.wait_ge(s.h, u_number(0, c) + 1)
                nc.scalar.activation(first[:, c, :], ps[:, H_BANK + p, 0:T], ACT.Gelu_apprx_tanh, scale=1.0 / U_SCALE
                                     ).then_inc(s.gelu, 1)

            def u_opening_pool(pool, c, p):
                pool.wait_ge(s.uh, split_number(0, c) + 1)
                nc.gpsimd.tensor_tensor(u_lo[:, p], u_in[:, p], u_hi[:, p], ALU.subtract).then_inc(s.ul, 1)

            def v_high(act, q, c, p):
                act.wait_ge(v_sem[p], (number(q, c) - p) * 8 + 16)
                if later(q, c):
                    act.wait_ge(s.y, number(q, c) - 1)
                nc.scalar.activation(v_hi[:, p], v_in[:, p], ACT.Copy, scale=V_SCALE).then_inc(s.vh, 1)

            def u_low(dve, q, c, p):
                dve.wait_ge(s.uh, split_number(q, c) + 1)
                nc.vector.scalar_tensor_tensor(out=u_lo[:, p].rearrange("p k e -> p (k e)"),
                                               in0=u_in[:, p].rearrange("p k e -> p (k e)"), scalar=U_SCALE,
                                               in1=u_hi[:, p].rearrange("p k e -> p (k e)"), op0=ALU.mult,
                                               op1=ALU.subtract).then_inc(s.ul, 1)

            def v_low(dve, q, c, p):
                dve.wait_ge(s.vh, number(q, c) + 1)
                nc.vector.scalar_tensor_tensor(out=v_lo[:, p], in0=v_in[:, p], scalar=V_SCALE, in1=v_hi[:, p],
                                               op0=ALU.mult, op1=ALU.subtract).then_inc(s.vl, 1)

            def gelu(act, q, c, p):
                if q > 0:
                    n = number(q, c)
                    act.wait_ge(s.h, u_number(q, c) + 1)
                    if later(q, c):
                        act.wait_ge(s.w, n - 1)
                    nc.scalar.activation(ge[:, p], ps[:, H_BANK + p, 0:T], ACT.Gelu_apprx_tanh, scale=1.0 / U_SCALE
                                         ).then_inc(s.gelu, 1)

            def w_high(act, q, c, p):
                n = number(q, c)
                act.wait_ge(s.w, n + 1)
                if later(q, c):
                    act.wait_ge(s.y, n - 1)
                nc.scalar.copy(w_hi[:, p], w[:, p]).then_inc(s.wh, 1)

            def gate(dve, q, c, p):
                n = number(q, c)
                if q > 0:
                    dve.wait_ge(s.gelu, u_number(q, c) + 1)
                elif isinstance(c, int) and c == 0:
                    dve.wait_ge(s.gelu, QUARTER - UNDER)
                dve.wait_ge(s.g_used, QUARTER * (q + 1))
                if later(q, c):
                    dve.wait_ge(s.wl, n - 1)
                src = ge[:, p] if q > 0 else first[:, bass.ds(c, 1), :].rearrange("p o t -> p (o t)")
                nc.vector.tensor_tensor(w[:, p], src,
                                        gates[:, q % 2, bass.ds(c, 1), :].rearrange("p o t -> p (o t)"), ALU.mult
                                        ).then_inc(s.w, 1)

            def w_low(pool, q, c, p):
                pool.wait_ge(s.wh, number(q, c) + 1)
                nc.gpsimd.tensor_tensor(w_lo[:, p], w[:, p], w_hi[:, p], ALU.subtract).then_inc(s.wl, 1)

            def u_ready(pe, q, c):
                n = u_number(q, c)
                if not (q == 0 and c < SPLIT):
                    pe.wait_ge(s.uh, split_number(q, c) + 1)
                    pe.wait_ge(s.ul, split_number(q, c) + 1)
                if not (q == 0 and n < 2):
                    pe.wait_ge(s.gelu, n - 1)

            def u_part(p, k, start, stop):
                dst = ps[:, H_BANK + p, 0:T]
                at = slice(k, k + 1) if isinstance(k, int) else bass.ds(k, 1)
                high, low = (u[:, p, at, :].rearrange("p o e -> p (o e)") for u in (u_hi, u_lo))
                x_high, x_low = (x[:, at, :].rearrange("p o t -> p (o t)") for x in (x_hi, x_lo))
                nc.tensor.matmul(dst, high, x_high, start=start, stop=False)
                nc.tensor.matmul(dst, high, x_low, start=False, stop=False)
                return nc.tensor.matmul(dst, low, x_high, start=False, stop=stop)

            def product_u(pe, q, c, p):
                u_ready(pe, q, c)
                for k in range(KT):
                    last = u_part(p, k, k == 0, k == KT - 1)
                last.then_inc(s.h, 1)

            def product_v(pe, q, c, p):
                n = number(q, c)
                begin = isinstance(n, int) and n == 0
                end = isinstance(n, int) and n == NK - 1
                pe.wait_ge(s.vl, n + 1)
                pe.wait_ge(s.wl, n + 1)
                for f in range(KT):
                    for m, (vv, ww) in enumerate(((v_hi, w_hi), (v_hi, w_lo), (v_lo, w_hi))):
                        lhs = vv[:, p, 128 * f:128 * f + 128]
                        nc.tensor.matmul(ps[:, f // 2, 256 * (f % 2):256 * (f % 2) + 256], lhs, ww[:, p, 0:PROMPT],
                                         start=(begin and m == 0 and f % 2 == 0), stop=(end and m == 2),
                                         skip_group_check=True)
                        last = nc.tensor.matmul(ps[:, 4, SAMPLE * f:SAMPLE * f + SAMPLE], lhs, ww[:, p, PROMPT:T],
                                                start=(begin and m == 0 and f == 0), stop=(end and m == 2),
                                                skip_group_check=True)
                last.then_inc(s.y, 1)

            def pairs(eng, q, head, tail, pair):
                if head:
                    pair(q, 0)
                with eng.Fori(1 if head else 0, QUARTER // 2 - (1 if tail else 0)) as n:
                    pair(q, n * 2)
                if tail:
                    pair(q, QUARTER - 2)

            def each_pair(eng, pair, begin=None):
                for q in range(4):
                    if begin:
                        begin(q)
                    pairs(eng, q, q <= 1, True, pair)

            def opening(eng, step, begin=None, middle=None, end=None):
                for b in range(UNDER, QUARTER):
                    c = KT * (b - UNDER)
                    if begin:
                        begin(b)
                    step(b, c, 0)
                    if middle:
                        middle(b)
                    with eng.Fori(1, KT // 2 - 1) as n:
                        step(b, n * 2 + c, n * 2)
                    step(b, c + KT - 2, KT - 2)
                    if end:
                        end(b)

            def w_next(c, p):
                return not (isinstance(c, int) and c + p == QUARTER - 1)

            def u_ahead(q, c, p, by):
                at_end = isinstance(c, int) and c + p + by >= QUARTER
                return at_end if q == 0 else not (q == 3 and at_end)

            @block.sync
            def _(sp):
                for c in range(SPLIT, QUARTER):
                    load_u(sp, 0, c, c % 2)

                def pair(q, c):
                    for p in range(2):
                        if q > 0:
                            load_u(sp, q, c + p, p)
                        load_v(sp, q, c + p, p)
                each_pair(sp, pair)

            @block.scalar
            def _(act):
                def step(b, c, k):
                    scatter_scalar(act, 0, c, 0)
                    scatter_scalar(act, 0, c + 1, 1)

                def end(b):
                    if b + 2 < QUARTER:
                        u_opening_scalar(act, b + 2, b % 2)
                    gelu_opening(act, b, b % 2)
                    if b == UNDER:
                        v_high(act, 0, 0, 0)
                opening(act, step, end=end)

                def pair(q, c):
                    done = q == 3 and isinstance(c, int) and c == QUARTER - 2
                    for p in range(2):
                        if w_next(c, p):
                            gelu(act, q, c + p + 1, 1 - p)
                        if u_ahead(q, c, p, 2):
                            u_high(act, *block_at(q, c + p + 2), p)
                        if not (done and p):
                            v_high(act, q, c + p + 1, 1 - p)
                        if w_next(c, p):
                            w_high(act, q, c + p + 1, 1 - p)
                        if q < 3:
                            scatter_scalar(act, q + 1, c + p, p)

                def begin(q):
                    gelu(act, q, 0, 0)
                    w_high(act, q, 0, 0)
                each_pair(act, pair, begin)

            @block.vector
            def _(dve):
                def step(b, c, k):
                    scatter_vector(dve, 0, c, 0)
                    scatter_vector(dve, 0, c + 1, 1)
                opening(dve, step)

                def begin(q):
                    gate(dve, q, 0, 0)
                    if q == 0:
                        v_low(dve, 0, 0, 0)

                def pair(q, c):
                    done = q == 3 and isinstance(c, int) and c == QUARTER - 2
                    for p in range(2):
                        if q < 3:
                            scatter_vector(dve, q + 1, c + p, p)
                        if w_next(c, p):
                            gate(dve, q, c + p + 1, 1 - p)
                        if u_ahead(q, c, p, 2):
                            u_low(dve, *block_at(q, c + p + 2), p)
                        if not (done and p):
                            v_low(dve, q, c + p + 1, 1 - p)
                each_pair(dve, pair, begin)

            @block.gpsimd
            def _(pool):
                def step(b, c, k):
                    scatter_pool(pool, 0, c, 0)
                    scatter_pool(pool, 0, c + 1, 1)

                def middle(b):
                    if SPLIT <= b + 1 < QUARTER:
                        u_opening_pool(pool, b + 1, (b + 1) % 2)
                opening(pool, step, middle=middle)

                def pair(q, c):
                    for p in range(2):
                        if q < 3:
                            scatter_pool(pool, q + 1, c + p, p)
                        if w_next(c, p):
                            w_low(pool, q, c + p + 1, 1 - p)
                each_pair(pool, pair, lambda q: w_low(pool, q, 0, 0))

            @block.tensor
            def _(pe):
                def begin(b):
                    u_ready(pe, 0, b)

                def step(b, c, k):
                    for m in range(2):
                        scatter_tensor(pe, 0, c + m, m)
                        first_k, last_k = isinstance(k, int) and k + m == 0, isinstance(k, int) and k + m == KT - 1
                        last = u_part(b % 2, k + m, first_k, last_k)
                    if last_k:
                        last.then_inc(s.h, 1)
                opening(pe, step, begin=begin)

                def pair(q, c):
                    for p in range(2):
                        if u_ahead(q, c, p, 1):
                            product_u(pe, *block_at(q, c + p + 1), 1 - p)
                        if q < 3:
                            scatter_tensor(pe, q + 1, c + p, p)
                        product_v(pe, q, c + p, p)
                each_pair(pe, pair)

    with root:
        yield_layers = (sgu, retention, gla)
        for layer in range(DEPTH):
            yield_layers[layer % 3](layer // 3, layer)
            peer(layer)
        with phase("stored") as (block, s):
            @block.sync
            def _(sp):
                sp.dma_start(out[0].rearrange("b (i p) d -> p (b i) d", p=128), x_tok[:, 0:2, :]
                             ).then_inc(s.stored, 16)
                sp.dma_start(out[1].rearrange("b l d -> (b l) d"), x_tok[0:SAMPLE, 2, :]).then_inc(s.stored, 16)
                sp.wait_ge(s.stored, 32)


_PLAIN = ["x_prompt", "x_sample", "state_ret", "state_gla", "sgu_w_in", "sgu_b_in", "sgu_v_g", "sgu_v_b", "sgu_b_s",
          "sgu_w_out", "ret_w_in", "ret_w_out", "gla_w_in", "gla_w_a2", "gla_w_out", "peer_w_q", "ln_g", "ln_b"]
_OUTS = [(1, PROMPT, D), (NB, LS, D), (1, 1, H, 256, 512), (1, NB, H, 256, 512), (1, 1, H, 128, 256),
         (1, NB, H, 128, 256), (2, NB, LS, D)]


def kernel(**inputs):
    import concourse.bacc as bacc
    from concourse.bass_utils import run_bass_kernel_spmd

    a = {k: np.asarray(v) for k, v in inputs.items()}
    arrays = {n: a[n] for n in _PLAIN}
    arrays["sgu_b_col"] = a["sgu_b_in"].reshape(2, 16, 128).transpose(0, 2, 1)
    arrays["ret_gain"] = a["ret_gn_g"].reshape(1, 16, 128).transpose(0, 2, 1)
    arrays["gla_b_col"] = a["gla_b_a"].reshape(1, 4, 128).transpose(0, 2, 1)
    arrays["gla_gain"] = np.tile(a["gla_rms_g"].reshape(1, 2, 128).transpose(0, 2, 1), (1, 1, H))
    arrays["sgu_w_sT"] = a["sgu_w_s"].transpose(0, 1, 3, 2)
    arrays["peer_keys_aT"] = a["peer_keys_a"].transpose(0, 2, 1)
    arrays["peer_keys_bT"] = a["peer_keys_b"].transpose(0, 2, 1)
    arrays["peer_uT"] = a["peer_u"].reshape(DEPTH * NK, 128, KT, 128).transpose(0, 3, 2, 1)
    arrays["peer_v"] = a["peer_v"].reshape(DEPTH * NK, 128, D)
    arrays.update(shape_constants())
    arrays = {f"in_{n}": np.ascontiguousarray(v) for n, v in arrays.items()}
    nc = bacc.Bacc("TRN2", target_bir_lowering=False, num_devices=1)
    io = {n[3:]: nc.dram_tensor(n, v.shape, mybir.dt.from_np(v.dtype), kind="ExternalInput").ap()
          for n, v in arrays.items()}
    out = [nc.dram_tensor(f"out_{i}", shape, F32, kind="ExternalOutput").ap() for i, shape in enumerate(_OUTS)]
    build(nc, io, out)
    r = run_bass_kernel_spmd(nc, [arrays], core_ids=[0])
    return tuple(r.results[0][f"out_{i}"] for i in range(len(_OUTS)))
```
